# Optimizing a Trainium2 kernel written in Bass

```python
import jax, jax.numpy as jnp
from jax import lax
import numpy as np

D_MODEL = 1024
BATCH = 1
SEQ = 1024
DEPTH = 1

PLE_DIM = 256
HG_WIDTH = 512
HG_HEADS = 4
HG_DK = HG_WIDTH // HG_HEADS
HG_CHUNK = 64
AT_WIDTH = D_MODEL - HG_WIDTH
AT_HEAD_DIM = 64
AT_Q_HEADS = AT_WIDTH // AT_HEAD_DIM
AT_KV_HEADS = 2
AT_GROUP = AT_Q_HEADS // AT_KV_HEADS
WINDOW = 128
D_FF = 2816
CONV_W = 3
EPS = 1e-6
MASK_VALUE = -1e30
LB_FLOOR = 1e-30
SPLIT_SIZES = [HG_WIDTH, HG_WIDTH, HG_WIDTH, HG_WIDTH, AT_WIDTH,
               AT_KV_HEADS * AT_HEAD_DIM, AT_KV_HEADS * AT_HEAD_DIM]
IN_WIDTH = sum(SPLIT_SIZES)

kernel_name = "hymba_style_hgrn2_swa_sink_convffn_ple"

def rmsnorm(x, g):
    xf = x.astype(jnp.float32)
    y = xf * lax.rsqrt(jnp.mean(xf * xf, axis=-1, keepdims=True) + EPS)
    return (y * g.astype(jnp.float32)).astype(x.dtype)

def hgrn2_mixer(q_pre, f_pre, i_in, g_pre, lb, norm_g):
    B, S, _ = q_pre.shape
    nc = S // HG_CHUNK
    f32 = jnp.float32
    lbf = lb.astype(f32)
    z = f_pre.astype(f32)
    q = jax.nn.silu(q_pre.astype(f32))
    logf = jnp.logaddexp(jnp.log(jnp.maximum(lbf, LB_FLOOR)),
                         jnp.log1p(-lbf) + jax.nn.log_sigmoid(z))
    k = (1.0 - lbf) * jax.nn.sigmoid(-z)
    v = i_in.astype(f32)

    def to_chunks(t):
        return t.reshape(B, nc, HG_CHUNK, HG_HEADS, HG_DK).transpose(1, 0, 3, 2, 4)

    qc, kc, vc, lc = to_chunks(q), to_chunks(k), to_chunks(v), to_chunks(logf)
    causal = jnp.tril(jnp.ones((HG_CHUNK, HG_CHUNK), dtype=bool))[:, :, None]

    def step(state, inp):
        qi, ki, vi, li = inp
        b = jnp.cumsum(li, axis=2)
        diff = b[:, :, :, None, :] - b[:, :, None, :, :]
        decay = jnp.where(causal, jnp.exp(jnp.where(causal, diff, 0.0)), 0.0)
        att = jnp.einsum('bhtk,bhsk,bhtsk->bhts', qi, ki, decay)
        o = (jnp.einsum('bhts,bhsv->bhtv', att, vi)
             + jnp.einsum('bhtk,bhkv->bhtv', qi * jnp.exp(b), state))
        b_last = b[:, :, -1:, :]
        new_state = (jnp.exp(b_last[:, :, 0, :])[..., None] * state
                     + jnp.einsum('bhsk,bhsv->bhkv', ki * jnp.exp(b_last - b), vi))
        return new_state, o

    s0 = jnp.zeros((B, HG_HEADS, HG_DK, HG_DK), f32)
    _, o = lax.scan(step, s0, (qc, kc, vc, lc))
    o = o.transpose(1, 0, 3, 2, 4).reshape(B, S, HG_HEADS, HG_DK)
    o = o * lax.rsqrt(jnp.mean(o * o, axis=-1, keepdims=True) + EPS)
    o = o * norm_g.astype(f32).reshape(HG_HEADS, HG_DK)
    o = o.reshape(B, S, HG_WIDTH) * jax.nn.sigmoid(g_pre.astype(f32))
    return o.astype(i_in.dtype)

def swa_sink_attention(q, k, v, sinks):
    B, S, _ = q.shape
    nb = S // WINDOW
    q = q.reshape(B, nb, WINDOW, AT_KV_HEADS, AT_GROUP, AT_HEAD_DIM)
    k = k.reshape(B, nb, WINDOW, AT_KV_HEADS, AT_HEAD_DIM)
    v = v.reshape(B, nb, WINDOW, AT_KV_HEADS, AT_HEAD_DIM)
    pad = ((0, 0), (1, 0), (0, 0), (0, 0), (0, 0))
    kk = jnp.concatenate([jnp.pad(k[:, :-1], pad), k], axis=2)
    vv = jnp.concatenate([jnp.pad(v[:, :-1], pad), v], axis=2)
    scale = AT_HEAD_DIM ** -0.5
    scores = jnp.einsum('bnqhgd,bnkhd->bnhgqk', q, kk).astype(jnp.float32) * scale
    qpos = jnp.arange(WINDOW)[:, None] + WINDOW
    kpos = jnp.arange(2 * WINDOW)[None, :]
    rel = qpos - kpos
    band = (rel >= 0) & (rel < WINDOW)
    first = (jnp.arange(nb) == 0)[:, None, None]
    valid = band[None] & ~(first & (kpos < WINDOW)[None])
    scores = jnp.where(valid[None, :, None, None], scores, MASK_VALUE)
    sink = sinks.astype(jnp.float32).reshape(AT_KV_HEADS, AT_GROUP)[None, None, :, :, None, None]
    m = jnp.maximum(jnp.max(scores, axis=-1, keepdims=True), sink)
    e = jnp.exp(scores - m)
    probs = (e / (jnp.sum(e, axis=-1, keepdims=True) + jnp.exp(sink - m))).astype(v.dtype)
    out = jnp.einsum('bnhgqk,bnkhd->bnqhgd', probs, vv)
    return out.reshape(B, S, AT_WIDTH)

def conv_ffn(u, w_up, conv_w, conv_b, w_down):
    h = u @ w_up
    a, b = h[..., :D_FF], h[..., D_FF:]
    a = lax.conv_general_dilated(
        a, conv_w[:, None, :], window_strides=(1,), padding=[(CONV_W - 1, 0)],
        dimension_numbers=('NWC', 'WIO', 'NWC'), feature_group_count=D_FF) + conv_b
    return (jax.nn.silu(a) * b) @ w_down

def setup_inputs(seed: int = 0) -> dict:
    key = jax.random.key(seed)
    ks = jax.random.split(key, 20)
    f32 = jnp.float32
    nrm = lambda k, shape, s: jax.random.normal(k, shape, f32) * s
    res_scale = (2.0 * DEPTH) ** -0.5
    return {
        "x": nrm(ks[0], (BATCH, SEQ, D_MODEL), 1.0),
        "p": nrm(ks[1], (DEPTH, BATCH, SEQ, PLE_DIM), 1.0),
        "g_mix": 1.0 + nrm(ks[2], (DEPTH, D_MODEL), 0.02),
        "w_in": nrm(ks[3], (DEPTH, D_MODEL, IN_WIDTH), D_MODEL ** -0.5),
        "lb_logits": nrm(ks[4], (DEPTH, HG_WIDTH), 0.1),
        "hg_norm_g": 1.0 + nrm(ks[5], (DEPTH, HG_WIDTH), 0.02),
        "attn_sinks": nrm(ks[6], (DEPTH, AT_Q_HEADS), 0.5),
        "w_out": nrm(ks[7], (DEPTH, D_MODEL, D_MODEL), D_MODEL ** -0.5 * res_scale),
        "g_ffn": 1.0 + nrm(ks[8], (DEPTH, D_MODEL), 0.02),
        "w_up": nrm(ks[9], (DEPTH, D_MODEL, 2 * D_FF), D_MODEL ** -0.5),
        "conv_w": nrm(ks[10], (DEPTH, CONV_W, D_FF), CONV_W ** -0.5),
        "conv_b": nrm(ks[11], (DEPTH, D_FF), 0.01),
        "w_down": nrm(ks[12], (DEPTH, D_FF, D_MODEL), D_FF ** -0.5 * res_scale),
        "g_ple": 1.0 + nrm(ks[13], (DEPTH, D_MODEL), 0.02),
        "w_ple_gate": nrm(ks[14], (DEPTH, D_MODEL, D_MODEL), D_MODEL ** -0.5),
        "w_ple_up": nrm(ks[15], (DEPTH, PLE_DIM, D_MODEL), PLE_DIM ** -0.5 * res_scale),
        "g_final": 1.0 + nrm(ks[16], (D_MODEL,), 0.02),
    }

def reference(x, p, g_mix, w_in, lb_logits, hg_norm_g, attn_sinks, w_out, g_ffn,
              w_up, conv_w, conv_b, w_down, g_ple, w_ple_gate, w_ple_up, g_final):
    lb_p = jax.nn.softmax(lb_logits.astype(jnp.float32), axis=0)
    lb_all = jnp.cumsum(lb_p, axis=0) - lb_p[0]
    cuts = list(np.cumsum(SPLIT_SIZES)[:-1])
    h = x
    for i in range(DEPTH):
        u = rmsnorm(h, g_mix[i])
        proj = u @ w_in[i]
        hq, hf, hi, hg, aq, ak, av = jnp.split(proj, cuts, axis=-1)
        y_hg = hgrn2_mixer(hq, hf, hi, hg, lb_all[i], hg_norm_g[i])
        y_at = swa_sink_attention(aq, ak, av, attn_sinks[i])
        h = h + jnp.concatenate([y_hg, y_at], axis=-1) @ w_out[i]
        h = h + conv_ffn(rmsnorm(h, g_ffn[i]), w_up[i], conv_w[i], conv_b[i], w_down[i])
        gate = jax.nn.sigmoid(rmsnorm(h, g_ple[i]) @ w_ple_gate[i])
        h = h + gate * (p[i] @ w_ple_up[i])
    return rmsnorm(h, g_final)


_drawn_inputs = setup_inputs


def setup_inputs(seed=0):
    import zlib

    import numpy as np

    out = dict(_drawn_inputs(seed))
    spreads = {}
    factors = {'g_mix': 8.0,
     'hg_norm_g': 28.605,
     'attn_sinks': 200.0,
     'g_ffn': 5.658,
     'conv_b': 33.57,
     'g_ple': 200.0,
     'g_final': 23.358,
     'w_ple_gate': 9.067}
    for name, (base, spread) in spreads.items():
        noise = np.random.default_rng([zlib.crc32(name.encode()), seed]).standard_normal(out[name].shape)
        drawn = base * np.exp(spread * noise) if base else spread * noise
        out[name] = __import__('jax').numpy.asarray(drawn.astype(out[name].dtype))
    for name, factor in factors.items():
        out[name] = (out[name] * factor).astype(out[name].dtype)
    return out
```

```python
from contextlib import ExitStack

import concourse.bass as bass
from concourse import mybir

F32 = mybir.dt.float32
F32R = mybir.dt.float32r
BF16 = mybir.dt.bfloat16
U16 = mybir.dt.uint16
ALU = mybir.AluOpType
ACT = mybir.ActivationFunctionType
AX = mybir.AxisListType

P = 128
S = 1024
D = 1024
NT = S // P
KT = D // P
HH = 4
HW = HH * P
QH, KVH, DH = 8, 2, 64
GR = QH // KVH
F = 2816
FT = F // P
PD = 256
PK = PD // P
EPS = 1e-6
MASK_VALUE = -1e30
LB_FLOOR = 1e-30
LEVELS = 7
SW = 256
ds = bass.ds


def wait(eng, sem, count):
    if not isinstance(count, int) or count > 0:
        eng.wait_ge(sem, count)


def turns(eng, count, body):
    body(0)
    with eng.Fori(1, count) as i:
        body(i)


def trunk_kernel(nc, x, p, g_mix, w_in, lb_logits, hg_norm_g, attn_sinks, w_out, g_ffn, w_up,
                 conv_w, conv_b, w_down, g_ple, w_ple_gate, w_ple_up, g_final, out):
    x_t = x[0].rearrange("(n p) d -> n p d", p=P)
    out_t = out[0].rearrange("(n p) d -> n p d", p=P)
    p_t = p[0, 0].rearrange("(n p) e -> p n e", p=P)
    w_in_v = w_in[0].rearrange("(k p) n -> p k n", p=P)
    w_out_v = w_out[0].rearrange("(k p) n -> p k n", p=P)
    w_up_v = w_up[0].rearrange("(k p) n -> p k n", p=P)
    w_down_v = w_down[0].rearrange("(k p) n -> p k n", p=P)
    w_gate_v = w_ple_gate[0].rearrange("(k p) n -> p k n", p=P)
    w_pup_v = w_ple_up[0].rearrange("(k p) n -> p k n", p=P)
    h_dram = nc.dram_tensor("h_after_mixer", (NT, P, D), F32, kind="Internal").ap()

    ctx = ExitStack()
    with ctx:
        def sb(scope, name, shape, dt=F32):
            return scope.enter_context(nc.sbuf_tensor(name, shape, dt))

        def sem(name):
            return ctx.enter_context(nc.semaphore(name))

        ident = sb(ctx, "ident", [P, P])
        rows = sb(ctx, "rows", [P, P])
        cols = sb(ctx, "cols", [P, P])
        CONV_W0, CONV_B0, LB0, HGG0 = 0, 3 * FT, 4 * FT, 4 * FT + HH
        lbv = sb(ctx, "lbv", [P, 8, HH])
        neg_half = sb(ctx, "neg_half", [P, HH])
        ssq = sb(ctx, "ssq", [P, 2 + HH])
        msq = sb(ctx, "msq", [P, 2 + HH])
        rstd = sb(ctx, "rstd", [P, 2 + HH])
        ident_b = sb(ctx, "ident_b", [P, P], BF16)
        level_mask = sb(ctx, "level_mask", [P, LEVELS * 256], BF16)
        band = sb(ctx, "band", [P, 4, P], BF16)

        with ExitStack() as scope:
            gain_mix = sb(scope, "gain_mix", [P, D])
            xt_mix = sb(scope, "xt_mix", [P, 2, D])
            junk_mix = sb(scope, "junk_mix", [P, D], BF16)
        with ExitStack() as mixer_scope:
            qT = sb(mixer_scope, "qT", [P, HH, S])
            fT = sb(mixer_scope, "fT", [P, HH, S])
            kT = sb(mixer_scope, "kT", [P, HH, S])
            sgT = sb(mixer_scope, "sgT", [P, HH, S])
            aqT = sb(mixer_scope, "aqT", [P, GR, S])
            akT = sb(mixer_scope, "akT", [P, S])
            with ExitStack() as scope:
                uh1 = sb(scope, "uh1", [P, KT, S], F32R)
                ul1 = sb(scope, "ul1", [P, KT, S], F32R)
                raw1 = sb(scope, "raw1", [P, 2, KT, SW])
                wh1 = sb(scope, "wh1", [P, 2, KT, P], F32R)
                wl1 = sb(scope, "wl1", [P, 2, KT, P], F32R)
                vT = sb(scope, "vT", [P, HH + 1, S])
            with ExitStack() as scope:
                wo = sb(scope, "wo", [P, KT, D])
                v_tok = sb(scope, "v_tok", [P, NT, HW])
                av_tok = sb(scope, "av_tok", [P, NT + 1, P])
                sink = sb(scope, "sink", [P, QH])
                qst = sb(scope, "qst", [P, GR, P])
                kst = sb(scope, "kst", [P, 2, P])
                smax = sb(scope, "smax", [P, 3, QH])
                sden = sb(scope, "sden", [P, 5, QH])
                probs = sb(scope, "probs", [P, GR, 2, P])
                probsT = sb(scope, "probsT", [P, GR, 2, P])
                Ql = sb(scope, "Ql", [P, 2, HW])
                Kl = sb(scope, "Kl", [P, 2, HW])
                FQ = sb(scope, "FQ", [P, 1024])
                FK = sb(scope, "FK", [P, 1024])
                total = sb(scope, "total", [P, HH])
                attT = sb(scope, "attT", [P, HW])
                state = sb(scope, "state", [P, HW])
                k_tok = sb(scope, "k_tok", [P, HW])
                osq = sb(scope, "osq", [P, HW])
                y_tok = sb(scope, "y_tok", [P, D])
                yT = sb(scope, "yT", [P, KT, P])
                x2 = sb(scope, "x2", [P, 2, D])
        with ExitStack() as scope:
            xt_ffn = sb(scope, "xt_ffn", [P, 2, D])
            gain_ffn = sb(scope, "gain_ffn", [P, D])
            junk_ffn = sb(scope, "junk_ffn", [P, D], BF16)
        with ExitStack() as scope:
            un_ple = sb(scope, "un_ple", [P, 2, D])
            gain_ple = sb(scope, "gain_ple", [P, D])
            junk_ple = sb(scope, "junk_ple", [P, D], BF16)
        conv = sb(ctx, "conv", [P, 2, S])
        sgm = sb(ctx, "sgm", [P, S])
        pad = sb(ctx, "pad", [P, 512])
        raw2 = sb(ctx, "raw2", [P, 2, KT, SW])
        wh2 = sb(ctx, "wh2", [P, 2, KT, P], F32R)
        wl2 = sb(ctx, "wl2", [P, 2, KT, P], F32R)
        with ExitStack() as scope:
            G = sb(scope, "G", [P, FT, S])
        with ExitStack() as scope:
            uh3 = sb(scope, "uh3", [P, KT, S], F32R)
            ul3 = sb(scope, "ul3", [P, KT, S], F32R)
            pTh = sb(scope, "pTh", [P, PK, S], F32R)
            pTl = sb(scope, "pTl", [P, PK, S], F32R)
            w_pup = sb(scope, "w_pup", [P, PK, D])
            over_G = sb(scope, "over_G", [P, FT * S - 20 * S - PK * D + 256])
            with ExitStack() as deeper:
                uh2 = sb(deeper, "uh2", [P, KT, S], F32R)
                ul2 = sb(deeper, "ul2", [P, KT, S], F32R)
            h = sb(scope, "h", [P, NT, D])
            pwh = sb(scope, "pwh", [P, 2, PK, P], F32R)
            pwl = sb(scope, "pwl", [P, 2, PK, P], F32R)
            with ExitStack() as deeper:
                gh = sb(deeper, "gh", [P, 2, S], F32R)
                gl = sb(deeper, "gl", [P, 2, S], F32R)
                dh = sb(deeper, "dh", [P, 2, 512], F32R)
                dl = sb(deeper, "dl", [P, 2, 512], F32R)
            with ExitStack() as deeper:
                p_tok = sb(deeper, "p_tok", [P, NT, PD])
                pleT = sb(deeper, "pleT", [P, 2, S])
                gain_fin = sb(deeper, "gain_fin", [P, D])
        Q = [ctx.enter_context(nc.psum_tensor(f"Q{n}", [P, 1024], F32)) for n in range(4)]
        acc = [Q[t // 2][:, 512 * (t % 2):512 * (t % 2) + 512] for t in range(NT)]

        consts = sem("consts")
        rows_in = sem("rows_in")
        cols_ready = sem("cols_ready")
        colsT = sem("colsT")
        lb_step = sem("lb_step")
        gain_in = [sem(f"gain_in{n}") for n in range(4)]
        mask_step = sem("mask_step")
        sink_arg = sem("sink_arg")
        sink_exped = sem("sink_exped")
        x_in = [sem(f"x_in{n}") for n in range(2)]
        squared = sem("squared")
        mean_ready = sem("mean_ready")
        rstd_ready = sem("rstd_ready")
        normed = sem("normed")
        turned = sem("turned")
        u_hi = sem("u_hi")
        u_lo = sem("u_lo")
        raw_in = [sem(f"raw_in{n}") for n in range(2)]
        w_hi = sem("w_hi")
        w_lo = sem("w_lo")
        product = sem("product")
        proj_act = sem("proj_act")
        freed = [sem(f"freed{n}") for n in range(2)]
        scaled = sem("scaled")
        v_turned = sem("v_turned")
        v_ready = [sem(f"v_ready{n}") for n in range(2)]
        start_ready = sem("start_ready")
        wo_in = sem("wo_in")
        sink_in = sem("sink_in")
        x2_in = [sem(f"x2_in{n}") for n in range(2)]
        qk_static = sem("qk_static")
        scores = sem("scores")
        max_step = sem("max_step")
        max_ready = sem("max_ready")
        exped = sem("exped")
        den_step = sem("den_step")
        den_ready = sem("den_ready")
        probs_turned = sem("probs_turned")
        probsT_ready = sem("probsT_ready")
        attended = sem("attended")
        y_att = sem("y_att")
        factors = sem("factors")
        q_level = sem("q_level")
        k_level = sem("k_level")
        level_product = sem("level_product")
        picked = sem("picked")
        h_half = sem("h_half")
        turn_of_pick = sem("turn_of_pick")
        turn_of_mean = sem("turn_of_mean")
        k_turned = sem("k_turned")
        k_tok_ready = sem("k_tok_ready")
        delta_ready = sem("delta_ready")
        o_ready = sem("o_ready")
        state_ready = sem("state_ready")
        o_squared = sem("o_squared")
        o_sum = sem("o_sum")
        o_mean = sem("o_mean")
        o_rstd = sem("o_rstd")
        y_hg = sem("y_hg")
        y_turned = sem("y_turned")
        yT_at = sem("yT_at")
        yT_hg = sem("yT_hg")
        mixed = sem("mixed")
        h_out = sem("h_out")
        conv_a = sem("conv_a")
        conv_b1 = sem("conv_b1")
        conv_sig = sem("conv_sig")
        silued = sem("silued")
        h_in = sem("h_in")
        d_in = [sem(f"d_in{n}") for n in range(2)]
        d_hi = sem("d_hi")
        d_lo = sem("d_lo")
        g_hi = sem("g_hi")
        g_lo = sem("g_lo")
        down_step = sem("down_step")
        down_half = sem("down_half")
        h_added = sem("h_added")
        p_in = sem("p_in")
        p_turned = sem("p_turned")
        p_hi = sem("p_hi")
        p_lo = sem("p_lo")
        pup_in = sem("pup_in")
        pw_hi = sem("pw_hi")
        pw_lo = sem("pw_lo")
        ple_gate = sem("ple_gate")
        ple_ready = sem("ple_ready")
        ple_turned = sem("ple_turned")
        ple_added = sem("ple_added")
        stored = sem("stored")

        N_IN = 22
        N_UP = 2 * FT
        N_PLE = KT
        UP0, PLE0 = N_IN, N_IN + N_UP
        MASK_STEPS = 3 + 3 + 2 * LEVELS
        START_STEPS = 6
        block = ctx.enter_context(nc.Block())

        def halves(n):
            return slice(512 * n, 512 * n + 512)

        def in_strip(j):
            if 8 <= j < 10:
                a = 4 * HW + P * (j - 8)
                return [(a, P), (a + GR * DH, P)]
            return [(SW * j if j < 8 else 4 * HW + QH * DH, SW)]

        @block.sync
        def _(sp):
            sp.dma_start(rows[0:3 * FT, :], conv_w[0].rearrange("j (f p) -> (j f) p", p=P)).then_inc(rows_in, 16)
            sp.dma_start(rows[CONV_B0:CONV_B0 + FT, :], conv_b[0].rearrange("(f p) -> f p", p=P)).then_inc(rows_in, 16)
            sp.dma_start(rows[LB0:LB0 + HH, :], lb_logits[0].rearrange("(f p) -> f p", p=P)).then_inc(rows_in, 16)
            sp.dma_start(rows[HGG0:HGG0 + HH, :], hg_norm_g[0].rearrange("(f p) -> f p", p=P)).then_inc(rows_in, 16)
            sp.dma_start(gain_mix[:, :], g_mix[0:1, :].to_broadcast([P, D])).then_inc(gain_in[0], 16)
            def load_x(i):
                for t in range(2):
                    wait(sp, turned, 2 * i)
                    sp.dma_start(xt_mix[:, t, :], x_t[ds(2 * i + t, 1), :, :].rearrange("a p d -> (a p) d")).then_inc(x_in[t], 16)

            turns(sp, NT // 2, load_x)
            for j in range(N_IN // 2):
                if j >= 2:
                    sp.wait_ge(w_lo, 2 * (j - 1))
                at = 0
                for c, w in in_strip(j):
                    sp.dma_start(raw1[:, j % 2, :, at:at + w], w_in_v[:, :, c:c + w]).then_inc(raw_in[j % 2], 16)
                    at += w

            sp.wait_ge(product, N_IN)
            for k in range(KT):
                sp.dma_start(wo[:, k, :], w_out_v[:, k, :]).then_inc(wo_in, 16)
            for n in range(2):
                sp.wait_ge(v_ready[n], (HH + 2 - n) // 2)
            sp.dma_start(sink[:, :], attn_sinks[0:1, :].to_broadcast([P, QH])).then_inc(sink_in, 16)

            def residual_rows(i):
                for t in range(2):
                    wait(sp, h_out, 32 * i)
                    sp.dma_start(x2[:, t, :], x_t[ds(2 * i + t, 1), :, :].rearrange("a p d -> (a p) d")).then_inc(x2_in[t], 16)
                for t in range(2):
                    sp.wait_ge(h_half, 4 * i + 2 * t + 2)
                    sp.dma_start(h_dram[ds(2 * i + t, 1), :, :].rearrange("a p d -> (a p) d"), x2[:, t, :]).then_inc(h_out, 16)

            turns(sp, NT // 2, residual_rows)

            sp.wait_ge(h_out, 16 * NT)
            sp.dma_start(gain_ffn[:, :], g_ffn[0:1, :].to_broadcast([P, D])).then_inc(gain_in[1], 16)
            with sp.Fori(0, NT // 2) as i:
                for t in range(2):
                    sp.wait_ge(turned, NT + 2 * i)
                    sp.dma_start(xt_ffn[:, t, :], h_dram[ds(2 * i + t, 1), :, :].rearrange("a p d -> (a p) d")).then_inc(x_in[t], 16)
            with sp.Fori(0, FT // 2) as i:
                sp.wait_ge(w_lo, UP0 - 1 + 4 * i)
                sp.dma_start(raw2[:, 0, :, :], w_up_v[:, :, ds(SW * i, SW)]).then_inc(raw_in[0], 16)
                sp.wait_ge(w_lo, UP0 + 4 * i)
                sp.dma_start(raw2[:, 1, :, :], w_up_v[:, :, ds(F + SW * i, SW)]).then_inc(raw_in[1], 16)

            sp.wait_ge(w_lo, PLE0)
            def load_down(k, t, hf):
                sp.dma_start(raw2[:, t, 0:2, :].rearrange("p a b -> p (a b)"),
                             w_down_v[:, ds(k, 1), 512 * hf:512 * hf + 512].rearrange("p a n -> p (a n)")).then_inc(d_in[t], 16)

            for hf in range(2):
                for t in range(2):
                    if hf:
                        sp.wait_ge(d_lo, FT + t - 1)
                    load_down(t, t, hf)
                with sp.Fori(1, FT // 2) as i:
                    for t in range(2):
                        sp.wait_ge(d_lo, FT * hf + 2 * i + t - 1)
                        load_down(2 * i + t, t, hf)
                if hf == 0:
                    sp.wait_ge(product, PLE0)
                    sp.dma_start(h[:, :, :], h_dram.rearrange("n p d -> p n d")).then_inc(h_in, 16)

            sp.wait_ge(freed[1], (N_IN + N_UP) // 2)
            sp.dma_start(gain_ple[:, :], g_ple[0:1, :].to_broadcast([P, D])).then_inc(gain_in[2], 16)
            sp.wait_ge(d_lo, 2 * FT)
            for j in range(2):
                sp.dma_start(raw2[:, j, :, :], w_gate_v[:, :, SW * j:SW * j + SW]).then_inc(raw_in[j], 16)
            sp.wait_ge(down_half, 2 * NT)
            sp.dma_start(p_tok[:, :, :], p_t).then_inc(p_in, 16)
            sp.dma_start(w_pup[:, :, :], w_pup_v).then_inc(pup_in, 16)
            sp.dma_start(gain_fin[:, :], g_final.rearrange("(a d) -> a d", a=1).to_broadcast([P, D])).then_inc(gain_in[3], 16)
            for j in range(2, 4):
                sp.wait_ge(w_lo, PLE0 + 2 * (j - 1))
                sp.dma_start(raw2[:, j % 2, :, :], w_gate_v[:, :, SW * j:SW * j + SW]).then_inc(raw_in[j % 2], 16)
            for n in range(NT):
                sp.wait_ge(normed, 3 * NT + n + 1)
                sp.dma_start(out_t[n], h[:, n, :]).then_inc(stored, 16)
            sp.wait_ge(stored, 16 * NT)

        def chunk(n):
            return ds(P * n, P)

        def f_off(l):
            return sum(HW >> m for m in range(l))

        def factor(t, l):
            return t[:, f_off(l):f_off(l) + (HW >> l)].rearrange("p (b two) -> p b two", two=2)

        @block.gpsimd
        def _(pool):
            nc.gpsimd.memset(ident[:, :], 0.0).then_inc(consts, 1)
            nc.gpsimd.memset(neg_half[:, :], -0.5).then_inc(consts, 1)
            pool.wait_ge(consts, 2)
            nc.gpsimd.affine_select(out=ident[:, :], in_=ident[:, :], compare_op=ALU.not_equal, fill=1.0, base=0,
                                    pattern=[[-1, P]], channel_multiplier=1).then_inc(consts, 1)

            def norm_rows(first):
                with pool.Fori(0, NT // 2) as i:
                    for t in range(2):
                        pool.wait_ge(squared, first + 2 * i + t + 1)
                        pool.sem_inc(turn_of_mean, 1)
                        nc.gpsimd.tensor_scalar(msq[:, t:t + 1], ssq[:, t:t + 1], 1.0 / D, EPS,
                                                ALU.mult, ALU.add).then_inc(mean_ready, 1)
                        pool.wait_ge(mean_ready, first + 2 * i + t + 1)
                        nc.gpsimd.tensor_tensor(rstd[:, t:t + 1], msq[:, t:t + 1], neg_half[:, 0:1],
                                                ALU.pow).then_inc(rstd_ready, 1)

            pool.wait_ge(consts, 3)
            nc.gpsimd.tensor_copy(ident_b[:, :], ident[:, :]).then_inc(mask_step, 1)
            nc.gpsimd.memset(level_mask[:, :], 1.0).then_inc(mask_step, 1)
            nc.gpsimd.memset(band[:, 0:3, :], 0.0).then_inc(mask_step, 1)
            nc.gpsimd.memset(band[:, 3, :], MASK_VALUE)
            norm_rows(0)
            steps = 3
            pool.wait_ge(mask_step, steps)
            for block_of_band, (op, sign) in enumerate(((ALU.is_gt, 1), (ALU.is_ge, -1), (ALU.is_gt, 1))):
                nc.gpsimd.affine_select(out=band[:, block_of_band, :], in_=band[:, block_of_band, :], compare_op=op,
                                        fill=MASK_VALUE, base=0, pattern=[[sign, P]],
                                        channel_multiplier=-sign).then_inc(mask_step, 1)
                steps += 1
            for l in range(LEVELS):
                b = 1 << l
                m = level_mask[:, 256 * l:256 * l + 256].rearrange("p (a c r) -> p a c r", a=HH, r=b)
                nc.gpsimd.affine_select(out=m, in_=m, compare_op=ALU.is_ge, fill=0.0, base=0,
                                        pattern=[[0, HH], [-2 * b, 64 // b], [0, b]],
                                        channel_multiplier=1).then_inc(mask_step, 1)
                steps += 1
                pool.wait_ge(mask_step, steps)
                nc.gpsimd.affine_select(out=m, in_=m, compare_op=ALU.is_ge, fill=0.0, base=b - 1,
                                        pattern=[[0, HH], [2 * b, 64 // b], [0, b]],
                                        channel_multiplier=-1).then_inc(mask_step, 1)
                steps += 1
            assert steps == MASK_STEPS

            pool.wait_ge(product, N_IN)
            nc.gpsimd.memset(kst[:, 1, :], 0.0).then_inc(start_ready, 1)
            nc.gpsimd.memset(FQ[:, :], 1.0).then_inc(start_ready, 1)
            nc.gpsimd.memset(FK[:, :], 1.0).then_inc(start_ready, 1)
            nc.gpsimd.memset(attT[:, :], 0.0).then_inc(start_ready, 1)
            nc.gpsimd.memset(state[:, :], 0.0).then_inc(start_ready, 1)
            nc.gpsimd.memset(av_tok[:, 0, :], 0.0).then_inc(start_ready, 1)

            def k_step(n, l):
                if l == 1:
                    wait(pool, k_turned, n)
                else:
                    pool.wait_ge(level_product, 8 * n + l)
                pool.wait_ge(k_level, 8 * n + l)
                pool.wait_ge(factors, 15 * n + 2 * l)
                b = 1 << (l - 1)
                nc.gpsimd.tensor_tensor(Kl[:, l % 2, :].rearrange("p (c r) -> p c r", r=b),
                                        Kl[:, (l - 1) % 2, :].rearrange("p (c r) -> p c r", r=b),
                                        FK[:, f_off(l - 1):f_off(l)].unsqueeze(2).to_broadcast([P, HW // b, b]),
                                        ALU.mult).then_inc(k_level, 1)

            def o_norm(n):
                pool.wait_ge(o_sum, n + 1)
                pool.sem_inc(turn_of_mean, 1)
                nc.gpsimd.tensor_scalar(msq[:, 2:2 + HH], ssq[:, 2:2 + HH], 1.0 / P, EPS,
                                        ALU.mult, ALU.add).then_inc(o_mean, 1)
                pool.wait_ge(o_mean, n + 1)
                nc.gpsimd.tensor_tensor(rstd[:, 2:2 + HH], msq[:, 2:2 + HH], neg_half[:, :],
                                        ALU.pow).then_inc(o_rstd, 1)

            def pool_tile(n, first=False):
                k_step(n, 1)
                if not first:
                    o_norm(n - 1)
                for l in range(2, LEVELS + 1):
                    k_step(n, l)

            pool_tile(0, True)
            pool_tile(1)
            with pool.Fori(1, NT // 2) as i:
                for t in range(2):
                    pool_tile(2 * i + t)
            o_norm(NT - 1)
            norm_rows(NT)
            norm_rows(2 * NT)
            norm_rows(3 * NT)

        N0 = 7
        N1 = 6

        def split_count(m):
            s = m // 2
            return sum(16 * len(in_strip(j)) for j in range(s % 2, s + 1, 2))

        def in_split(t, m):
            s = m // 2
            if t is raw1:
                if 8 <= s < 10:
                    return raw1[:, s % 2, :, :].rearrange("p k (a c) -> p k a c", a=2)[:, :, :, DH * (m % 2):DH * (m % 2) + DH]
                return raw1[:, s % 2, :, P * (m % 2):P * (m % 2) + P]
            v = t[:, m % 2, :, :]
            return v.rearrange("p k (a c) -> p k a c", a=2) if 8 <= s < 10 else v

        @block.scalar
        def _(act):
            def norm_turn(first, src, u, junk, load):
                def turn(i):
                    for t in range(2):
                        if load:
                            act.wait_ge(x_in[t], 16 * (load - 1) * (NT // 2) + 16 * i + 16)
                        wait(act, normed, first + 2 * i)
                        wait(act, squared, first + 2 * i + t)
                        nc.scalar.activation(junk, src(i, t), ACT.Square,
                                             accum_out=ssq[:, t:t + 1]).then_inc(squared, 1)
                    for t in range(2):
                        act.wait_ge(turned, first + 2 * i + t + 1)
                        nc.scalar.activation(u[:, :, ds(P * (2 * i + t), P)],
                                             Q[2 + t][:, :].rearrange("p (k c) -> p k c", c=P),
                                             ACT.Copy).then_inc(u_hi, 1)

                turns(act, NT // 2, turn)

            act.wait_ge(lb_step, 2)
            nc.scalar.activation(lbv[:, 2, :], lbv[:, 1, :], ACT.Exp).then_inc(lb_step, 1)
            norm_turn(0, lambda i, t: xt_mix[:, t, :], uh1, junk_mix[:, :], 1)

            def split_in(m):
                act.wait_ge(raw_in[(m // 2) % 2], split_count(m))
                if m >= 2:
                    act.wait_ge(product, m - 1)
                nc.scalar.activation(in_split(wh1, m), in_split(raw1, m), ACT.Copy).then_inc(w_hi, 1)

            split_in(0)
            for m in range(N_IN):
                if m + 1 < N_IN:
                    split_in(m + 1)
                act.wait_ge(product, m + 1)
                src = Q[m % 2][:, :]
                if m < 4:
                    nc.scalar.activation(qT[:, m, :], src, ACT.Sigmoid).then_inc(proj_act, 1)
                elif m < 8:
                    nc.scalar.activation(fT[:, m - 4, :], src, ACT.Sigmoid)
                    nc.scalar.activation(kT[:, m - 4, :], src, ACT.Sigmoid, scale=-1.0).then_inc(freed[m % 2], 1)
                elif m < 12:
                    nc.scalar.activation(vT[:, m - 8, :], src, ACT.Copy).then_inc(freed[m % 2], 1)
                elif m < 16:
                    nc.scalar.activation(sgT[:, m - 12, :], src, ACT.Sigmoid).then_inc(freed[m % 2], 1)
                elif m < 20:
                    nc.scalar.activation(aqT[:, m - 16, :], src, ACT.Copy).then_inc(freed[m % 2], 1)
                else:
                    nc.scalar.activation(akT[:, :] if m == 20 else vT[:, HH, :], src,
                                         ACT.Copy).then_inc(freed[m % 2], 1)

            for c in range(1, HH + 1, 2):
                act.wait_ge(v_turned, c + 1)
                nc.scalar.activation(v_tok[:, :, P * c:P * c + P], Q[3][:, :].rearrange("p (n c) -> p n c", c=P),
                                     ACT.Copy).then_inc(v_ready[1], 1)

            def static_operands(n, t):
                wait(act, scores, 2 * n)
                nc.scalar.activation(qst[:, :, :], aqT[:, :, chunk(n)], ACT.Copy).then_inc(qk_static, 1)
                nc.scalar.activation(kst[:, t, :], akT[:, chunk(n)], ACT.Copy).then_inc(qk_static, 1)
                wait(act, k_level, 8 * n)
                wait(act, level_product, 8 * n)
                nc.scalar.activation(Kl[:, 0, :].rearrange("p (a t) -> p a t", t=P), kT[:, :, chunk(n)],
                                     ACT.Copy).then_inc(k_level, 1)

            def exps(n, g):
                act.wait_ge(max_ready, 2 * n + g + 1)
                wait(act, probs_turned, 2 * n + g)
                for j in range(GR):
                    nc.scalar.activation(probs[:, j, :, :].rearrange("p a c -> p (a c)"),
                                         Q[0][:, 2 * P * j:2 * P * j + 2 * P], ACT.Exp,
                                         bias=smax[:, 2, GR * g + j:GR * g + j + 1], scale=DH ** -0.5,
                                         accum_out=sden[:, 0, GR * g + j:GR * g + j + 1]).then_inc(exped, 1)
                act.wait_ge(sink_arg, 2 * n + g + 1)
                nc.scalar.activation(sden[:, 2, GR * g:GR * g + GR], sden[:, 1, GR * g:GR * g + GR],
                                     ACT.Exp).then_inc(sink_exped, 1)

            def probs_out(n, g):
                act.wait_ge(probs_turned, 2 * n + g + 1)
                wait(act, attended, 2 * n + g)
                nc.scalar.activation(probsT[:, :, :, :].rearrange("p a b c -> p (a b c)"), Q[1][:, :],
                                     ACT.Copy).then_inc(probsT_ready, 1)

            def chunk_end(n):
                act.wait_ge(k_turned, n + 1)
                wait(act, delta_ready, n)
                nc.scalar.activation(k_tok[:, :], Q[3][:, 512:1024], ACT.Copy).then_inc(k_tok_ready, 1)
                act.wait_ge(o_ready, n + 1)
                wait(act, o_sum, n)
                nc.scalar.activation(osq[:, :], Q[3][:, 0:512], ACT.Square).then_inc(o_squared, 1)

            def y_att_out(n):
                act.wait_ge(y_turned, n + 1)
                nc.scalar.activation(yT[:, HH:KT, :].rearrange("p k c -> p (k c)"), Q[1][:, 512:1024],
                                     ACT.Copy).then_inc(yT_at, 1)

            def act_tile(n, t, first=False):
                static_operands(n, t)
                if not first:
                    chunk_end(n - 1)
                exps(n, 0)
                if not first:
                    y_att_out(n - 1)
                probs_out(n, 0)
                exps(n, 1)
                probs_out(n, 1)

            act_tile(0, 0, True)
            act_tile(1, 1)
            with act.Fori(1, NT // 2) as i:
                for t in range(2):
                    act_tile(2 * i + t, t)
            chunk_end(NT - 1)
            y_att_out(NT - 1)

            norm_turn(NT, lambda i, t: xt_ffn[:, t, :], uh2, junk_ffn[:, :], 2)

            def split_up(i, q):
                act.wait_ge(raw_in[q % 2], 16 * (N0 if q % 2 == 0 else N1) + 16 * i + 16)
                act.wait_ge(product, UP0 - 1 + 4 * i + q)
                nc.scalar.activation(wh2[:, q % 2, :, :], raw2[:, q % 2, :, P * (q // 2):P * (q // 2) + P],
                                     ACT.Copy).then_inc(w_hi, 1)

            def up_turn(i, last):
                for q in range(4):
                    if q < 3:
                        split_up(i, q + 1)
                    elif not last:
                        split_up(i + 1, 0)
                    f = 2 * i + q // 2
                    if q % 2 == 0:
                        act.wait_ge(product, UP0 + 4 * i + q + 1)
                        act.wait_ge(freed[1], N_IN // 2 - 1 + f)
                        nc.scalar.activation(conv[:, q // 2, :], Q[q][:, :], ACT.Identity,
                                             bias=cols[:, ds(CONV_B0 + f, 1)],
                                             scale=cols[:, ds(CONV_W0 + 2 * FT + f, 1)]).then_inc(conv_a, 1)
                    else:
                        act.wait_ge(freed[0], N_IN // 2 + f + 1)
                        nc.scalar.activation(sgm[:, :], conv[:, q // 2, :], ACT.Sigmoid).then_inc(conv_sig, 1)

            split_up(0, 0)
            with act.Fori(0, FT // 2 - 1) as i:
                up_turn(i, False)
            up_turn(FT // 2 - 1, True)

            act.wait_ge(product, PLE0)
            act.wait_ge(w_lo, PLE0)
            def split_down(k, t, s):
                if s is not None:
                    act.wait_ge(d_in[t], 16 * (FT // 2) * (s // FT) + 16)
                nc.scalar.activation(gh[:, t, :], G[:, ds(k, 1), :].rearrange("p a s -> p (a s)"),
                                     ACT.Copy).then_inc(g_hi, 1)
                nc.scalar.activation(dh[:, t, :], raw2[:, t, 0:2, :].rearrange("p a b -> p (a b)"),
                                     ACT.Copy).then_inc(d_hi, 1)

            act.wait_ge(freed[1], (N_IN + N_UP) // 2)
            for hf in range(2):
                for t in range(2):
                    if hf and t == 0:
                        act.wait_ge(down_step, FT - 1)
                    if hf and t == 1:
                        act.wait_ge(down_half, NT)
                    split_down(t, t, FT * hf + t)
                with act.Fori(1, FT // 2) as i:
                    for t in range(2):
                        act.wait_ge(down_step, (FT - 1) * hf + 2 * i + t - 1)
                        act.wait_ge(d_in[t], 16 * (FT // 2) * hf + 16 * i + 16)
                        split_down(2 * i + t, t, None)

            act.wait_ge(h_added, 2 * NT)
            norm_turn(2 * NT, lambda i, t: h[:, ds(2 * i + t, 1), :].rearrange("p a d -> p (a d)"), uh3,
                      junk_ple[:, :], 0)
            for k in range(PK):
                act.wait_ge(p_turned, k + 1)
                nc.scalar.activation(pTh[:, k, :], Q[2 + k][:, :], ACT.Copy).then_inc(p_hi, 1)

            def split_ple(c):
                act.wait_ge(raw_in[(c // 2) % 2], 16 * ((N0, N1)[(c // 2) % 2] + FT // 2 + c // 4 + 1))
                act.wait_ge(product, PLE0 - 1 + c)
                nc.scalar.activation(wh2[:, c % 2, :, :], raw2[:, (c // 2) % 2, :, P * (c % 2):P * (c % 2) + P],
                                     ACT.Copy).then_inc(w_hi, 1)
                act.wait_ge(pup_in, 16)
                nc.scalar.activation(pwh[:, c % 2, :, :], w_pup[:, :, P * c:P * c + P], ACT.Copy).then_inc(pw_hi, 1)

            split_ple(0)
            for c in range(N_PLE):
                if c + 1 < N_PLE:
                    split_ple(c + 1)
                act.wait_ge(product, PLE0 + c + 1)
                if c >= 2:
                    act.wait_ge(ple_turned, c - 1)
                nc.scalar.activation(pleT[:, c % 2, :], Q[2 * (c % 2)][:, :], ACT.Sigmoid).then_inc(ple_gate, 1)
            act.wait_ge(ple_added, N_PLE)
            with act.Fori(0, NT // 2) as i:
                for t in range(2):
                    act.wait_ge(normed, 3 * NT + 2 * i)
                    act.wait_ge(squared, 3 * NT + 2 * i + t)
                    nc.scalar.activation(junk_ple[:, :], h[:, ds(2 * i + t, 1), :].rearrange("p a d -> p (a d)"),
                                         ACT.Square, accum_out=ssq[:, t:t + 1]).then_inc(squared, 1)

        def parts(wh, wl, uh, ul):
            return ((wh, uh), (wh, ul), (wl, uh))

        @block.tensor
        def _(pe):
            def turn_rows(first, src):
                def turn(i):
                    for t in range(2):
                        pe.wait_ge(normed, first + 2 * i + t + 1)
                        wait(pe, u_lo, first + 2 * i)
                        for k in range(KT):
                            tr = nc.tensor.transpose(Q[2 + t][:, P * k:P * k + P], src[:, t, P * k:P * k + P],
                                                     ident[:, :])
                        tr.then_inc(turned, 1)

                turns(pe, NT // 2, turn)

            def project(wh, wl, uh, ul, slot, dst, kt):
                for k in range(kt):
                    for a, b in parts(wh, wl, uh, ul):
                        for half in range(2):
                            mm = nc.tensor.matmul(dst[:, 512 * half:512 * half + 512], a[:, slot, k, :],
                                                  b[:, k, 512 * half:512 * half + 512],
                                                  start=(k == 0 and a is wh and b is uh),
                                                  stop=(k == kt - 1 and a is wl))
                return mm

            pe.wait_ge(consts, 3)
            pe.wait_ge(rows_in, 64)
            nc.tensor.transpose(Q[0][:, 0:96], rows[0:96, :], ident[0:96, 0:96]).then_inc(colsT, 1)
            turn_rows(0, xt_mix)
            pe.wait_ge(cols_ready, 1)
            pe.wait_ge(u_lo, NT)

            def in_turn(i):
                for t in range(2):
                    pe.wait_ge(w_lo, 2 * i + t + 1)
                    wait(pe, freed[t], i)
                    project(wh1, wl1, uh1, ul1, t, Q[t], KT).then_inc(product, 1)

            turns(pe, N_IN // 2, in_turn)

            pe.wait_ge(freed[1], N_IN // 2)
            for c in range(HH + 1):
                if c >= 2:
                    pe.wait_ge(v_ready[c % 2], c // 2)
                for n in range(NT):
                    tr = nc.tensor.transpose(Q[2 + c % 2][:, P * n:P * n + P], vT[:, c, P * n:P * n + P], ident[:, :])
                tr.then_inc(v_turned, 1)

            def score(n, t, g, first):
                if g == 0:
                    pe.wait_ge(qk_static, 2 * n + 2)
                    wait(pe, exped, 8 * n)
                else:
                    pe.wait_ge(exped, 8 * n + 4)
                mask = band[:, 0:2, :] if t else band[:, 1:4:2, :] if first else band[:, 1:3, :]
                for j in range(GR):
                    dst = Q[0][:, 2 * P * j:2 * P * j + 2 * P]
                    nc.tensor.matmul(dst, qst[DH * g:DH * g + DH, j, :],
                                     kst[DH * g:DH * g + DH, :, :].rearrange("p a c -> p (a c)"), start=True, stop=False)
                    mm = nc.tensor.matmul(dst.rearrange("p (a c) -> p a c", a=2), ident_b[:, :], mask,
                                          start=False, stop=True)
                mm.then_inc(scores, 1)

            def turn_probs(n, g):
                pe.wait_ge(exped, 8 * n + 4 * g + 4)
                if g == 0:
                    wait(pe, yT_hg, n)
                    wait(pe, yT_at, n)
                else:
                    pe.wait_ge(probsT_ready, 2 * n + 1)
                for j in range(GR):
                    for s in range(2):
                        c = P * (2 * j + s)
                        tr = nc.tensor.transpose(Q[1][:, c:c + P], probs[:, j, s, :], ident[:, :])
                tr.then_inc(probs_turned, 1)

            def attend(n, t, g):
                pe.wait_ge(probsT_ready, 2 * n + g + 1)
                if g == 0:
                    wait(pe, y_hg, n)
                for j in range(GR):
                    for s in range(2):
                        blk = n + 1 if s == t else n
                        c = DH * (GR * g + j)
                        mm = nc.tensor.matmul(Q[3][:, c:c + DH], probsT[:, j, s, :],
                                              av_tok[:, ds(blk, 1), DH * g:DH * g + DH].rearrange("p a c -> p (a c)"),
                                              start=(s == 0), stop=(s == 1))
                mm.then_inc(attended, 1)

            def level(n, g):
                if g >= 2:
                    pe.wait_ge(picked, 8 * n + g - 1)
                else:
                    wait(pe, picked, 8 * n + g - 1)
                l = max(g - 1, 0)
                pe.wait_ge(k_level, 8 * n + l + 1)
                if g:
                    pe.wait_ge(q_level, 8 * n + l + 1)
                b = 1 << l
                base = 512 * (g % 2)
                for a in range(HH):
                    keys = Kl[:, l % 2, P * a:P * a + P]
                    if g == 0:
                        mm = nc.tensor.matmul(Q[2][:, base + P * a:base + P * a + P], keys, qT[:, a, chunk(n)],
                                              start=True, stop=True)
                    else:
                        right = Ql[:, l % 2, P * a:P * a + P].rearrange("p (c two r) -> p c two r", two=2, r=b)[:, :, 1, :]
                        mm = nc.tensor.matmul(Q[2][:, base + 64 * a:base + 64 * a + 64].rearrange("p (c r) -> p c r", r=b),
                                              keys, right, start=True, stop=True)
                mm.then_inc(level_product, 1)

            def hgrn_out(n):
                pe.wait_ge(q_level, 8 * n + 8)
                pe.wait_ge(k_level, 8 * n + 8)
                wait(pe, state_ready, 4 * n)
                wait(pe, h_half, 2 * n)
                for a in range(HH):
                    tr = nc.tensor.transpose(Q[3][:, 512 + P * a:512 + P * a + P], Kl[:, 1, P * a:P * a + P], ident[:, :])
                tr.then_inc(k_turned, 1)
                pe.wait_ge(picked, 8 * n + 8)
                pe.wait_ge(y_att, n + 1)
                for a in range(HH):
                    c = slice(P * a, P * a + P)
                    nc.tensor.matmul(Q[3][:, c], Ql[:, 1, c], state[:, c], start=True, stop=False)
                    mm = nc.tensor.matmul(Q[3][:, c], attT[:, c],
                                          v_tok[:, ds(n, 1), c].rearrange("p a c -> p (a c)"), start=False, stop=True)
                mm.then_inc(o_ready, 1)
                pe.wait_ge(k_tok_ready, n + 1)
                for a in range(HH):
                    c = slice(P * a, P * a + P)
                    mm = nc.tensor.matmul(Q[3][:, 512 + P * a:512 + P * a + P], k_tok[:, c],
                                          v_tok[:, ds(n, 1), c].rearrange("p a c -> p (a c)"), start=True, stop=True)
                mm.then_inc(delta_ready, 1)

            def turn_y(n):
                pe.wait_ge(y_hg, n + 1)
                pe.wait_ge(probsT_ready, 2 * n + 2)
                for k in range(KT):
                    tr = nc.tensor.transpose(Q[1][:, P * k:P * k + P], y_tok[:, P * k:P * k + P], ident[:, :])
                tr.then_inc(y_turned, 1)

            def mix_out(n, half, part):
                if part == 0 and half == 0:
                    pe.wait_ge(yT_hg, n + 1)
                    pe.wait_ge(yT_at, n + 1)
                    wait(pe, state_ready, 4 * min(n + 1, NT - 1) if isinstance(n, int) else 4 * n + 4)
                elif part == 0:
                    pe.wait_ge(h_half, 2 * n + 1)
                for k in range(KT // 2 * part, KT // 2 * part + KT // 2):
                    mm = nc.tensor.matmul(Q[3][:, 512:1024], yT[:, k, :], wo[:, k, halves(half)], start=(k == 0),
                                          stop=(k == KT - 1))
                if part:
                    mm.then_inc(mixed, 1)

            def pe_tile(n, t, first=False):
                score(n, t, 0, first)
                level(n, 0)
                level(n, 1)
                if not first:
                    turn_y(n - 1)
                level(n, 2)
                turn_probs(n, 0)
                score(n, t, 1, first)
                if not first:
                    mix_out(n - 1, 0, 0)
                level(n, 3)
                attend(n, t, 0)
                turn_probs(n, 1)
                level(n, 4)
                if not first:
                    mix_out(n - 1, 0, 1)
                level(n, 5)
                attend(n, t, 1)
                if not first:
                    mix_out(n - 1, 1, 0)
                level(n, 6)
                if not first:
                    mix_out(n - 1, 1, 1)
                level(n, 7)
                hgrn_out(n)

            pe.wait_ge(mask_step, MASK_STEPS)
            pe.wait_ge(start_ready, START_STEPS)
            for n in range(2):
                pe.wait_ge(v_ready[n], (HH + 2 - n) // 2)
            pe.wait_ge(scaled, 12)
            pe_tile(0, 0, True)
            pe.wait_ge(wo_in, 16 * KT)
            pe_tile(1, 1)
            with pe.Fori(1, NT // 2) as i:
                for t in range(2):
                    pe_tile(2 * i + t, t)
            turn_y(NT - 1)
            for half in range(2):
                mix_out(NT - 1, half, 0)
                mix_out(NT - 1, half, 1)

            turn_rows(NT, xt_ffn)
            pe.wait_ge(u_lo, 2 * NT)
            pe.wait_ge(h_half, 2 * NT)
            with pe.Fori(0, FT // 2) as i:
                for q in range(4):
                    pe.wait_ge(w_lo, UP0 + 4 * i + q + 1)
                    pe.wait_ge(freed[q % 2], N_IN // 2 - 1 + 2 * i + q // 2)
                    project(wh2, wl2, uh2, ul2, q % 2, Q[q], KT).then_inc(product, 1)

            def down(k, t, hf, first, last):
                s = hf * FT + k
                pe.wait_ge(d_lo, s + 1)
                pe.wait_ge(g_lo, s + 1)
                for n in range(NT):
                    if first and hf:
                        pe.wait_ge(h_added, n + 1)
                    for j, (a, b) in enumerate(parts(gh, gl, dh, dl)):
                        mm = nc.tensor.matmul(acc[n], a[:, t, P * n:P * n + P], b[:, t, :],
                                              start=(first and j == 0), stop=(last and j == 2))
                    if last:
                        mm.then_inc(down_half, 1)
                return mm

            pe.wait_ge(freed[0], (N_IN + N_UP) // 2)
            pe.wait_ge(freed[1], (N_IN + N_UP) // 2)
            for hf in range(2):
                down(0, 0, hf, True, False).then_inc(down_step, 1)
                down(1, 1, hf, False, False).then_inc(down_step, 1)
                with pe.Fori(1, FT // 2 - 1) as i:
                    for t in range(2):
                        down(2 * i + t, t, hf, False, False).then_inc(down_step, 1)
                down(FT - 2, 0, hf, False, False).then_inc(down_step, 1)
                down(FT - 1, 1, hf, False, True)

            pe.wait_ge(h_added, 2 * NT)
            turn_rows(2 * NT, un_ple)
            pe.wait_ge(u_lo, 3 * NT)
            pe.wait_ge(p_in, 16)
            for k in range(PK):
                for n in range(NT):
                    tr = nc.tensor.transpose(Q[2 + k][:, P * n:P * n + P], p_tok[:, n, P * k:P * k + P], ident[:, :])
                tr.then_inc(p_turned, 1)
            pe.wait_ge(p_lo, PK)

            def turn_ple(c):
                pe.wait_ge(ple_ready, c + 1)
                for n in range(NT):
                    tr = nc.tensor.transpose(Q[2 * (c % 2)][:, P * n:P * n + P], pleT[:, c % 2, P * n:P * n + P],
                                             ident[:, :])
                tr.then_inc(ple_turned, 1)

            for c in range(N_PLE):
                pe.wait_ge(w_lo, PLE0 + c + 1)
                pe.wait_ge(pw_lo, c + 1)
                if c >= 2:
                    pe.wait_ge(ple_added, c - 1)
                project(wh2, wl2, uh3, ul3, c % 2, Q[2 * (c % 2)], KT)
                project(pwh, pwl, pTh, pTl, c % 2, Q[2 * (c % 2) + 1], PK).then_inc(product, 1)
                if c:
                    turn_ple(c - 1)
            turn_ple(N_PLE - 1)

        @block.vector
        def _(dve):
            def norm_turn(first, src, out_rows, gain, ul, uh):
                def turn(i):
                    for t in range(2):
                        dve.wait_ge(rstd_ready, first + 2 * i + t + 1)
                        wait(dve, turned, first + 2 * i)
                        nc.vector.scalar_tensor_tensor(out=out_rows[:, t, :], in0=src(i, t), scalar=rstd[:, t:t + 1],
                                                       in1=gain[:, :], op0=ALU.mult, op1=ALU.mult).then_inc(normed, 1)
                    for t in range(2):
                        dve.wait_ge(u_hi, first + 2 * i + t + 1)
                        at = ds(P * (2 * i + t), P)
                        nc.vector.tensor_tensor(ul[:, :, at], Q[2 + t][:, :].rearrange("p (k c) -> p k c", c=P),
                                                uh[:, :, at].bitcast(F32), ALU.subtract).then_inc(u_lo, 1)

                turns(dve, NT // 2, turn)

            dve.wait_ge(colsT, 1)
            nc.vector.tensor_copy(cols[:, 0:96], Q[0][:, 0:96]).then_inc(cols_ready, 1)
            dve.wait_ge(cols_ready, 1)
            nc.vector.tensor_copy(lbv[:, 0, :], cols[:, LB0:LB0 + HH]).then_inc(lb_step, 1)
            dve.wait_ge(lb_step, 1)
            nc.vector.tensor_tensor(lbv[:, 1, :], cols[:, LB0:LB0 + HH], lbv[:, 0, :], ALU.subtract).then_inc(lb_step, 1)
            dve.wait_ge(lb_step, 3)
            nc.vector.reciprocal(lbv[:, 3, :], lbv[:, 2, :]).then_inc(lb_step, 1)
            dve.wait_ge(lb_step, 4)
            nc.vector.tensor_tensor(lbv[:, 4, :], lbv[:, 2, :], lbv[:, 3, :], ALU.mult).then_inc(lb_step, 1)
            dve.wait_ge(lb_step, 5)
            nc.vector.tensor_tensor(lbv[:, 5, :], lbv[:, 4, :], lbv[:, 4, :], ALU.subtract).then_inc(lb_step, 1)
            dve.wait_ge(lb_step, 6)
            nc.vector.tensor_scalar(lbv[:, 6, :], lbv[:, 5, :], LB_FLOOR, None, ALU.max).then_inc(lb_step, 1)
            nc.vector.tensor_scalar(lbv[:, 7, :], lbv[:, 5, :], -1.0, 1.0, ALU.mult, ALU.add).then_inc(lb_step, 1)

            dve.wait_ge(gain_in[0], 16)
            norm_turn(0, lambda i, t: xt_mix[:, t, :], xt_mix, gain_mix, ul1, uh1)

            def split_in(m):
                dve.wait_ge(w_hi, m + 1)
                nc.vector.tensor_tensor(in_split(wl1, m), in_split(raw1, m), in_split(wh1, m).bitcast(F32),
                                        ALU.subtract).then_inc(w_lo, 1)

            dve.wait_ge(lb_step, 8)
            split_in(0)
            for m in range(N_IN):
                if m + 1 < N_IN:
                    split_in(m + 1)
                if m < 4:
                    dve.wait_ge(proj_act, m + 1)
                    nc.vector.tensor_tensor(qT[:, m, :], Q[m % 2][:, :], qT[:, m, :], ALU.mult).then_inc(freed[m % 2], 1)
                elif m < 8:
                    a = m - 4
                    dve.wait_ge(freed[m % 2], m // 2 + 1)
                    nc.vector.tensor_scalar(fT[:, a, :], fT[:, a, :], lbv[:, 7, a:a + 1], lbv[:, 6, a:a + 1],
                                            ALU.mult, ALU.add).then_inc(scaled, 1)
                    nc.vector.tensor_scalar(kT[:, a, :], kT[:, a, :], lbv[:, 7, a:a + 1], None,
                                            ALU.mult).then_inc(scaled, 1)
                elif 12 <= m < 16:
                    a = m - 12
                    dve.wait_ge(freed[m % 2], m // 2 + 1)
                    nc.vector.tensor_scalar(sgT[:, a, :], sgT[:, a, :], cols[:, HGG0 + a:HGG0 + a + 1], None,
                                            ALU.mult).then_inc(scaled, 1)

            dve.wait_ge(product, N_IN)
            for c in range(0, HH + 1, 2):
                dve.wait_ge(v_turned, c + 1)
                dst = v_tok[:, :, P * c:P * c + P] if c < HH else av_tok[:, 1:NT + 1, :]
                nc.vector.tensor_copy(dst, Q[2][:, :].rearrange("p (n c) -> p n c", c=P)).then_inc(v_ready[0], 1)

            def row_max(n, g):
                dve.wait_ge(scores, 2 * n + g + 1)
                c = slice(GR * g, GR * g + GR)
                z = 4 * n + 2 * g
                nc.vector.tensor_reduce(smax[:, 0, c], Q[0][:, :].rearrange("p (j k) -> p j k", j=GR), AX.X,
                                        ALU.max).then_inc(max_step, 1)
                dve.wait_ge(max_step, z + 1)
                nc.vector.scalar_tensor_tensor(out=smax[:, 1, c], in0=smax[:, 0, c], scalar=DH ** -0.5, in1=sink[:, c],
                                               op0=ALU.mult, op1=ALU.max).then_inc(max_step, 1)
                dve.wait_ge(max_step, z + 2)
                nc.vector.tensor_scalar(smax[:, 2, c], smax[:, 1, c], -1.0, None, ALU.mult).then_inc(max_ready, 1)
                nc.vector.tensor_tensor(sden[:, 1, c], sink[:, c], smax[:, 1, c], ALU.subtract).then_inc(sink_arg, 1)

            def denominators(n):
                dve.wait_ge(exped, 8 * n + 8)
                dve.wait_ge(sink_exped, 2 * n + 2)
                nc.vector.tensor_tensor(sden[:, 3, :], sden[:, 0, :], sden[:, 2, :], ALU.add).then_inc(den_step, 1)
                dve.wait_ge(den_step, n + 1)
                nc.vector.reciprocal(sden[:, 4, :], sden[:, 3, :]).then_inc(den_ready, 1)

            def att_rows(n):
                dve.wait_ge(attended, 2 * n + 2)
                dve.wait_ge(den_ready, n + 1)
                wait(dve, y_turned, n)
                nc.vector.tensor_tensor(y_tok[:, HW:D].rearrange("p (h d) -> p h d", d=DH),
                                        Q[3][:, 0:512].rearrange("p (h d) -> p h d", d=DH),
                                        sden[:, 4, :].unsqueeze(2).to_broadcast([P, QH, DH]), ALU.mult).then_inc(y_att, 1)

            def factor_step(n, l):
                if l == 0:
                    wait(dve, k_level, 8 * n)
                    wait(dve, q_level, 8 * n)
                    f = fT[:, :, chunk(n)].rearrange("p a (c two) -> p a c two", two=2)
                    nc.vector.tensor_copy(factor(FQ, 0)[:, :, 1].rearrange("p (a c) -> p a c", a=HH),
                                          f[:, :, :, 0]).then_inc(factors, 1)
                    nc.vector.tensor_copy(factor(FK, 0)[:, :, 0].rearrange("p (a c) -> p a c", a=HH),
                                          f[:, :, :, 1]).then_inc(factors, 1)
                    return
                dve.wait_ge(factors, 15 * n + 2 * l)
                left, right = factor(FQ, l - 1)[:, :, 1], factor(FK, l - 1)[:, :, 0]
                if l == LEVELS:
                    nc.vector.tensor_tensor(total[:, :], left, right, ALU.mult).then_inc(factors, 1)
                    return
                left = left.rearrange("p (c two) -> p c two", two=2)
                right = right.rearrange("p (c two) -> p c two", two=2)
                nc.vector.tensor_tensor(factor(FQ, l)[:, :, 1], left[:, :, 0], right[:, :, 0],
                                        ALU.mult).then_inc(factors, 1)
                nc.vector.tensor_tensor(factor(FK, l)[:, :, 0], left[:, :, 1], right[:, :, 1],
                                        ALU.mult).then_inc(factors, 1)

            def q_step(n, l):
                if l == 0:
                    wait(dve, level_product, 8 * n)
                    nc.vector.tensor_tensor(Ql[:, 0, :].rearrange("p (a t) -> p a t", t=P), qT[:, :, chunk(n)],
                                            fT[:, :, chunk(n)], ALU.mult).then_inc(q_level, 1)
                    return
                if l == 1:
                    wait(dve, o_ready, n)
                else:
                    dve.wait_ge(level_product, 8 * n + l)
                dve.wait_ge(q_level, 8 * n + l)
                dve.wait_ge(factors, 15 * n + 2 * l)
                b = 1 << (l - 1)
                nc.vector.tensor_tensor(Ql[:, l % 2, :].rearrange("p (c r) -> p c r", r=b),
                                        Ql[:, (l - 1) % 2, :].rearrange("p (c r) -> p c r", r=b),
                                        FQ[:, f_off(l - 1):f_off(l)].unsqueeze(2).to_broadcast([P, HW // b, b]),
                                        ALU.mult).then_inc(q_level, 1)

            def pick(n, g):
                dve.wait_ge(level_product, 8 * n + g + 1)
                base = 512 * (g % 2)
                if g == 0:
                    wait(dve, o_ready, n)
                else:
                    dve.wait_ge(picked, 8 * n + g)
                dve.sem_inc(turn_of_pick, 1)
                if g == 0:
                    nc.vector.copy_predicated(attT[:, :].rearrange("p (a t) -> p a t", t=P),
                                              ident_b[:, :].bitcast(U16).unsqueeze(1).to_broadcast([P, HH, P]),
                                              Q[2][:, base:base + HW].rearrange("p (a t) -> p a t", t=P)).then_inc(picked, 1)
                    return
                b = 1 << (g - 1)
                m = level_mask[:, 256 * (g - 1):256 * g].bitcast(U16)
                nc.vector.copy_predicated(attT[:, :].rearrange("p (c two r) -> p c two r", two=2, r=b)[:, :, 1, :],
                                          m.rearrange("p (c r) -> p c r", r=b),
                                          Q[2][:, base:base + 256].rearrange("p (c r) -> p c r", r=b)).then_inc(picked, 1)

            def output_half(n, t, pair, half):
                dve.wait_ge(mixed, 2 * n + half + 1)
                dve.wait_ge(x2_in[t], 16 * pair + 16)
                nc.vector.tensor_tensor(x2[:, t, halves(half)], Q[3][:, 512:1024], x2[:, t, halves(half)],
                                        ALU.add).then_inc(h_half, 1)

            def o_sums(n):
                dve.wait_ge(o_squared, n + 1)
                nc.vector.tensor_reduce(ssq[:, 2:2 + HH], osq[:, :].rearrange("p (a c) -> p a c", a=HH), AX.X,
                                        ALU.add).then_inc(o_sum, 1)

            def next_state(n):
                dve.wait_ge(delta_ready, n + 1)
                dve.wait_ge(factors, 15 * n + 15)
                for a in range(HH):
                    c = slice(P * a, P * a + P)
                    nc.vector.scalar_tensor_tensor(out=state[:, c], in0=state[:, c], scalar=total[:, a:a + 1],
                                                   in1=Q[3][:, 512 + P * a:512 + P * a + P], op0=ALU.mult,
                                                   op1=ALU.add).then_inc(state_ready, 1)

            def hg_rows(n):
                dve.wait_ge(o_rstd, n + 1)
                nc.vector.tensor_tensor(y_tok[:, 0:HW].rearrange("p (a c) -> p a c", a=HH),
                                        Q[3][:, 0:512].rearrange("p (a c) -> p a c", a=HH),
                                        rstd[:, 2:2 + HH].unsqueeze(2).to_broadcast([P, HH, P]),
                                        ALU.mult).then_inc(y_hg, 1)

            def gated_rows(n):
                dve.wait_ge(y_turned, n + 1)
                nc.vector.tensor_tensor(yT[:, 0:HH, :], Q[1][:, 0:512].rearrange("p (a c) -> p a c", a=HH),
                                        sgT[:, :, chunk(n)], ALU.mult).then_inc(yT_hg, 1)

            def dve_tile(n, t, pair, first=False):
                last_pair = pair - 1 + t
                factor_step(n, 0)
                q_step(n, 0)
                factor_step(n, 1)
                if not first:
                    o_sums(n - 1)
                q_step(n, 1)
                if not first:
                    next_state(n - 1)
                    hg_rows(n - 1)
                row_max(n, 0)
                pick(n, 0)
                pick(n, 1)
                factor_step(n, 2)
                q_step(n, 2)
                if not first:
                    gated_rows(n - 1)
                pick(n, 2)
                factor_step(n, 3)
                q_step(n, 3)
                row_max(n, 1)
                pick(n, 3)
                factor_step(n, 4)
                q_step(n, 4)
                pick(n, 4)
                factor_step(n, 5)
                q_step(n, 5)
                denominators(n)
                if not first:
                    output_half(n - 1, 1 - t, last_pair, 0)
                pick(n, 5)
                factor_step(n, 6)
                q_step(n, 6)
                att_rows(n)
                pick(n, 6)
                factor_step(n, 7)
                q_step(n, 7)
                if not first:
                    output_half(n - 1, 1 - t, last_pair, 1)
                pick(n, 7)

            dve.wait_ge(sink_in, 16)
            dve.wait_ge(mask_step, MASK_STEPS)
            dve.wait_ge(start_ready, START_STEPS)
            dve.wait_ge(scaled, 12)
            dve_tile(0, 0, 0, True)
            dve_tile(1, 1, 0)
            with dve.Fori(1, NT // 2) as i:
                for t in range(2):
                    dve_tile(2 * i + t, t, i)
            o_sums(NT - 1)
            hg_rows(NT - 1)
            gated_rows(NT - 1)
            for half in range(2):
                output_half(NT - 1, 1, NT // 2 - 1, half)

            dve.wait_ge(gain_in[1], 16)
            norm_turn(NT, lambda i, t: xt_ffn[:, t, :], xt_ffn, gain_ffn, ul2, uh2)

            def split_up(i, q):
                dve.wait_ge(w_hi, UP0 + 4 * i + q + 1)
                nc.vector.tensor_tensor(wl2[:, q % 2, :, :], raw2[:, q % 2, :, P * (q // 2):P * (q // 2) + P],
                                        wh2[:, q % 2, :, :].bitcast(F32), ALU.subtract).then_inc(w_lo, 1)

            def up_turn(i, last):
                for q in range(4):
                    if q < 3:
                        split_up(i, q + 1)
                    elif not last:
                        split_up(i + 1, 0)
                    f = 2 * i + q // 2
                    cv = conv[:, q // 2, :]
                    if q % 2 == 0:
                        dve.wait_ge(conv_a, f + 1)
                        nc.vector.scalar_tensor_tensor(out=cv[:, 1:S], in0=Q[q][:, 0:S - 1],
                                                       scalar=cols[:, ds(CONV_W0 + FT + f, 1)], in1=cv[:, 1:S],
                                                       op0=ALU.mult, op1=ALU.add).then_inc(conv_b1, 1)
                        dve.wait_ge(conv_b1, f + 1)
                        nc.vector.scalar_tensor_tensor(out=cv[:, 2:S], in0=Q[q][:, 0:S - 2],
                                                       scalar=cols[:, ds(CONV_W0 + f, 1)], in1=cv[:, 2:S],
                                                       op0=ALU.mult, op1=ALU.add).then_inc(freed[0], 1)
                    else:
                        dve.wait_ge(conv_sig, f + 1)
                        nc.vector.tensor_tensor(cv, cv, sgm[:, :], ALU.mult).then_inc(silued, 1)
                        dve.wait_ge(silued, f + 1)
                        dve.wait_ge(product, UP0 + 4 * i + q + 1)
                        nc.vector.tensor_tensor(G[:, ds(f, 1), :].rearrange("p a s -> p (a s)"), Q[q][:, :], cv,
                                                ALU.mult).then_inc(freed[1], 1)
            split_up(0, 0)
            with dve.Fori(0, FT // 2 - 1) as i:
                up_turn(i, False)
            up_turn(FT // 2 - 1, True)

            def split_down(k, t, s):
                dve.wait_ge(g_hi, s + 1)
                nc.vector.tensor_tensor(gl[:, t, :], G[:, ds(k, 1), :].rearrange("p a s -> p (a s)"),
                                        gh[:, t, :].bitcast(F32), ALU.subtract).then_inc(g_lo, 1)
                dve.wait_ge(d_hi, s + 1)
                nc.vector.tensor_tensor(dl[:, t, :], raw2[:, t, 0:2, :].rearrange("p a b -> p (a b)"),
                                        dh[:, t, :].bitcast(F32), ALU.subtract).then_inc(d_lo, 1)

            def add_down(hf):
                for n in range(NT):
                    dve.wait_ge(down_half, NT * hf + n + 1)
                    c = halves(hf)
                    nc.vector.tensor_tensor(h[:, n, c], acc[n], h[:, n, c], ALU.add).then_inc(h_added, 1)

            with dve.Fori(0, FT // 2) as i:
                for t in range(2):
                    split_down(2 * i + t, t, 2 * i + t)
            split_down(0, 0, FT)
            dve.wait_ge(h_in, 16)
            add_down(0)
            split_down(1, 1, FT + 1)
            with dve.Fori(1, FT // 2) as i:
                for t in range(2):
                    split_down(2 * i + t, t, FT + 2 * i + t)
            add_down(1)

            dve.wait_ge(gain_in[2], 16)
            norm_turn(2 * NT, lambda i, t: h[:, ds(2 * i + t, 1), :].rearrange("p a d -> p (a d)"), un_ple,
                      gain_ple, ul3, uh3)
            for k in range(PK):
                dve.wait_ge(p_hi, k + 1)
                nc.vector.tensor_tensor(pTl[:, k, :], Q[2 + k][:, :], pTh[:, k, :].bitcast(F32),
                                        ALU.subtract).then_inc(p_lo, 1)

            def split_ple(c):
                dve.wait_ge(w_hi, PLE0 + c + 1)
                nc.vector.tensor_tensor(wl2[:, c % 2, :, :], raw2[:, (c // 2) % 2, :, P * (c % 2):P * (c % 2) + P],
                                        wh2[:, c % 2, :, :].bitcast(F32), ALU.subtract).then_inc(w_lo, 1)
                dve.wait_ge(pw_hi, c + 1)
                nc.vector.tensor_tensor(pwl[:, c % 2, :, :], w_pup[:, :, P * c:P * c + P],
                                        pwh[:, c % 2, :, :].bitcast(F32), ALU.subtract).then_inc(pw_lo, 1)

            def add_ple(c):
                dve.wait_ge(ple_turned, c + 1)
                dst = h[:, :, P * c:P * c + P]
                nc.vector.tensor_tensor(dst, Q[2 * (c % 2)][:, :].rearrange("p (n c) -> p n c", c=P), dst,
                                        ALU.add).then_inc(ple_added, 1)

            split_ple(0)
            for c in range(N_PLE):
                if c + 1 < N_PLE:
                    split_ple(c + 1)
                dve.wait_ge(ple_gate, c + 1)
                nc.vector.tensor_tensor(pleT[:, c % 2, :], Q[2 * (c % 2) + 1][:, :], pleT[:, c % 2, :],
                                        ALU.mult).then_inc(ple_ready, 1)
                if c:
                    add_ple(c - 1)
            add_ple(N_PLE - 1)

            dve.wait_ge(gain_in[3], 16)
            with dve.Fori(0, NT // 2) as i:
                for t in range(2):
                    dve.wait_ge(rstd_ready, 3 * NT + 2 * i + t + 1)
                    row = h[:, ds(2 * i + t, 1), :].rearrange("p a d -> p (a d)")
                    nc.vector.scalar_tensor_tensor(out=row, in0=row, scalar=rstd[:, t:t + 1], in1=gain_fin[:, :],
                                                   op0=ALU.mult, op1=ALU.mult).then_inc(normed, 1)


_INS = ["x", "p", "g_mix", "w_in", "lb_logits", "hg_norm_g", "attn_sinks", "w_out", "g_ffn", "w_up", "conv_w",
        "conv_b", "w_down", "g_ple", "w_ple_gate", "w_ple_up", "g_final"]
_OUTS = [((1, 1024, 1024), "float32")]


def kernel(**inputs):
    import numpy as _np
    import concourse.bacc as _bacc
    from concourse import mybir as _mybir
    from concourse.bass_utils import run_bass_kernel_spmd as _run

    nc = _bacc.Bacc("TRN2", target_bir_lowering=False, num_devices=1)
    arrays, args = {}, []
    for name in _INS:
        a = _np.ascontiguousarray(inputs[name])
        arrays[f"in_{name}_dram"] = a
        args.append(nc.dram_tensor(f"in_{name}_dram", a.shape, _mybir.dt.from_np(a.dtype), kind="ExternalInput").ap())
    for i, (shape, dtype) in enumerate(_OUTS):
        dt = _mybir.dt.from_np(_np.dtype(dtype))
        args.append(nc.dram_tensor(f"out_{i}_dram", shape, dt, kind="ExternalOutput").ap())
    trunk_kernel(nc, *args)
    r = _run(nc, [arrays], core_ids=[0])
    got = tuple(r.results[0][f"out_{i}_dram"] for i in range(len(_OUTS)))
    return got[0]
```

```python
from contextlib import ExitStack

import concourse.bass as bass
from concourse import mybir

F32 = mybir.dt.float32
F32R = mybir.dt.float32r
BF16 = mybir.dt.bfloat16
U16 = mybir.dt.uint16
ALU = mybir.AluOpType
ACT = mybir.ActivationFunctionType
AX = mybir.AxisListType

P = 128
S = 1024
D = 1024
NT = S // P
KT = D // P
HH = 4
HW = HH * P
QH, KVH, DH = 8, 2, 64
GR = QH // KVH
F = 2816
FT = F // P
PD = 256
PK = PD // P
EPS = 1e-6
MASK_VALUE = -1e30
LB_FLOOR = 1e-30
LEVELS = 7
SW = 256
ds = bass.ds


def wait(eng, sem, count):
    if not isinstance(count, int) or count > 0:
        eng.wait_ge(sem, count)


def turns(eng, count, body):
    body(0)
    with eng.Fori(1, count) as i:
        body(i)


def trunk_kernel(nc, x, p, g_mix, w_in, lb_logits, hg_norm_g, attn_sinks, w_out, g_ffn, w_up,
                 conv_w, conv_b, w_down, g_ple, w_ple_gate, w_ple_up, g_final, out):
    x_t = x[0].rearrange("(n p) d -> n p d", p=P)
    out_t = out[0].rearrange("(n p) d -> n p d", p=P)
    p_t = p[0, 0].rearrange("(n p) e -> p n e", p=P)
    w_in_v = w_in[0].rearrange("(k p) n -> p k n", p=P)
    w_out_v = w_out[0].rearrange("(k p) n -> p k n", p=P)
    w_up_v = w_up[0].rearrange("(k p) n -> p k n", p=P)
    w_down_v = w_down[0].rearrange("(k p) n -> p k n", p=P)
    w_gate_v = w_ple_gate[0].rearrange("(k p) n -> p k n", p=P)
    w_pup_v = w_ple_up[0].rearrange("(k p) n -> p k n", p=P)
    h_dram = nc.dram_tensor("h_after_mixer", (NT, P, D), F32, kind="Internal").ap()

    ctx = ExitStack()
    with ctx:
        def sb(scope, name, shape, dt=F32):
            return scope.enter_context(nc.sbuf_tensor(name, shape, dt))

        def sem(name):
            return ctx.enter_context(nc.semaphore(name))

        ident = sb(ctx, "ident", [P, P])
        rows = sb(ctx, "rows", [P, P])
        cols = sb(ctx, "cols", [P, P])
        CONV_W0, CONV_B0, LB0, HGG0 = 0, 3 * FT, 4 * FT, 4 * FT + HH
        lbv = sb(ctx, "lbv", [P, 8, HH])
        neg_half = sb(ctx, "neg_half", [P, HH])
        ssq = sb(ctx, "ssq", [P, NT + HH])
        msq = sb(ctx, "msq", [P, NT + HH])
        rstd = sb(ctx, "rstd", [P, NT + HH])
        ident_b = sb(ctx, "ident_b", [P, P], BF16)
        level_mask = sb(ctx, "level_mask", [P, LEVELS * 256], BF16)
        band = sb(ctx, "band", [P, 4, P], BF16)

        with ExitStack() as scope:
            gain_mix = sb(scope, "gain_mix", [P, D])
            xt_mix = sb(scope, "xt_mix", [P, NT, D])
            junk_mix = sb(scope, "junk_mix", [P, D], BF16)
        with ExitStack() as mixer_scope:
            qT = sb(mixer_scope, "qT", [P, HH, S])
            fT = sb(mixer_scope, "fT", [P, HH, S])
            kT = sb(mixer_scope, "kT", [P, HH, S])
            aqT = sb(mixer_scope, "aqT", [P, GR, S])
            akT = sb(mixer_scope, "akT", [P, S])
            sgT = sb(mixer_scope, "sgT", [P, HH, S])
            with ExitStack() as scope:
                uh1 = sb(scope, "uh1", [P, KT, S], F32R)
                ul1 = sb(scope, "ul1", [P, KT, S], F32R)
                raw1 = sb(scope, "raw1", [P, 2, KT, SW])
                wh1 = sb(scope, "wh1", [P, 2, KT, P], F32R)
                wl1 = sb(scope, "wl1", [P, 2, KT, P], F32R)
                vT = sb(scope, "vT", [P, HH + 1, S])
            with ExitStack() as scope:
                wo = sb(scope, "wo", [P, KT, D])
                y_tok = sb(scope, "y_tok", [P, D])
                yT = sb(scope, "yT", [P, KT, P])
                x2 = sb(scope, "x2", [P, 2, D])
                v_tok = sb(scope, "v_tok", [P, NT, HW])
                av_tok = sb(scope, "av_tok", [P, NT + 1, P])
                sink = sb(scope, "sink", [P, QH])
                qst = sb(scope, "qst", [P, GR, P])
                kst = sb(scope, "kst", [P, 2, P])
                attT = sb(scope, "attT", [P, HW])
                state = sb(scope, "state", [P, HW])
                Ql = sb(scope, "Ql", [P, 2, HW])
                Kl = sb(scope, "Kl", [P, 2, HW])
                FQ = sb(scope, "FQ", [P, 1024])
                FK = sb(scope, "FK", [P, 1024])
                total = sb(scope, "total", [P, HH])
                smax = sb(scope, "smax", [P, 3, QH])
                sden = sb(scope, "sden", [P, 5, QH])
                probs = sb(scope, "probs", [P, GR, 2, P])
                probsT = sb(scope, "probsT", [P, GR, 2, P])
                k_tok = sb(scope, "k_tok", [P, HW])
                osq = sb(scope, "osq", [P, HW])
        with ExitStack() as scope:
            gain_ffn = sb(scope, "gain_ffn", [P, D])
            junk_ffn = sb(scope, "junk_ffn", [P, D], BF16)
        with ExitStack() as scope:
            un_ple = sb(scope, "un_ple", [P, 2, D])
            gain_ple = sb(scope, "gain_ple", [P, D])
            junk_ple = sb(scope, "junk_ple", [P, D], BF16)
        conv = sb(ctx, "conv", [P, 2, S])
        sgm = sb(ctx, "sgm", [P, S])
        pad = sb(ctx, "pad", [P, 512])
        raw2 = sb(ctx, "raw2", [P, 2, KT, SW])
        wh2 = sb(ctx, "wh2", [P, 2, KT, P], F32R)
        wl2 = sb(ctx, "wl2", [P, 2, KT, P], F32R)
        with ExitStack() as scope:
            xt_ffn = sb(scope, "xt_ffn", [P, 4, D])
        with ExitStack() as scope:
            G = sb(scope, "G", [P, FT, S])
        with ExitStack() as scope:
            uh3 = sb(scope, "uh3", [P, KT, S], F32R)
            ul3 = sb(scope, "ul3", [P, KT, S], F32R)
            pTh = sb(scope, "pTh", [P, PK, S], F32R)
            pTl = sb(scope, "pTl", [P, PK, S], F32R)
            w_pup = sb(scope, "w_pup", [P, PK, D])
            over_G = sb(scope, "over_G", [P, FT * S - 20 * S - PK * D + 256])
            with ExitStack() as deeper:
                uh2 = sb(deeper, "uh2", [P, KT, S], F32R)
                ul2 = sb(deeper, "ul2", [P, KT, S], F32R)
            h = sb(scope, "h", [P, NT, D])
            pwh = sb(scope, "pwh", [P, 2, PK, P], F32R)
            pwl = sb(scope, "pwl", [P, 2, PK, P], F32R)
            with ExitStack() as deeper:
                gh = sb(deeper, "gh", [P, 2, S], F32R)
                gl = sb(deeper, "gl", [P, 2, S], F32R)
                dh = sb(deeper, "dh", [P, 2, 512], F32R)
                dl = sb(deeper, "dl", [P, 2, 512], F32R)
            with ExitStack() as deeper:
                p_tok = sb(deeper, "p_tok", [P, NT, PD])
                pleT = sb(deeper, "pleT", [P, 2, S])
                gain_fin = sb(deeper, "gain_fin", [P, D])
        Q = [ctx.enter_context(nc.psum_tensor(f"Q{n}", [P, 1024], F32)) for n in range(4)]
        acc = [Q[t // 2][:, 512 * (t % 2):512 * (t % 2) + 512] for t in range(NT)]

        consts = sem("consts")
        rows_in = sem("rows_in")
        cols_ready = sem("cols_ready")
        colsT = sem("colsT")
        lb_step = sem("lb_step")
        gain_in = [sem(f"gain_in{n}") for n in range(4)]
        mask_step = sem("mask_step")
        sink_arg = sem("sink_arg")
        sink_exped = sem("sink_exped")
        x_in = [sem(f"x_in{n}") for n in range(NT)]
        squared = sem("squared")
        mean_ready = sem("mean_ready")
        rstd_ready = sem("rstd_ready")
        normed = sem("normed")
        turned = sem("turned")
        u_hi = sem("u_hi")
        u_lo = sem("u_lo")
        raw_in = [sem(f"raw_in{n}") for n in range(2)]
        w_hi = sem("w_hi")
        w_lo = sem("w_lo")
        product = sem("product")
        proj_act = sem("proj_act")
        freed = [sem(f"freed{n}") for n in range(2)]
        scaled = sem("scaled")
        v_turned = sem("v_turned")
        v_ready = [sem(f"v_ready{n}") for n in range(2)]
        start_ready = sem("start_ready")
        wo_in = sem("wo_in")
        sink_in = sem("sink_in")
        x2_in = [sem(f"x2_in{n}") for n in range(2)]
        qk_static = sem("qk_static")
        scores = sem("scores")
        max_step = sem("max_step")
        max_ready = sem("max_ready")
        exped = sem("exped")
        den_step = sem("den_step")
        den_ready = sem("den_ready")
        probs_turned = sem("probs_turned")
        probsT_ready = sem("probsT_ready")
        attended = sem("attended")
        y_att = sem("y_att")
        factors = sem("factors")
        q_level = sem("q_level")
        k_level = sem("k_level")
        level_product = sem("level_product")
        picked = sem("picked")
        h_half = sem("h_half")
        turn_of_pick = sem("turn_of_pick")
        turn_of_mean = sem("turn_of_mean")
        k_turned = sem("k_turned")
        k_tok_ready = sem("k_tok_ready")
        delta_ready = sem("delta_ready")
        o_ready = sem("o_ready")
        state_ready = sem("state_ready")
        o_squared = sem("o_squared")
        o_sum = sem("o_sum")
        o_mean = sem("o_mean")
        o_rstd = sem("o_rstd")
        y_hg = sem("y_hg")
        y_turned = sem("y_turned")
        yT_at = sem("yT_at")
        yT_hg = sem("yT_hg")
        mixed = sem("mixed")
        h_out = sem("h_out")
        conv_a = sem("conv_a")
        conv_b1 = sem("conv_b1")
        conv_sig = sem("conv_sig")
        silued = sem("silued")
        h_in = sem("h_in")
        d_in = [sem(f"d_in{n}") for n in range(2)]
        d_hi = sem("d_hi")
        d_lo = sem("d_lo")
        g_hi = sem("g_hi")
        g_lo = sem("g_lo")
        down_step = sem("down_step")
        down_half = sem("down_half")
        h_added = sem("h_added")
        p_in = sem("p_in")
        p_turned = sem("p_turned")
        p_hi = sem("p_hi")
        p_lo = sem("p_lo")
        pup_in = sem("pup_in")
        pw_hi = sem("pw_hi")
        pw_lo = sem("pw_lo")
        embedded = sem("embedded")
        ple_gate = sem("ple_gate")
        ple_ready = sem("ple_ready")
        ple_turned = sem("ple_turned")
        ple_added = sem("ple_added")
        stored = sem("stored")

        N_IN = 22
        N_UP = 2 * FT
        N_PLE = KT
        UP0, PLE0 = N_IN, N_IN + N_UP
        MASK_STEPS = 3 + 3 + 2 * LEVELS
        START_STEPS = 6
        block = ctx.enter_context(nc.Block())

        def halves(n):
            return slice(512 * n, 512 * n + 512)

        def in_strip(j):
            if 8 <= j < 10:
                a = 4 * HW + P * (j - 8)
                return [(a, P), (a + GR * DH, P)]
            return [(SW * j if j < 8 else 4 * HW + QH * DH, SW)]

        @block.sync
        def _(sp):
            sp.dma_start(rows[0:3 * FT, :], conv_w[0].rearrange("j (f p) -> (j f) p", p=P)).then_inc(rows_in, 16)
            sp.dma_start(rows[CONV_B0:CONV_B0 + FT, :], conv_b[0].rearrange("(f p) -> f p", p=P)).then_inc(rows_in, 16)
            sp.dma_start(rows[LB0:LB0 + HH, :], lb_logits[0].rearrange("(f p) -> f p", p=P)).then_inc(rows_in, 16)
            sp.dma_start(rows[HGG0:HGG0 + HH, :], hg_norm_g[0].rearrange("(f p) -> f p", p=P)).then_inc(rows_in, 16)
            sp.dma_start(gain_mix[:, :], g_mix[0:1, :].to_broadcast([P, D])).then_inc(gain_in[0], 16)
            def load_strip(j):
                at = 0
                for c, w in in_strip(j):
                    sp.dma_start(raw1[:, j % 2, :, at:at + w], w_in_v[:, :, c:c + w]).then_inc(raw_in[j % 2], 16)
                    at += w

            for n in range(NT):
                sp.dma_start(xt_mix[:, n, :], x_t[n]).then_inc(x_in[n], 16)
                if n in (NT // 2, NT - 1):
                    load_strip(n // (NT - 1))
            for j in range(2, N_IN // 2):
                sp.wait_ge(w_lo, 2 * (j - 1))
                load_strip(j)

            sp.wait_ge(product, N_IN)
            for k in range(KT):
                sp.dma_start(wo[:, k, :], w_out_v[:, k, :]).then_inc(wo_in, 16)
            for n in range(2):
                sp.wait_ge(v_ready[n], (HH + 2 - n) // 2)
            sp.dma_start(sink[:, :], attn_sinks[0:1, :].to_broadcast([P, QH])).then_inc(sink_in, 16)

            def residual_rows(i):
                for t in range(2):
                    wait(sp, h_out, 32 * i)
                    sp.dma_start(x2[:, t, :], x_t[ds(2 * i + t, 1), :, :].rearrange("a p d -> (a p) d")).then_inc(x2_in[t], 16)

            def store_h(n, t):
                sp.wait_ge(h_half, 2 * n + 2)
                sp.dma_start(h_dram[ds(n, 1), :, :].rearrange("a p d -> (a p) d"), x2[:, t, :]).then_inc(h_out, 16)

            residual_rows(0)
            store_h(0, 0)
            store_h(1, 1)
            with sp.Fori(1, NT // 2 - 1) as i:
                residual_rows(i)
                store_h(2 * i, 0)
                store_h(2 * i + 1, 1)
            residual_rows(NT // 2 - 1)

            sp.wait_ge(q_level, 8 * NT)
            sp.wait_ge(k_level, 8 * NT)
            sp.wait_ge(qk_static, 2 * NT)
            sp.dma_start(gain_ffn[:, :], g_ffn[0:1, :].to_broadcast([P, D])).then_inc(gain_in[1], 16)

            def load_h(n):
                sp.dma_start(xt_ffn[:, n % 4, :], h_dram[n]).then_inc(x_in[n], 16)

            def load_up(i):
                for half in range(2):
                    sp.wait_ge(w_lo, UP0 - 1 + 4 * i + half)
                    sp.dma_start(raw2[:, half, :, :], w_up_v[:, :, ds(F * half + SW * i, SW)]).then_inc(raw_in[half], 16)

            sp.wait_ge(h_out, 16 * (NT - 2))
            for n in range(4):
                load_h(n)
            store_h(NT - 2, 0)
            load_up(0)
            for n in range(4, NT - 1):
                sp.wait_ge(turned, NT + n - 3)
                if n == NT - 2:
                    sp.wait_ge(h_out, 16 * (NT - 1))
                load_h(n)
            store_h(NT - 1, 1)

            with sp.Fori(1, FT // 2) as i:
                load_up(i)

            sp.wait_ge(w_lo, PLE0)
            def load_down(k, t, hf):
                sp.dma_start(raw2[:, t, 0:2, :].rearrange("p a b -> p (a b)"),
                             w_down_v[:, ds(k, 1), 512 * hf:512 * hf + 512].rearrange("p a n -> p (a n)")).then_inc(d_in[t], 16)

            for hf in range(2):
                for t in range(2):
                    if hf:
                        sp.wait_ge(d_lo, FT + t - 1)
                    load_down(t, t, hf)
                with sp.Fori(1, FT // 2) as i:
                    for t in range(2):
                        sp.wait_ge(d_lo, FT * hf + 2 * i + t - 1)
                        load_down(2 * i + t, t, hf)
                if hf == 0:
                    sp.wait_ge(product, PLE0)
                    sp.wait_ge(h_out, 16 * NT)
                    sp.dma_start(h[:, :, :], h_dram.rearrange("n p d -> p n d")).then_inc(h_in, 16)

            sp.wait_ge(freed[1], (N_IN + N_UP) // 2)
            sp.dma_start(gain_ple[:, :], g_ple[0:1, :].to_broadcast([P, D])).then_inc(gain_in[2], 16)
            sp.wait_ge(d_lo, 2 * FT)
            for j in range(2):
                sp.dma_start(raw2[:, j, :, :], w_gate_v[:, :, SW * j:SW * j + SW]).then_inc(raw_in[j], 16)
            sp.wait_ge(down_half, 2 * NT)
            sp.dma_start(p_tok[:, :, :], p_t).then_inc(p_in, 16)
            sp.dma_start(w_pup[:, :, :], w_pup_v).then_inc(pup_in, 16)
            sp.dma_start(gain_fin[:, :], g_final.rearrange("(a d) -> a d", a=1).to_broadcast([P, D])).then_inc(gain_in[3], 16)
            for j in range(2, 4):
                sp.wait_ge(w_lo, PLE0 + 2 * (j - 1))
                sp.dma_start(raw2[:, j % 2, :, :], w_gate_v[:, :, SW * j:SW * j + SW]).then_inc(raw_in[j % 2], 16)
            for n in range(NT):
                sp.wait_ge(normed, 3 * NT + n + 1)
                sp.dma_start(out_t[n], h[:, n, :]).then_inc(stored, 16)
            sp.wait_ge(stored, 16 * NT)

        def chunk(n):
            return ds(P * n, P)

        def f_off(l):
            return sum(HW >> m for m in range(l))

        def factor(t, l):
            return t[:, f_off(l):f_off(l) + (HW >> l)].rearrange("p (b two) -> p b two", two=2)

        @block.gpsimd
        def _(pool):
            nc.gpsimd.memset(ident[:, :], 0.0).then_inc(consts, 1)
            nc.gpsimd.memset(neg_half[:, :], -0.5).then_inc(consts, 1)
            pool.wait_ge(consts, 2)
            nc.gpsimd.affine_select(out=ident[:, :], in_=ident[:, :], compare_op=ALU.not_equal, fill=1.0, base=0,
                                    pattern=[[-1, P]], channel_multiplier=1).then_inc(consts, 1)

            def norm_rows(first):
                for n in range(NT):
                    pool.wait_ge(squared, first + n + 1)
                    nc.gpsimd.tensor_scalar(msq[:, n:n + 1], ssq[:, n:n + 1], 1.0 / D, EPS,
                                            ALU.mult, ALU.add).then_inc(mean_ready, 1)
                    pool.wait_ge(mean_ready, first + n + 1)
                    nc.gpsimd.tensor_tensor(rstd[:, n:n + 1], msq[:, n:n + 1], neg_half[:, 0:1],
                                            ALU.pow).then_inc(rstd_ready, 1)

            pool.wait_ge(consts, 3)
            nc.gpsimd.tensor_copy(ident_b[:, :], ident[:, :]).then_inc(mask_step, 1)
            nc.gpsimd.memset(level_mask[:, :], 1.0).then_inc(mask_step, 1)
            nc.gpsimd.memset(band[:, 0:3, :], 0.0).then_inc(mask_step, 1)
            nc.gpsimd.memset(band[:, 3, :], MASK_VALUE)
            norm_rows(0)
            steps = 3
            pool.wait_ge(mask_step, steps)
            for block_of_band, (op, sign) in enumerate(((ALU.is_gt, 1), (ALU.is_ge, -1), (ALU.is_gt, 1))):
                nc.gpsimd.affine_select(out=band[:, block_of_band, :], in_=band[:, block_of_band, :], compare_op=op,
                                        fill=MASK_VALUE, base=0, pattern=[[sign, P]],
                                        channel_multiplier=-sign).then_inc(mask_step, 1)
                steps += 1
            for l in range(LEVELS):
                b = 1 << l
                m = level_mask[:, 256 * l:256 * l + 256].rearrange("p (a c r) -> p a c r", a=HH, r=b)
                nc.gpsimd.affine_select(out=m, in_=m, compare_op=ALU.is_ge, fill=0.0, base=0,
                                        pattern=[[0, HH], [-2 * b, 64 // b], [0, b]],
                                        channel_multiplier=1).then_inc(mask_step, 1)
                steps += 1
                pool.wait_ge(mask_step, steps)
                nc.gpsimd.affine_select(out=m, in_=m, compare_op=ALU.is_ge, fill=0.0, base=b - 1,
                                        pattern=[[0, HH], [2 * b, 64 // b], [0, b]],
                                        channel_multiplier=-1).then_inc(mask_step, 1)
                steps += 1
            assert steps == MASK_STEPS

            pool.wait_ge(product, N_IN)
            nc.gpsimd.memset(kst[:, 1, :], 0.0).then_inc(start_ready, 1)
            nc.gpsimd.memset(FQ[:, :], 1.0).then_inc(start_ready, 1)
            nc.gpsimd.memset(FK[:, :], 1.0).then_inc(start_ready, 1)
            nc.gpsimd.memset(attT[:, :], 0.0).then_inc(start_ready, 1)
            nc.gpsimd.memset(state[:, :], 0.0).then_inc(start_ready, 1)
            nc.gpsimd.memset(av_tok[:, 0, :], 0.0).then_inc(start_ready, 1)

            def k_step(n, l):
                if l == 1:
                    wait(pool, k_turned, n)
                else:
                    pool.wait_ge(level_product, 8 * n + l)
                pool.wait_ge(k_level, 8 * n + l)
                pool.wait_ge(factors, 15 * n + 2 * l)
                b = 1 << (l - 1)
                nc.gpsimd.tensor_tensor(Kl[:, l % 2, :].rearrange("p (c r) -> p c r", r=b),
                                        Kl[:, (l - 1) % 2, :].rearrange("p (c r) -> p c r", r=b),
                                        FK[:, f_off(l - 1):f_off(l)].unsqueeze(2).to_broadcast([P, HW // b, b]),
                                        ALU.mult).then_inc(k_level, 1)

            def o_norm(n):
                pool.wait_ge(o_sum, n + 1)
                pool.sem_inc(turn_of_mean, 1)
                nc.gpsimd.tensor_scalar(msq[:, NT:NT + HH], ssq[:, NT:NT + HH], 1.0 / P, EPS,
                                        ALU.mult, ALU.add).then_inc(o_mean, 1)
                pool.wait_ge(o_mean, n + 1)
                nc.gpsimd.tensor_tensor(rstd[:, NT:NT + HH], msq[:, NT:NT + HH], neg_half[:, :],
                                        ALU.pow).then_inc(o_rstd, 1)

            def pool_tile(n, first=False):
                k_step(n, 1)
                if not first:
                    o_norm(n - 1)
                for l in range(2, LEVELS + 1):
                    k_step(n, l)

            pool_tile(0, True)
            pool_tile(1)
            with pool.Fori(1, NT // 2) as i:
                for t in range(2):
                    pool_tile(2 * i + t)
            o_norm(NT - 1)
            norm_rows(NT)
            norm_rows(2 * NT)
            norm_rows(3 * NT)

        N0 = 7
        N1 = 6

        def split_count(m):
            s = m // 2
            return sum(16 * len(in_strip(j)) for j in range(s % 2, s + 1, 2))

        def in_split(t, m):
            s = m // 2
            if t is raw1:
                if 8 <= s < 10:
                    return raw1[:, s % 2, :, :].rearrange("p k (a c) -> p k a c", a=2)[:, :, :, DH * (m % 2):DH * (m % 2) + DH]
                return raw1[:, s % 2, :, P * (m % 2):P * (m % 2) + P]
            v = t[:, m % 2, :, :]
            return v.rearrange("p k (a c) -> p k a c", a=2) if 8 <= s < 10 else v

        @block.scalar
        def _(act):
            def square(first, n, src, junk):
                wait(act, squared, first + n)
                nc.scalar.activation(junk[:, :], src, ACT.Square, accum_out=ssq[:, n:n + 1]).then_inc(squared, 1)

            def high_half(first, n, uh):
                act.wait_ge(turned, first + n + 1)
                nc.scalar.activation(uh[:, :, P * n:P * n + P], Q[2 + n % 2][:, :].rearrange("p (k c) -> p k c", c=P),
                                     ACT.Copy).then_inc(u_hi, 1)

            act.wait_ge(lb_step, 2)
            nc.scalar.activation(lbv[:, 2, :], lbv[:, 1, :], ACT.Exp).then_inc(lb_step, 1)
            def split_in(m):
                act.wait_ge(raw_in[(m // 2) % 2], split_count(m))
                if m >= 2:
                    act.wait_ge(product, m - 1)
                nc.scalar.activation(in_split(wh1, m), in_split(raw1, m), ACT.Copy).then_inc(w_hi, 1)

            def square_x(n):
                act.wait_ge(x_in[n], 16)
                square(0, n, xt_mix[:, n, :], junk_mix)

            for n in range(2):
                square_x(n)
            for n in range(NT):
                high_half(0, n, uh1)
                if n + 2 < NT:
                    square_x(n + 2)
                if n in (2, 3):
                    split_in(n - 2)

            for m in range(N_IN):
                if 1 <= m < N_IN - 1:
                    split_in(m + 1)
                act.wait_ge(product, m + 1)
                src = Q[m % 2][:, :]
                if m < 4:
                    nc.scalar.activation(qT[:, m, :], src, ACT.Sigmoid).then_inc(proj_act, 1)
                elif m < 8:
                    nc.scalar.activation(fT[:, m - 4, :], src, ACT.Sigmoid)
                    nc.scalar.activation(kT[:, m - 4, :], src, ACT.Sigmoid, scale=-1.0).then_inc(freed[m % 2], 1)
                elif m < 12:
                    nc.scalar.activation(vT[:, m - 8, :], src, ACT.Copy).then_inc(freed[m % 2], 1)
                elif m < 16:
                    nc.scalar.activation(sgT[:, m - 12, :], src, ACT.Sigmoid).then_inc(freed[m % 2], 1)
                elif m < 20:
                    nc.scalar.activation(aqT[:, m - 16, :], src, ACT.Copy).then_inc(freed[m % 2], 1)
                else:
                    nc.scalar.activation(akT[:, :] if m == 20 else vT[:, HH, :], src,
                                         ACT.Copy).then_inc(freed[m % 2], 1)

            for c in range(1, HH + 1, 2):
                act.wait_ge(v_turned, c + 1)
                nc.scalar.activation(v_tok[:, :, P * c:P * c + P], Q[3][:, :].rearrange("p (n c) -> p n c", c=P),
                                     ACT.Copy).then_inc(v_ready[1], 1)

            def static_operands(n, t):
                wait(act, scores, 2 * n)
                nc.scalar.activation(qst[:, :, :], aqT[:, :, chunk(n)], ACT.Copy).then_inc(qk_static, 1)
                nc.scalar.activation(kst[:, t, :], akT[:, chunk(n)], ACT.Copy).then_inc(qk_static, 1)
                wait(act, k_level, 8 * n)
                wait(act, level_product, 8 * n)
                nc.scalar.activation(Kl[:, 0, :].rearrange("p (a t) -> p a t", t=P), kT[:, :, chunk(n)],
                                     ACT.Copy).then_inc(k_level, 1)

            def exps(n, g):
                act.wait_ge(max_ready, 2 * n + g + 1)
                wait(act, probs_turned, 2 * n + g)
                for j in range(GR):
                    nc.scalar.activation(probs[:, j, :, :].rearrange("p a c -> p (a c)"),
                                         Q[0][:, 2 * P * j:2 * P * j + 2 * P], ACT.Exp,
                                         bias=smax[:, 2, GR * g + j:GR * g + j + 1], scale=DH ** -0.5,
                                         accum_out=sden[:, 0, GR * g + j:GR * g + j + 1]).then_inc(exped, 1)
                act.wait_ge(sink_arg, 2 * n + g + 1)
                nc.scalar.activation(sden[:, 2, GR * g:GR * g + GR], sden[:, 1, GR * g:GR * g + GR],
                                     ACT.Exp).then_inc(sink_exped, 1)

            def probs_out(n, g):
                act.wait_ge(probs_turned, 2 * n + g + 1)
                wait(act, attended, 2 * n + g)
                nc.scalar.activation(probsT[:, :, :, :].rearrange("p a b c -> p (a b c)"), Q[1][:, :],
                                     ACT.Copy).then_inc(probsT_ready, 1)

            def chunk_end(n):
                act.wait_ge(k_turned, n + 1)
                wait(act, delta_ready, n)
                nc.scalar.activation(k_tok[:, :], Q[3][:, 512:1024], ACT.Copy).then_inc(k_tok_ready, 1)
                act.wait_ge(o_ready, n + 1)
                wait(act, o_sum, n)
                nc.scalar.activation(osq[:, :], Q[3][:, 0:512], ACT.Square).then_inc(o_squared, 1)

            def y_att_out(n):
                act.wait_ge(y_turned, n + 1)
                nc.scalar.activation(yT[:, HH:KT, :].rearrange("p k c -> p (k c)"), Q[1][:, 512:1024],
                                     ACT.Copy).then_inc(yT_at, 1)

            def act_tile(n, t, first=False):
                static_operands(n, t)
                if not first:
                    chunk_end(n - 1)
                exps(n, 0)
                if not first:
                    y_att_out(n - 1)
                probs_out(n, 0)
                exps(n, 1)
                probs_out(n, 1)

            act_tile(0, 0, True)
            act_tile(1, 1)
            with act.Fori(1, NT // 2) as i:
                for t in range(2):
                    act_tile(2 * i + t, t)
            def square_h(n):
                if n < NT - 1:
                    act.wait_ge(x_in[n], 32)
                else:
                    act.wait_ge(h_half, 2 * NT)
                square(NT, n, xt_ffn[:, n % 4, :] if n < NT - 1 else x2[:, 1, :], junk_ffn)

            def split_up(i, q):
                act.wait_ge(raw_in[q % 2], 16 * (N0 if q % 2 == 0 else N1) + 16 * i + 16)
                act.wait_ge(product, UP0 - 1 + 4 * i + q)
                nc.scalar.activation(wh2[:, q % 2, :, :], raw2[:, q % 2, :, P * (q // 2):P * (q // 2) + P],
                                     ACT.Copy).then_inc(w_hi, 1)

            chunk_end(NT - 1)
            for n in range(2):
                square_h(n)
            y_att_out(NT - 1)
            for n in range(NT):
                high_half(NT, n, uh2)
                if n + 2 < NT:
                    square_h(n + 2)
                if n in (2, 3):
                    split_up(0, n - 2)

            def up_turn(i, first=False, last=False):
                for q in range(4):
                    if q < 3:
                        if q or not first:
                            split_up(i, q + 1)
                    elif not last:
                        split_up(i + 1, 0)
                    f = 2 * i + q // 2
                    if q % 2 == 0:
                        act.wait_ge(product, UP0 + 4 * i + q + 1)
                        act.wait_ge(freed[1], N_IN // 2 - 1 + f)
                        nc.scalar.activation(conv[:, q // 2, :], Q[q][:, :], ACT.Identity,
                                             bias=cols[:, ds(CONV_B0 + f, 1)],
                                             scale=cols[:, ds(CONV_W0 + 2 * FT + f, 1)]).then_inc(conv_a, 1)
                    else:
                        act.wait_ge(freed[0], N_IN // 2 + f + 1)
                        nc.scalar.activation(sgm[:, :], conv[:, q // 2, :], ACT.Sigmoid).then_inc(conv_sig, 1)

            up_turn(0, first=True)
            with act.Fori(1, FT // 2 - 1) as i:
                up_turn(i)
            up_turn(FT // 2 - 1, last=True)

            act.wait_ge(product, PLE0)
            act.wait_ge(w_lo, PLE0)
            def split_down(k, t, s):
                if s is not None:
                    act.wait_ge(d_in[t], 16 * (FT // 2) * (s // FT) + 16)
                nc.scalar.activation(gh[:, t, :], G[:, ds(k, 1), :].rearrange("p a s -> p (a s)"),
                                     ACT.Copy).then_inc(g_hi, 1)
                nc.scalar.activation(dh[:, t, :], raw2[:, t, 0:2, :].rearrange("p a b -> p (a b)"),
                                     ACT.Copy).then_inc(d_hi, 1)

            act.wait_ge(freed[1], (N_IN + N_UP) // 2)
            for hf in range(2):
                for t in range(2):
                    if hf and t == 0:
                        act.wait_ge(down_step, FT - 1)
                    if hf and t == 1:
                        act.wait_ge(down_half, NT)
                    split_down(t, t, FT * hf + t)
                with act.Fori(1, FT // 2) as i:
                    for t in range(2):
                        act.wait_ge(down_step, (FT - 1) * hf + 2 * i + t - 1)
                        act.wait_ge(d_in[t], 16 * (FT // 2) * hf + 16 * i + 16)
                        split_down(2 * i + t, t, None)

            def square_sum(n):
                act.wait_ge(h_added, NT + n + 1)
                square(2 * NT, n, h[:, n, :], junk_ple)

            def split_gate(c):
                act.wait_ge(raw_in[(c // 2) % 2], 16 * ((N0, N1)[(c // 2) % 2] + FT // 2 + c // 4 + 1))
                act.wait_ge(product, PLE0 - 1 + c)
                nc.scalar.activation(wh2[:, c % 2, :, :], raw2[:, (c // 2) % 2, :, P * (c % 2):P * (c % 2) + P],
                                     ACT.Copy).then_inc(w_hi, 1)

            def split_embed(c):
                act.wait_ge(pup_in, 16)
                if c >= 2:
                    act.wait_ge(embedded, c - 1)
                nc.scalar.activation(pwh[:, c % 2, :, :], w_pup[:, :, P * c:P * c + P], ACT.Copy).then_inc(pw_hi, 1)

            for n in range(2):
                square_sum(n)
            for n in range(NT):
                high_half(2 * NT, n, uh3)
                if n + 2 < NT:
                    square_sum(n + 2)
                if n in (2, 3):
                    split_gate(n - 2)
            for c in range(2):
                split_embed(c)
            for k in range(PK):
                act.wait_ge(p_turned, k + 1)
                nc.scalar.activation(pTh[:, k, :], Q[2 + k][:, :], ACT.Copy).then_inc(p_hi, 1)
            for c in range(N_PLE):
                act.wait_ge(product, PLE0 + c + 1)
                if c >= 2:
                    act.wait_ge(ple_turned, c - 1)
                nc.scalar.activation(pleT[:, c % 2, :], Q[c % 2][:, :], ACT.Sigmoid).then_inc(ple_gate, 1)
                if c + 2 < N_PLE:
                    split_gate(c + 2)
                if 1 <= c < N_PLE - 1:
                    split_embed(c + 1)

            for n in range(NT):
                act.wait_ge(ple_added, N_PLE)
                square(3 * NT, n, h[:, n, :], junk_ple)

        def parts(wh, wl, uh, ul):
            return ((wh, uh), (wh, ul), (wl, uh))

        @block.tensor
        def _(pe):
            def turn_rows(first, n, src):
                pe.wait_ge(normed, first + n + 1)
                if n >= 2:
                    pe.wait_ge(u_lo, first + n - 1)
                for k in range(KT):
                    tr = nc.tensor.transpose(Q[2 + n % 2][:, P * k:P * k + P], src[:, P * k:P * k + P], ident[:, :])
                tr.then_inc(turned, 1)

            def project(wh, wl, uh, ul, slot, dst, kt):
                for k in range(kt):
                    for a, b in parts(wh, wl, uh, ul):
                        for half in range(2):
                            mm = nc.tensor.matmul(dst[:, 512 * half:512 * half + 512], a[:, slot, k, :],
                                                  b[:, k, 512 * half:512 * half + 512],
                                                  start=(k == 0 and a is wh and b is uh),
                                                  stop=(k == kt - 1 and a is wl))
                return mm

            def project_half(wh, wl, uh, ul, slot, half, rows):
                for k in rows:
                    for a, b in parts(wh, wl, uh, ul):
                        mm = nc.tensor.matmul(Q[slot][:, halves(half)], a[:, slot, k, :], b[:, k, halves(half)],
                                              start=(k == 0 and a is wh and b is uh), stop=(k == KT - 1 and a is wl))
                return mm

            def first_products(first, wh, wl, uh, ul, src, done, between=None):
                pe.wait_ge(u_lo, first + NT // 2)
                pe.wait_ge(w_lo, done + 1)
                project_half(wh, wl, uh, ul, 0, 0, range(KT // 2))
                turn_rows(first, NT - 2, src(NT - 2))
                project_half(wh, wl, uh, ul, 0, 0, range(KT // 2, KT))
                turn_rows(first, NT - 1, src(NT - 1))
                pe.wait_ge(w_lo, done + 2)
                project_half(wh, wl, uh, ul, 1, 0, range(KT))
                pe.wait_ge(u_lo, first + NT)
                if between:
                    between()
                for m in range(2):
                    project_half(wh, wl, uh, ul, m, 1, range(KT)).then_inc(product, 1)

            pe.wait_ge(consts, 3)
            pe.wait_ge(rows_in, 64)
            nc.tensor.transpose(Q[0][:, 0:96], rows[0:96, :], ident[0:96, 0:96]).then_inc(colsT, 1)
            for n in range(NT - 2):
                turn_rows(0, n, xt_mix[:, n, :])
            pe.wait_ge(cols_ready, 1)
            first_products(0, wh1, wl1, uh1, ul1, lambda n: xt_mix[:, n, :], 0)

            def in_turn(i):
                for t in range(2):
                    pe.wait_ge(w_lo, 2 * i + t + 1)
                    pe.wait_ge(freed[t], i)
                    project(wh1, wl1, uh1, ul1, t, Q[t], KT).then_inc(product, 1)

            with pe.Fori(1, N_IN // 2) as i:
                in_turn(i)

            pe.wait_ge(freed[1], N_IN // 2)
            for c in range(HH + 1):
                if c >= 2:
                    pe.wait_ge(v_ready[c % 2], c // 2)
                for n in range(NT):
                    tr = nc.tensor.transpose(Q[2 + c % 2][:, P * n:P * n + P], vT[:, c, P * n:P * n + P], ident[:, :])
                tr.then_inc(v_turned, 1)

            def score(n, t, g, first):
                if g == 0:
                    pe.wait_ge(qk_static, 2 * n + 2)
                    wait(pe, exped, 8 * n)
                else:
                    pe.wait_ge(exped, 8 * n + 4)
                mask = band[:, 0:2, :] if t else band[:, 1:4:2, :] if first else band[:, 1:3, :]
                for j in range(GR):
                    dst = Q[0][:, 2 * P * j:2 * P * j + 2 * P]
                    nc.tensor.matmul(dst, qst[DH * g:DH * g + DH, j, :],
                                     kst[DH * g:DH * g + DH, :, :].rearrange("p a c -> p (a c)"), start=True, stop=False)
                    mm = nc.tensor.matmul(dst.rearrange("p (a c) -> p a c", a=2), ident_b[:, :], mask,
                                          start=False, stop=True)
                mm.then_inc(scores, 1)

            def turn_probs(n, g):
                pe.wait_ge(exped, 8 * n + 4 * g + 4)
                if g == 0:
                    wait(pe, yT_hg, n)
                    wait(pe, yT_at, n)
                else:
                    pe.wait_ge(probsT_ready, 2 * n + 1)
                for j in range(GR):
                    for s in range(2):
                        c = P * (2 * j + s)
                        tr = nc.tensor.transpose(Q[1][:, c:c + P], probs[:, j, s, :], ident[:, :])
                tr.then_inc(probs_turned, 1)

            def attend(n, t, g):
                pe.wait_ge(probsT_ready, 2 * n + g + 1)
                if g == 0:
                    wait(pe, y_hg, n)
                for j in range(GR):
                    for s in range(2):
                        blk = n + 1 if s == t else n
                        c = DH * (GR * g + j)
                        mm = nc.tensor.matmul(Q[3][:, c:c + DH], probsT[:, j, s, :],
                                              av_tok[:, ds(blk, 1), DH * g:DH * g + DH].rearrange("p a c -> p (a c)"),
                                              start=(s == 0), stop=(s == 1))
                mm.then_inc(attended, 1)

            def level(n, g):
                if g >= 2:
                    pe.wait_ge(picked, 8 * n + g - 1)
                else:
                    wait(pe, picked, 8 * n + g - 1)
                l = max(g - 1, 0)
                pe.wait_ge(k_level, 8 * n + l + 1)
                if g:
                    pe.wait_ge(q_level, 8 * n + l + 1)
                b = 1 << l
                base = 512 * (g % 2)
                for a in range(HH):
                    keys = Kl[:, l % 2, P * a:P * a + P]
                    if g == 0:
                        mm = nc.tensor.matmul(Q[2][:, base + P * a:base + P * a + P], keys, qT[:, a, chunk(n)],
                                              start=True, stop=True)
                    else:
                        right = Ql[:, l % 2, P * a:P * a + P].rearrange("p (c two r) -> p c two r", two=2, r=b)[:, :, 1, :]
                        mm = nc.tensor.matmul(Q[2][:, base + 64 * a:base + 64 * a + 64].rearrange("p (c r) -> p c r", r=b),
                                              keys, right, start=True, stop=True)
                mm.then_inc(level_product, 1)

            def hgrn_out(n):
                pe.wait_ge(q_level, 8 * n + 8)
                pe.wait_ge(k_level, 8 * n + 8)
                wait(pe, state_ready, 4 * n)
                wait(pe, h_half, 2 * n)
                for a in range(HH):
                    tr = nc.tensor.transpose(Q[3][:, 512 + P * a:512 + P * a + P], Kl[:, 1, P * a:P * a + P], ident[:, :])
                tr.then_inc(k_turned, 1)
                pe.wait_ge(picked, 8 * n + 8)
                pe.wait_ge(y_att, n + 1)
                for a in range(HH):
                    c = slice(P * a, P * a + P)
                    nc.tensor.matmul(Q[3][:, c], Ql[:, 1, c], state[:, c], start=True, stop=False)
                    mm = nc.tensor.matmul(Q[3][:, c], attT[:, c],
                                          v_tok[:, ds(n, 1), c].rearrange("p a c -> p (a c)"), start=False, stop=True)
                mm.then_inc(o_ready, 1)
                pe.wait_ge(k_tok_ready, n + 1)
                for a in range(HH):
                    c = slice(P * a, P * a + P)
                    mm = nc.tensor.matmul(Q[3][:, 512 + P * a:512 + P * a + P], k_tok[:, c],
                                          v_tok[:, ds(n, 1), c].rearrange("p a c -> p (a c)"), start=True, stop=True)
                mm.then_inc(delta_ready, 1)

            def turn_y(n):
                pe.wait_ge(y_hg, n + 1)
                pe.wait_ge(probsT_ready, 2 * n + 2)
                for k in range(KT):
                    tr = nc.tensor.transpose(Q[1][:, P * k:P * k + P], y_tok[:, P * k:P * k + P], ident[:, :])
                tr.then_inc(y_turned, 1)

            def mix_out(n, half, part, dst=None):
                if part == 0 and half == 0:
                    pe.wait_ge(yT_hg, n + 1)
                    pe.wait_ge(yT_at, n + 1)
                elif part == 0 and dst is None:
                    pe.wait_ge(h_half, 2 * n + 1)
                if part == 0 and half == 0:
                    if dst is None:
                        pe.wait_ge(state_ready, 4 * n + 4)
                dst = Q[3][:, 512:1024] if dst is None else dst[:, halves(half)]
                for k in range(KT // 2 * part, KT // 2 * part + KT // 2):
                    mm = nc.tensor.matmul(dst, yT[:, k, :], wo[:, k, halves(half)], start=(k == 0),
                                          stop=(k == KT - 1))
                if part:
                    mm.then_inc(mixed, 1)

            def pe_tile(n, t, first=False):
                score(n, t, 0, first)
                level(n, 0)
                level(n, 1)
                if not first:
                    turn_y(n - 1)
                level(n, 2)
                turn_probs(n, 0)
                score(n, t, 1, first)
                if not first:
                    mix_out(n - 1, 0, 0)
                level(n, 3)
                attend(n, t, 0)
                turn_probs(n, 1)
                level(n, 4)
                if not first:
                    mix_out(n - 1, 0, 1)
                level(n, 5)
                attend(n, t, 1)
                if not first:
                    mix_out(n - 1, 1, 0)
                level(n, 6)
                if not first:
                    mix_out(n - 1, 1, 1)
                level(n, 7)
                hgrn_out(n)

            pe.wait_ge(mask_step, MASK_STEPS)
            pe.wait_ge(start_ready, START_STEPS)
            for n in range(2):
                pe.wait_ge(v_ready[n], (HH + 2 - n) // 2)
            pe.wait_ge(scaled, 12)
            pe_tile(0, 0, True)
            pe.wait_ge(wo_in, 16 * KT)
            pe_tile(1, 1)
            with pe.Fori(1, NT // 2) as i:
                for t in range(2):
                    pe_tile(2 * i + t, t)
            def turn_h(n):
                turn_rows(NT, n, xt_ffn[:, n % 4, :])

            turn_h(0)
            turn_y(NT - 1)
            turn_h(1)
            for quarter in range(4):
                mix_out(NT - 1, quarter // 2, quarter % 2, Q[0])
                turn_h(quarter + 2)

            pe.wait_ge(h_half, 2 * NT)
            first_products(NT, wh2, wl2, uh2, ul2, lambda n: xt_ffn[:, n % 4, :], UP0)

            def up_product(i, q):
                pe.wait_ge(w_lo, UP0 + 4 * i + q + 1)
                pe.wait_ge(freed[q % 2], N_IN // 2 - 1 + 2 * i + q // 2)
                project(wh2, wl2, uh2, ul2, q % 2, Q[q], KT).then_inc(product, 1)

            for q in range(2, 4):
                up_product(0, q)
            with pe.Fori(1, FT // 2) as i:
                for q in range(4):
                    up_product(i, q)

            def down(k, t, hf, first, last):
                s = hf * FT + k
                pe.wait_ge(d_lo, s + 1)
                pe.wait_ge(g_lo, s + 1)
                for n in range(NT):
                    if first and hf:
                        pe.wait_ge(h_added, n + 1)
                    for j, (a, b) in enumerate(parts(gh, gl, dh, dl)):
                        mm = nc.tensor.matmul(acc[n], a[:, t, P * n:P * n + P], b[:, t, :],
                                              start=(first and j == 0), stop=(last and j == 2))
                    if last:
                        mm.then_inc(down_half, 1)
                return mm

            pe.wait_ge(freed[0], (N_IN + N_UP) // 2)
            pe.wait_ge(freed[1], (N_IN + N_UP) // 2)
            for hf in range(2):
                down(0, 0, hf, True, False).then_inc(down_step, 1)
                down(1, 1, hf, False, False).then_inc(down_step, 1)
                with pe.Fori(1, FT // 2 - 1) as i:
                    for t in range(2):
                        down(2 * i + t, t, hf, False, False).then_inc(down_step, 1)
                down(FT - 2, 0, hf, False, False).then_inc(down_step, 1)
                down(FT - 1, 1, hf, False, True)

            pe.wait_ge(h_added, 2 * NT)
            for n in range(NT - 2):
                turn_rows(2 * NT, n, un_ple[:, n % 2, :])

            def turn_p():
                pe.wait_ge(p_in, 16)
                for k in range(PK):
                    for n in range(NT):
                        tr = nc.tensor.transpose(Q[2 + k][:, P * n:P * n + P], p_tok[:, n, P * k:P * k + P],
                                                 ident[:, :])
                    tr.then_inc(p_turned, 1)

            first_products(2 * NT, wh2, wl2, uh3, ul3, lambda n: un_ple[:, n % 2, :], PLE0, turn_p)
            pe.wait_ge(p_lo, PK)

            def embed(c):
                pe.wait_ge(pw_lo, c + 1)
                wait(pe, ple_ready, c)
                project(pwh, pwl, pTh, pTl, c % 2, Q[2], PK).then_inc(embedded, 1)

            def turn_ple(c):
                pe.wait_ge(ple_ready, c + 1)
                wait(pe, ple_added, c)
                for n in range(NT):
                    tr = nc.tensor.transpose(Q[3][:, P * n:P * n + P], pleT[:, c % 2, P * n:P * n + P], ident[:, :])
                tr.then_inc(ple_turned, 1)

            embed(0)
            for c in range(2, N_PLE):
                pe.wait_ge(w_lo, PLE0 + c + 1)
                pe.wait_ge(ple_gate, c - 1)
                project(wh2, wl2, uh3, ul3, c % 2, Q[c % 2], KT).then_inc(product, 1)
                turn_ple(c - 2)
                embed(c - 1)
            turn_ple(N_PLE - 2)
            embed(N_PLE - 1)
            turn_ple(N_PLE - 1)

        @block.vector
        def _(dve):
            def normalise(first, n, src, dst, gain):
                dve.wait_ge(rstd_ready, first + n + 1)
                nc.vector.scalar_tensor_tensor(out=dst, in0=src, scalar=rstd[:, n:n + 1], in1=gain[:, :],
                                               op0=ALU.mult, op1=ALU.mult).then_inc(normed, 1)

            def low_half(first, n, ul, uh):
                dve.wait_ge(u_hi, first + n + 1)
                at = slice(P * n, P * n + P)
                nc.vector.tensor_tensor(ul[:, :, at], Q[2 + n % 2][:, :].rearrange("p (k c) -> p k c", c=P),
                                        uh[:, :, at].bitcast(F32), ALU.subtract).then_inc(u_lo, 1)

            dve.wait_ge(colsT, 1)
            nc.vector.tensor_copy(cols[:, 0:96], Q[0][:, 0:96]).then_inc(cols_ready, 1)
            dve.wait_ge(cols_ready, 1)
            nc.vector.tensor_copy(lbv[:, 0, :], cols[:, LB0:LB0 + HH]).then_inc(lb_step, 1)
            dve.wait_ge(lb_step, 1)
            nc.vector.tensor_tensor(lbv[:, 1, :], cols[:, LB0:LB0 + HH], lbv[:, 0, :], ALU.subtract).then_inc(lb_step, 1)
            dve.wait_ge(lb_step, 3)
            nc.vector.reciprocal(lbv[:, 3, :], lbv[:, 2, :]).then_inc(lb_step, 1)
            dve.wait_ge(lb_step, 4)
            nc.vector.tensor_tensor(lbv[:, 4, :], lbv[:, 2, :], lbv[:, 3, :], ALU.mult).then_inc(lb_step, 1)
            dve.wait_ge(lb_step, 5)
            nc.vector.tensor_tensor(lbv[:, 5, :], lbv[:, 4, :], lbv[:, 4, :], ALU.subtract).then_inc(lb_step, 1)
            dve.wait_ge(lb_step, 6)
            nc.vector.tensor_scalar(lbv[:, 6, :], lbv[:, 5, :], LB_FLOOR, None, ALU.max).then_inc(lb_step, 1)
            nc.vector.tensor_scalar(lbv[:, 7, :], lbv[:, 5, :], -1.0, 1.0, ALU.mult, ALU.add).then_inc(lb_step, 1)

            dve.wait_ge(gain_in[0], 16)
            def split_in(m):
                dve.wait_ge(w_hi, m + 1)
                nc.vector.tensor_tensor(in_split(wl1, m), in_split(raw1, m), in_split(wh1, m).bitcast(F32),
                                        ALU.subtract).then_inc(w_lo, 1)

            for n in range(2):
                normalise(0, n, xt_mix[:, n, :], xt_mix[:, n, :], gain_mix)
            for n in range(NT):
                low_half(0, n, ul1, uh1)
                if n + 2 < NT:
                    normalise(0, n + 2, xt_mix[:, n + 2, :], xt_mix[:, n + 2, :], gain_mix)
                if n in (2, 3):
                    split_in(n - 2)

            dve.wait_ge(lb_step, 8)
            for m in range(N_IN):
                if 1 <= m < N_IN - 1:
                    split_in(m + 1)
                if m < 4:
                    dve.wait_ge(proj_act, m + 1)
                    nc.vector.tensor_tensor(qT[:, m, :], Q[m % 2][:, :], qT[:, m, :], ALU.mult).then_inc(freed[m % 2], 1)
                elif m < 8:
                    a = m - 4
                    dve.wait_ge(freed[m % 2], m // 2 + 1)
                    nc.vector.tensor_scalar(fT[:, a, :], fT[:, a, :], lbv[:, 7, a:a + 1], lbv[:, 6, a:a + 1],
                                            ALU.mult, ALU.add).then_inc(scaled, 1)
                    nc.vector.tensor_scalar(kT[:, a, :], kT[:, a, :], lbv[:, 7, a:a + 1], None,
                                            ALU.mult).then_inc(scaled, 1)
                elif 12 <= m < 16:
                    a = m - 12
                    dve.wait_ge(freed[m % 2], m // 2 + 1)
                    nc.vector.tensor_scalar(sgT[:, a, :], sgT[:, a, :], cols[:, HGG0 + a:HGG0 + a + 1], None,
                                            ALU.mult).then_inc(scaled, 1)

            dve.wait_ge(product, N_IN)
            for c in range(0, HH + 1, 2):
                dve.wait_ge(v_turned, c + 1)
                dst = v_tok[:, :, P * c:P * c + P] if c < HH else av_tok[:, 1:NT + 1, :]
                nc.vector.tensor_copy(dst, Q[2][:, :].rearrange("p (n c) -> p n c", c=P)).then_inc(v_ready[0], 1)

            def row_max(n, g):
                dve.wait_ge(scores, 2 * n + g + 1)
                c = slice(GR * g, GR * g + GR)
                z = 4 * n + 2 * g
                nc.vector.tensor_reduce(smax[:, 0, c], Q[0][:, :].rearrange("p (j k) -> p j k", j=GR), AX.X,
                                        ALU.max).then_inc(max_step, 1)
                dve.wait_ge(max_step, z + 1)
                nc.vector.scalar_tensor_tensor(out=smax[:, 1, c], in0=smax[:, 0, c], scalar=DH ** -0.5, in1=sink[:, c],
                                               op0=ALU.mult, op1=ALU.max).then_inc(max_step, 1)
                dve.wait_ge(max_step, z + 2)
                nc.vector.tensor_scalar(smax[:, 2, c], smax[:, 1, c], -1.0, None, ALU.mult).then_inc(max_ready, 1)
                nc.vector.tensor_tensor(sden[:, 1, c], sink[:, c], smax[:, 1, c], ALU.subtract).then_inc(sink_arg, 1)

            def denominators(n):
                dve.wait_ge(exped, 8 * n + 8)
                dve.wait_ge(sink_exped, 2 * n + 2)
                nc.vector.tensor_tensor(sden[:, 3, :], sden[:, 0, :], sden[:, 2, :], ALU.add).then_inc(den_step, 1)
                dve.wait_ge(den_step, n + 1)
                nc.vector.reciprocal(sden[:, 4, :], sden[:, 3, :]).then_inc(den_ready, 1)

            def att_rows(n):
                dve.wait_ge(attended, 2 * n + 2)
                dve.wait_ge(den_ready, n + 1)
                wait(dve, y_turned, n)
                nc.vector.tensor_tensor(y_tok[:, HW:D].rearrange("p (h d) -> p h d", d=DH),
                                        Q[3][:, 0:512].rearrange("p (h d) -> p h d", d=DH),
                                        sden[:, 4, :].unsqueeze(2).to_broadcast([P, QH, DH]), ALU.mult).then_inc(y_att, 1)

            def factor_step(n, l):
                if l == 0:
                    wait(dve, k_level, 8 * n)
                    wait(dve, q_level, 8 * n)
                    f = fT[:, :, chunk(n)].rearrange("p a (c two) -> p a c two", two=2)
                    nc.vector.tensor_copy(factor(FQ, 0)[:, :, 1].rearrange("p (a c) -> p a c", a=HH),
                                          f[:, :, :, 0]).then_inc(factors, 1)
                    nc.vector.tensor_copy(factor(FK, 0)[:, :, 0].rearrange("p (a c) -> p a c", a=HH),
                                          f[:, :, :, 1]).then_inc(factors, 1)
                    return
                dve.wait_ge(factors, 15 * n + 2 * l)
                left, right = factor(FQ, l - 1)[:, :, 1], factor(FK, l - 1)[:, :, 0]
                if l == LEVELS:
                    nc.vector.tensor_tensor(total[:, :], left, right, ALU.mult).then_inc(factors, 1)
                    return
                left = left.rearrange("p (c two) -> p c two", two=2)
                right = right.rearrange("p (c two) -> p c two", two=2)
                nc.vector.tensor_tensor(factor(FQ, l)[:, :, 1], left[:, :, 0], right[:, :, 0],
                                        ALU.mult).then_inc(factors, 1)
                nc.vector.tensor_tensor(factor(FK, l)[:, :, 0], left[:, :, 1], right[:, :, 1],
                                        ALU.mult).then_inc(factors, 1)

            def q_step(n, l):
                if l == 0:
                    wait(dve, level_product, 8 * n)
                    nc.vector.tensor_tensor(Ql[:, 0, :].rearrange("p (a t) -> p a t", t=P), qT[:, :, chunk(n)],
                                            fT[:, :, chunk(n)], ALU.mult).then_inc(q_level, 1)
                    return
                if l == 1:
                    wait(dve, o_ready, n)
                else:
                    dve.wait_ge(level_product, 8 * n + l)
                dve.wait_ge(q_level, 8 * n + l)
                dve.wait_ge(factors, 15 * n + 2 * l)
                b = 1 << (l - 1)
                nc.vector.tensor_tensor(Ql[:, l % 2, :].rearrange("p (c r) -> p c r", r=b),
                                        Ql[:, (l - 1) % 2, :].rearrange("p (c r) -> p c r", r=b),
                                        FQ[:, f_off(l - 1):f_off(l)].unsqueeze(2).to_broadcast([P, HW // b, b]),
                                        ALU.mult).then_inc(q_level, 1)

            def pick(n, g):
                dve.wait_ge(level_product, 8 * n + g + 1)
                base = 512 * (g % 2)
                if g == 0:
                    wait(dve, o_ready, n)
                else:
                    dve.wait_ge(picked, 8 * n + g)
                dve.sem_inc(turn_of_pick, 1)
                if g == 0:
                    nc.vector.copy_predicated(attT[:, :].rearrange("p (a t) -> p a t", t=P),
                                              ident_b[:, :].bitcast(U16).unsqueeze(1).to_broadcast([P, HH, P]),
                                              Q[2][:, base:base + HW].rearrange("p (a t) -> p a t", t=P)).then_inc(picked, 1)
                    return
                b = 1 << (g - 1)
                m = level_mask[:, 256 * (g - 1):256 * g].bitcast(U16)
                nc.vector.copy_predicated(attT[:, :].rearrange("p (c two r) -> p c two r", two=2, r=b)[:, :, 1, :],
                                          m.rearrange("p (c r) -> p c r", r=b),
                                          Q[2][:, base:base + 256].rearrange("p (c r) -> p c r", r=b)).then_inc(picked, 1)

            def output_half(n, t, pair, half, src=Q[3][:, 512:1024]):
                dve.wait_ge(mixed, 2 * n + half + 1)
                dve.wait_ge(x2_in[t], 16 * pair + 16)
                nc.vector.tensor_tensor(x2[:, t, halves(half)], src, x2[:, t, halves(half)],
                                        ALU.add).then_inc(h_half, 1)

            def o_sums(n):
                dve.wait_ge(o_squared, n + 1)
                nc.vector.tensor_reduce(ssq[:, NT:NT + HH], osq[:, :].rearrange("p (a c) -> p a c", a=HH), AX.X,
                                        ALU.add).then_inc(o_sum, 1)

            def next_state(n):
                dve.wait_ge(delta_ready, n + 1)
                dve.wait_ge(factors, 15 * n + 15)
                for a in range(HH):
                    c = slice(P * a, P * a + P)
                    nc.vector.scalar_tensor_tensor(out=state[:, c], in0=state[:, c], scalar=total[:, a:a + 1],
                                                   in1=Q[3][:, 512 + P * a:512 + P * a + P], op0=ALU.mult,
                                                   op1=ALU.add).then_inc(state_ready, 1)

            def hg_rows(n):
                dve.wait_ge(o_rstd, n + 1)
                nc.vector.tensor_tensor(y_tok[:, 0:HW].rearrange("p (a c) -> p a c", a=HH),
                                        Q[3][:, 0:512].rearrange("p (a c) -> p a c", a=HH),
                                        rstd[:, NT:NT + HH].unsqueeze(2).to_broadcast([P, HH, P]),
                                        ALU.mult).then_inc(y_hg, 1)

            def gated_rows(n):
                dve.wait_ge(y_turned, n + 1)
                nc.vector.tensor_tensor(yT[:, 0:HH, :], Q[1][:, 0:512].rearrange("p (a c) -> p a c", a=HH),
                                        sgT[:, :, chunk(n)], ALU.mult).then_inc(yT_hg, 1)

            def dve_tile(n, t, pair, first=False):
                last_pair = pair - 1 + t
                factor_step(n, 0)
                q_step(n, 0)
                factor_step(n, 1)
                if not first:
                    o_sums(n - 1)
                q_step(n, 1)
                if not first:
                    next_state(n - 1)
                    hg_rows(n - 1)
                row_max(n, 0)
                pick(n, 0)
                pick(n, 1)
                factor_step(n, 2)
                q_step(n, 2)
                if not first:
                    gated_rows(n - 1)
                pick(n, 2)
                factor_step(n, 3)
                q_step(n, 3)
                row_max(n, 1)
                pick(n, 3)
                factor_step(n, 4)
                q_step(n, 4)
                pick(n, 4)
                factor_step(n, 5)
                q_step(n, 5)
                denominators(n)
                if not first:
                    output_half(n - 1, 1 - t, last_pair, 0)
                pick(n, 5)
                factor_step(n, 6)
                q_step(n, 6)
                att_rows(n)
                pick(n, 6)
                factor_step(n, 7)
                q_step(n, 7)
                if not first:
                    output_half(n - 1, 1 - t, last_pair, 1)
                pick(n, 7)

            dve.wait_ge(sink_in, 16)
            dve.wait_ge(mask_step, MASK_STEPS)
            dve.wait_ge(start_ready, START_STEPS)
            dve.wait_ge(scaled, 12)
            dve_tile(0, 0, 0, True)
            dve_tile(1, 1, 0)
            with dve.Fori(1, NT // 2) as i:
                for t in range(2):
                    dve_tile(2 * i + t, t, i)

            def normalise_h(n):
                if n == NT - 1:
                    dve.wait_ge(turned, NT + n - 3)
                row = xt_ffn[:, n % 4, :]
                normalise(NT, n, row if n < NT - 1 else x2[:, 1, :], row, gain_ffn)

            def split_up(i, q):
                dve.wait_ge(w_hi, UP0 + 4 * i + q + 1)
                nc.vector.tensor_tensor(wl2[:, q % 2, :, :], raw2[:, q % 2, :, P * (q // 2):P * (q // 2) + P],
                                        wh2[:, q % 2, :, :].bitcast(F32), ALU.subtract).then_inc(w_lo, 1)

            o_sums(NT - 1)
            dve.wait_ge(gain_in[1], 16)
            normalise_h(0)
            hg_rows(NT - 1)
            normalise_h(1)
            gated_rows(NT - 1)
            for n in range(NT):
                if n == NT - 3:
                    for half in range(2):
                        output_half(NT - 1, 1, NT // 2 - 1, half, Q[0][:, halves(half)])
                low_half(NT, n, ul2, uh2)
                if n + 2 < NT:
                    normalise_h(n + 2)
                if n in (2, 3):
                    split_up(0, n - 2)

            def up_turn(i, first=False, last=False):
                for q in range(4):
                    if q < 3:
                        if q or not first:
                            split_up(i, q + 1)
                    elif not last:
                        split_up(i + 1, 0)
                    f = 2 * i + q // 2
                    cv = conv[:, q // 2, :]
                    if q % 2 == 0:
                        dve.wait_ge(conv_a, f + 1)
                        nc.vector.scalar_tensor_tensor(out=cv[:, 1:S], in0=Q[q][:, 0:S - 1],
                                                       scalar=cols[:, ds(CONV_W0 + FT + f, 1)], in1=cv[:, 1:S],
                                                       op0=ALU.mult, op1=ALU.add).then_inc(conv_b1, 1)
                        dve.wait_ge(conv_b1, f + 1)
                        nc.vector.scalar_tensor_tensor(out=cv[:, 2:S], in0=Q[q][:, 0:S - 2],
                                                       scalar=cols[:, ds(CONV_W0 + f, 1)], in1=cv[:, 2:S],
                                                       op0=ALU.mult, op1=ALU.add).then_inc(freed[0], 1)
                    else:
                        dve.wait_ge(conv_sig, f + 1)
                        nc.vector.tensor_tensor(cv, cv, sgm[:, :], ALU.mult).then_inc(silued, 1)
                        dve.wait_ge(silued, f + 1)
                        dve.wait_ge(product, UP0 + 4 * i + q + 1)
                        nc.vector.tensor_tensor(G[:, ds(f, 1), :].rearrange("p a s -> p (a s)"), Q[q][:, :], cv,
                                                ALU.mult).then_inc(freed[1], 1)
            up_turn(0, first=True)
            with dve.Fori(1, FT // 2 - 1) as i:
                up_turn(i)
            up_turn(FT // 2 - 1, last=True)

            def split_down(k, t, s):
                dve.wait_ge(g_hi, s + 1)
                nc.vector.tensor_tensor(gl[:, t, :], G[:, ds(k, 1), :].rearrange("p a s -> p (a s)"),
                                        gh[:, t, :].bitcast(F32), ALU.subtract).then_inc(g_lo, 1)
                dve.wait_ge(d_hi, s + 1)
                nc.vector.tensor_tensor(dl[:, t, :], raw2[:, t, 0:2, :].rearrange("p a b -> p (a b)"),
                                        dh[:, t, :].bitcast(F32), ALU.subtract).then_inc(d_lo, 1)

            def add_down(hf):
                for n in range(NT):
                    dve.wait_ge(down_half, NT * hf + n + 1)
                    c = halves(hf)
                    nc.vector.tensor_tensor(h[:, n, c], acc[n], h[:, n, c], ALU.add).then_inc(h_added, 1)

            with dve.Fori(0, FT // 2) as i:
                for t in range(2):
                    split_down(2 * i + t, t, 2 * i + t)
            split_down(0, 0, FT)
            dve.wait_ge(h_in, 16)
            add_down(0)
            split_down(1, 1, FT + 1)
            with dve.Fori(1, FT // 2) as i:
                for t in range(2):
                    split_down(2 * i + t, t, FT + 2 * i + t)
            add_down(1)

            dve.wait_ge(gain_in[2], 16)
            def split_gate(c):
                dve.wait_ge(w_hi, PLE0 + c + 1)
                nc.vector.tensor_tensor(wl2[:, c % 2, :, :], raw2[:, (c // 2) % 2, :, P * (c % 2):P * (c % 2) + P],
                                        wh2[:, c % 2, :, :].bitcast(F32), ALU.subtract).then_inc(w_lo, 1)

            def split_embed(c):
                dve.wait_ge(pw_hi, c + 1)
                nc.vector.tensor_tensor(pwl[:, c % 2, :, :], w_pup[:, :, P * c:P * c + P],
                                        pwh[:, c % 2, :, :].bitcast(F32), ALU.subtract).then_inc(pw_lo, 1)

            def normalise_sum(n):
                wait(dve, turned, 2 * NT + n - 1 if n >= 2 else 0)
                normalise(2 * NT, n, h[:, n, :], un_ple[:, n % 2, :], gain_ple)

            for n in range(2):
                normalise_sum(n)
            for n in range(NT):
                low_half(2 * NT, n, ul3, uh3)
                if n + 2 < NT:
                    normalise_sum(n + 2)
                if n in (2, 3):
                    split_gate(n - 2)
            for c in range(2):
                split_embed(c)
            for k in range(PK):
                dve.wait_ge(p_hi, k + 1)
                nc.vector.tensor_tensor(pTl[:, k, :], Q[2 + k][:, :], pTh[:, k, :].bitcast(F32),
                                        ALU.subtract).then_inc(p_lo, 1)
            split_gate(2)
            for c in range(N_PLE):
                dve.wait_ge(ple_gate, c + 1)
                dve.wait_ge(embedded, c + 1)
                nc.vector.tensor_tensor(pleT[:, c % 2, :], Q[2][:, :], pleT[:, c % 2, :], ALU.mult).then_inc(ple_ready, 1)
                if c + 3 < N_PLE:
                    split_gate(c + 3)
                if c + 2 < N_PLE:
                    split_embed(c + 2)
                dve.wait_ge(ple_turned, c + 1)
                dst = h[:, :, P * c:P * c + P]
                nc.vector.tensor_tensor(dst, Q[3][:, :].rearrange("p (n c) -> p n c", c=P), dst,
                                        ALU.add).then_inc(ple_added, 1)

            dve.wait_ge(gain_in[3], 16)
            for n in range(NT):
                normalise(3 * NT, n, h[:, n, :], h[:, n, :], gain_fin)


_INS = ["x", "p", "g_mix", "w_in", "lb_logits", "hg_norm_g", "attn_sinks", "w_out", "g_ffn", "w_up", "conv_w",
        "conv_b", "w_down", "g_ple", "w_ple_gate", "w_ple_up", "g_final"]
_OUTS = [((1, 1024, 1024), "float32")]


def kernel(**inputs):
    import numpy as _np
    import concourse.bacc as _bacc
    from concourse import mybir as _mybir
    from concourse.bass_utils import run_bass_kernel_spmd as _run

    nc = _bacc.Bacc("TRN2", target_bir_lowering=False, num_devices=1)
    arrays, args = {}, []
    for name in _INS:
        a = _np.ascontiguousarray(inputs[name])
        arrays[f"in_{name}_dram"] = a
        args.append(nc.dram_tensor(f"in_{name}_dram", a.shape, _mybir.dt.from_np(a.dtype), kind="ExternalInput").ap())
    for i, (shape, dtype) in enumerate(_OUTS):
        dt = _mybir.dt.from_np(_np.dtype(dtype))
        args.append(nc.dram_tensor(f"out_{i}_dram", shape, dt, kind="ExternalOutput").ap())
    trunk_kernel(nc, *args)
    r = _run(nc, [arrays], core_ids=[0])
    got = tuple(r.results[0][f"out_{i}_dram"] for i in range(len(_OUTS)))
    return got[0]
```

```python
from contextlib import ExitStack

import concourse.bass as bass
from concourse import mybir

F32 = mybir.dt.float32
F32R = mybir.dt.float32r
BF16 = mybir.dt.bfloat16
U16 = mybir.dt.uint16
ALU = mybir.AluOpType
ACT = mybir.ActivationFunctionType
AX = mybir.AxisListType

P = 128
S = 1024
D = 1024
NT = S // P
KT = D // P
HH = 4
HW = HH * P
QH, KVH, DH = 8, 2, 64
GR = QH // KVH
F = 2816
FT = F // P
PD = 256
PK = PD // P
EPS = 1e-6
MASK_VALUE = -1e30
LB_FLOOR = 1e-30
LEVELS = 7
SW = 256
ds = bass.ds


def wait(eng, sem, count):
    if not isinstance(count, int) or count > 0:
        eng.wait_ge(sem, count)


def trunk_kernel(nc, x, p, g_mix, w_in, lb_logits, hg_norm_g, attn_sinks, w_out, g_ffn, w_up,
                 conv_w, conv_b, w_down, g_ple, w_ple_gate, w_ple_up, g_final, out):
    x_t = x[0].rearrange("(n p) d -> n p d", p=P)
    out_t = out[0].rearrange("(n p) d -> n p d", p=P)
    p_t = p[0, 0].rearrange("(n p) e -> p n e", p=P)
    w_in_v = w_in[0].rearrange("(k p) n -> p k n", p=P)
    w_out_v = w_out[0].rearrange("(k p) n -> p k n", p=P)
    w_up_v = w_up[0].rearrange("(k p) n -> p k n", p=P)
    w_down_v = w_down[0].rearrange("(k p) n -> p k n", p=P)
    w_gate_v = w_ple_gate[0].rearrange("(k p) n -> p k n", p=P)
    w_pup_v = w_ple_up[0].rearrange("(k p) n -> p k n", p=P)
    h_dram = nc.dram_tensor("h_after_mixer", (NT, P, D), F32, kind="Internal").ap()
    gate_dram = nc.dram_tensor("output_gates", (NT, P, HH, P), F32, kind="Internal").ap()
    aq_dram = nc.dram_tensor("attention_queries", (NT, P, GR, P), F32, kind="Internal").ap()
    ak_dram = nc.dram_tensor("attention_keys", (NT, P, P), F32, kind="Internal").ap()

    ctx = ExitStack()
    with ctx:
        def sb(scope, name, shape, dt=F32):
            return scope.enter_context(nc.sbuf_tensor(name, shape, dt))

        def sem(name):
            return ctx.enter_context(nc.semaphore(name))

        ident = sb(ctx, "ident", [P, P])
        rows = sb(ctx, "rows", [P, P])
        cols = sb(ctx, "cols", [P, P])
        CONV_W0, CONV_B0, LB0, HGG0 = 0, 3 * FT, 4 * FT, 4 * FT + HH
        lbv = sb(ctx, "lbv", [P, 8, HH])
        neg_half = sb(ctx, "neg_half", [P, HH])
        ssq = sb(ctx, "ssq", [P, NT + HH])
        msq = sb(ctx, "msq", [P, NT + HH])
        rstd = sb(ctx, "rstd", [P, NT + HH])
        ident_b = sb(ctx, "ident_b", [P, P], BF16)
        level_mask = sb(ctx, "level_mask", [P, LEVELS * 256], BF16)
        band = sb(ctx, "band", [P, 4, P], BF16)

        with ExitStack() as scope:
            gain_mix = sb(scope, "gain_mix", [P, D])
            xt_mix = sb(scope, "xt_mix", [P, NT, D])
            junk_mix = sb(scope, "junk_mix", [P, D], BF16)
        with ExitStack() as mixer_scope:
            qT = sb(mixer_scope, "qT", [P, HH, S])
            fT = sb(mixer_scope, "fT", [P, HH, S])
            kT = sb(mixer_scope, "kT", [P, HH, S])
            with ExitStack() as scope:
                aqT = sb(scope, "aqT", [P, GR, S])
                akT = sb(scope, "akT", [P, S])
                sgT = sb(scope, "sgT", [P, HH, S])
                uh1 = sb(scope, "uh1", [P, KT, S], F32R)
                ul1 = sb(scope, "ul1", [P, KT, S], F32R)
                raw1 = sb(scope, "raw1", [P, 2, KT, SW])
                wh1 = sb(scope, "wh1", [P, 2, KT, P], F32R)
                wl1 = sb(scope, "wl1", [P, 2, KT, P], F32R)
                vT = sb(scope, "vT", [P, HH + 1, S])
            with ExitStack() as scope:
                under_wo_raw = sb(scope, "under_wo_raw", [P, KT, D])
                wo_raw = sb(scope, "wo_raw", [P, KT, D])
            with ExitStack() as scope:
                wo_hi = sb(scope, "wo_hi", [P, KT, D], F32R)
                wo_lo = sb(scope, "wo_lo", [P, KT, D], F32R)
                y_tok = sb(scope, "y_tok", [P, D])
                yT_hi = sb(scope, "yT_hi", [P, KT, P], F32R)
                yT_lo = sb(scope, "yT_lo", [P, KT, P], F32R)
                x2 = sb(scope, "x2", [P, 2, D])
                v_tok = sb(scope, "v_tok", [P, NT, HW])
                av_tok = sb(scope, "av_tok", [P, NT + 1, P])
                sink = sb(scope, "sink", [P, QH])
                qst = sb(scope, "qst", [P, GR, P])
                kst = sb(scope, "kst", [P, 2, P])
                attT = sb(scope, "attT", [P, HW])
                state = sb(scope, "state", [P, HW])
                Ql = sb(scope, "Ql", [P, 2, HW])
                Kl = sb(scope, "Kl", [P, 2, HW])
                FQ = sb(scope, "FQ", [P, 1024])
                FK = sb(scope, "FK", [P, 1024])
                total = sb(scope, "total", [P, HH])
                smax = sb(scope, "smax", [P, 3, QH])
                sden = sb(scope, "sden", [P, 5, QH])
                gate_rows = sb(scope, "gate_rows", [P, 2, HH, P])
                probs = sb(scope, "probs", [P, GR, 2, P])
                probsT = sb(scope, "probsT", [P, GR, 2, P])
                k_tok = sb(scope, "k_tok", [P, HW])
                osq = sb(scope, "osq", [P, HW])
        with ExitStack() as scope:
            xt_ffn = sb(scope, "xt_ffn", [P, 2, D])
            gain_ffn = sb(scope, "gain_ffn", [P, D])
            junk_ffn = sb(scope, "junk_ffn", [P, D], BF16)
            under_xt_late = sb(scope, "under_xt_late", [P, 7 * D])
            xt_late = sb(scope, "xt_late", [P, D])
        with ExitStack() as scope:
            under_d_raw = sb(scope, "under_d_raw", [P, 2 * S + 512])
            d_raw1 = sb(scope, "d_raw1", [P, 512])
            d_raw0 = sb(scope, "d_raw0", [P, 512])
            d_raw = [d_raw0, d_raw1]
            gh = sb(scope, "gh", [P, 2, S], F32R)
            gl = sb(scope, "gl", [P, 2, S], F32R)
            dh = sb(scope, "dh", [P, 2, 512], F32R)
            second_slot = sb(scope, "second_slot", [P, KT, P])
            dl = sb(scope, "dl", [P, 2, 512], F32R)
        with ExitStack() as scope:
            un_ple = sb(scope, "un_ple", [P, 2, D])
            gain_ple = sb(scope, "gain_ple", [P, D])
            junk_ple = sb(scope, "junk_ple", [P, D], BF16)
            gated = sb(scope, "gated", [P, 2, D])
            gain_fin = sb(scope, "gain_fin", [P, D])
            junk_fin = sb(scope, "junk_fin", [P, D], BF16)
        conv = sb(ctx, "conv", [P, 2, S])
        sgm = sb(ctx, "sgm", [P, S])
        pad = sb(ctx, "pad", [P, 512])
        raw2 = sb(ctx, "raw2", [P, 2, KT, SW])
        wh2 = sb(ctx, "wh2", [P, 2, KT, P], F32R)
        wl2 = sb(ctx, "wl2", [P, 2, KT, P], F32R)
        with ExitStack() as scope:
            G = sb(scope, "G", [P, FT, S])
        with ExitStack() as scope:
            gate_raw = sb(scope, "gate_raw", [P, KT, D])
            pup_raw = sb(scope, "pup_raw", [P, PK, D])
        with ExitStack() as scope:
            gate_lo = sb(scope, "gate_lo", [P, KT, D], F32R)
            pup_lo = sb(scope, "pup_lo", [P, PK, D], F32R)
            pup_hi = sb(scope, "pup_hi", [P, PK, D], F32R)
            p_tok = sb(scope, "p_tok", [P, NT, PD])
            pTh = sb(scope, "pTh", [P, PK, S], F32R)
            pTl = sb(scope, "pTl", [P, PK, S], F32R)
            uh3 = sb(scope, "uh3", [P, 2, KT, P], F32R)
            ul3 = sb(scope, "ul3", [P, 2, KT, P], F32R)
            over_G = sb(scope, "over_G", [P, 256])
            with ExitStack() as deeper:
                uh2 = sb(deeper, "uh2", [P, KT, S], F32R)
                ul2 = sb(deeper, "ul2", [P, KT, S], F32R)
            h = sb(scope, "h", [P, NT, D])
            gate_hi = sb(scope, "gate_hi", [P, KT, D], F32R)
        Q = [ctx.enter_context(nc.psum_tensor(f"Q{n}", [P, 1024], F32)) for n in range(4)]
        acc = [Q[t // 2][:, 512 * (t % 2):512 * (t % 2) + 512] for t in range(NT)]

        consts = sem("consts")
        rows_in = sem("rows_in")
        cols_ready = sem("cols_ready")
        colsT = sem("colsT")
        lb_step = sem("lb_step")
        gain_in = [sem(f"gain_in{n}") for n in range(4)]
        mask_step = sem("mask_step")
        sink_arg = sem("sink_arg")
        sink_exped = sem("sink_exped")
        x_in = [sem(f"x_in{n}") for n in range(NT)]
        squared = sem("squared")
        mean_ready = sem("mean_ready")
        rstd_ready = sem("rstd_ready")
        normed = sem("normed")
        turned = sem("turned")
        u_hi = sem("u_hi")
        u_lo = sem("u_lo")
        raw_in = [sem(f"raw_in{n}") for n in range(2)]
        w_hi = sem("w_hi")
        w_lo = sem("w_lo")
        product = sem("product")
        proj_act = sem("proj_act")
        freed = [sem(f"freed{n}") for n in range(2)]
        scaled = sem("scaled")
        v_turned = sem("v_turned")
        v_ready = [sem(f"v_ready{n}") for n in range(2)]
        start_ready = sem("start_ready")
        wo_in = [sem(f"wo_in{n}") for n in range(2)]
        sink_in = sem("sink_in")
        x2_in = [sem(f"x2_in{n}") for n in range(2)]
        put_by = sem("put_by")
        wo_high = sem("wo_high")
        wo_low = sem("wo_low")
        qk_in = sem("qk_in")
        gate_in = [sem(f"gate_in{n}") for n in range(2)]
        scores = sem("scores")
        max_step = sem("max_step")
        max_ready = sem("max_ready")
        exped = sem("exped")
        den_step = sem("den_step")
        den_ready = sem("den_ready")
        probs_turned = sem("probs_turned")
        probsT_ready = sem("probsT_ready")
        attended = sem("attended")
        y_att = sem("y_att")
        factors = sem("factors")
        q_level = sem("q_level")
        k_level = sem("k_level")
        level_product = sem("level_product")
        picked = sem("picked")
        h_half = sem("h_half")
        turn_of_pick = sem("turn_of_pick")
        turn_of_mean = sem("turn_of_mean")
        k_turned = sem("k_turned")
        k_tok_ready = sem("k_tok_ready")
        delta_ready = sem("delta_ready")
        o_ready = sem("o_ready")
        state_ready = sem("state_ready")
        o_squared = sem("o_squared")
        o_sum = sem("o_sum")
        o_mean = sem("o_mean")
        o_rstd = sem("o_rstd")
        y_hg = sem("y_hg")
        y_turned = sem("y_turned")
        y_gated = sem("y_gated")
        y_high = sem("y_high")
        y_low = sem("y_low")
        mixed = sem("mixed")
        h_out = sem("h_out")
        conv_a = sem("conv_a")
        conv_b1 = sem("conv_b1")
        conv_sig = sem("conv_sig")
        silued = sem("silued")
        h_in = sem("h_in")
        d_in = [sem(f"d_in{n}") for n in range(2)]
        d_hi = sem("d_hi")
        d_lo = sem("d_lo")
        g_hi = sem("g_hi")
        g_lo = sem("g_lo")
        down_step = sem("down_step")
        down_half = sem("down_half")
        h_added = sem("h_added")
        p_in = sem("p_in")
        p_turned = sem("p_turned")
        p_hi = sem("p_hi")
        p_lo = sem("p_lo")
        pup_in = sem("pup_in")
        gate_w_in = [sem(f"gate_w_in{n}") for n in range(KT // 2)]
        gate_w_hi = sem("gate_w_hi")
        gate_w_lo = sem("gate_w_lo")
        gate_half = sem("gate_half")
        fin_squared = sem("fin_squared")
        fin_mean = sem("fin_mean")
        fin_rstd = sem("fin_rstd")
        fin_ready = sem("fin_ready")
        pw_hi = sem("pw_hi")
        pw_lo = sem("pw_lo")
        embedded = sem("embedded")
        ple_gate = sem("ple_gate")
        ple_ready = sem("ple_ready")
        ple_added = sem("ple_added")
        stored = sem("stored")

        N_IN = 22
        N_UP = 2 * FT
        UP0, UP_END = N_IN, N_IN + N_UP
        MASK_STEPS = 3 + 3 + 2 * LEVELS
        START_STEPS = 6
        block = ctx.enter_context(nc.Block())

        def h_row(n):
            return (xt_ffn[:, 0, :], xt_ffn[:, 1, :], xt_late[:, :], xt_ffn[:, 0, :], xt_ffn[:, 1, :],
                    y_tok[:, :], x2[:, 0, :], xt_ffn[:, 0, :])[n]

        def halves(n):
            return slice(512 * n, 512 * n + 512)

        v_psum = [Q[2], Q[3], Q[0], Q[1], Q[2]]

        def norm_psum(first, n):
            return Q[0] if first == 2 * NT else Q[2 + n % 2]

        def in_strip(j):
            if 8 <= j < 10:
                a = 4 * HW + P * (j - 8)
                return [(a, P), (a + GR * DH, P)]
            return [(SW * j if j < 8 else 4 * HW + QH * DH, SW)]

        @block.sync
        def _(sp):
            def load_vectors():
                sp.dma_start(rows[0:3 * FT, :], conv_w[0].rearrange("j (f p) -> (j f) p", p=P)).then_inc(rows_in, 16)
                sp.dma_start(rows[CONV_B0:CONV_B0 + FT, :], conv_b[0].rearrange("(f p) -> f p", p=P)).then_inc(rows_in, 16)
                sp.dma_start(rows[LB0:LB0 + HH, :], lb_logits[0].rearrange("(f p) -> f p", p=P)).then_inc(rows_in, 16)
                sp.dma_start(rows[HGG0:HGG0 + HH, :], hg_norm_g[0].rearrange("(f p) -> f p", p=P)).then_inc(rows_in, 16)

            def load_strip(j):
                at = 0
                for c, w in in_strip(j):
                    sp.dma_start(raw1[:, j % 2, :, at:at + w], w_in_v[:, :, c:c + w]).then_inc(raw_in[j % 2], 16)
                    at += w

            for n in range(NT):
                sp.dma_start(xt_mix[:, n, :], x_t[n]).then_inc(x_in[n], 16)
                if n == 0:
                    sp.dma_start(gain_mix[:, :], g_mix[0:1, :].to_broadcast([P, D])).then_inc(gain_in[0], 16)
                if n == 2:
                    load_vectors()
                if n in (NT // 2, NT - 1):
                    load_strip(n // (NT - 1))
            for j in range(2, N_IN // 2):
                sp.wait_ge(w_lo, 2 * (j - 1))
                load_strip(j)

            def put_by_rows(dram, sbuf):
                for a in range(HH):
                    sp.dma_start(dram[:, :, a, :].rearrange("n p c -> p n c"),
                                 sbuf[:, a, :].rearrange("p (n c) -> p n c", c=P)).then_inc(put_by, 16)

            sp.wait_ge(scaled, 12)
            put_by_rows(gate_dram, sgT)
            sp.wait_ge(freed[0], N_IN // 2 - 1)
            sp.wait_ge(freed[1], N_IN // 2 - 1)
            put_by_rows(aq_dram, aqT)
            sp.wait_ge(freed[0], N_IN // 2)
            sp.dma_start(ak_dram.rearrange("n p c -> p n c"),
                         akT[:, :].rearrange("p (n c) -> p n c", c=P)).then_inc(put_by, 16)

            sp.wait_ge(product, N_IN)
            sp.wait_ge(put_by, 16 * (HH + GR + 1))

            def load_qk(n, t):
                wait(sp, scores, 2 * n)
                sp.dma_start(qst[:, :, :], aq_dram[ds(n, 1), :, :, :].rearrange("a p j c -> (a p) j c")).then_inc(qk_in, 16)
                sp.dma_start(kst[:, t, :], ak_dram[ds(n, 1), :, :].rearrange("a p c -> (a p) c")).then_inc(qk_in, 16)

            def load_gate(n, t):
                wait(sp, y_gated, n - 1)
                sp.dma_start(gate_rows[:, t, :, :],
                             gate_dram[ds(n, 1), :, :, :].rearrange("b p a c -> (b p) a c")).then_inc(gate_in[t], 16)

            def load_residual(n, t):
                wait(sp, h_out, 16 * (n - 1))
                sp.dma_start(x2[:, t, :], x_t[ds(n, 1), :, :].rearrange("a p d -> (a p) d")).then_inc(x2_in[t], 16)

            def store_h(n, t):
                sp.wait_ge(h_half, 2 * n + 2)
                sp.dma_start(h_dram[ds(n, 1), :, :].rearrange("a p d -> (a p) d"), x2[:, t, :]).then_inc(h_out, 16)

            load_qk(0, 0)
            sp.dma_start(sink[:, :], attn_sinks[0:1, :].to_broadcast([P, QH])).then_inc(sink_in, 16)
            for k in range(KT):
                sp.dma_start(wo_raw[:, k, :], w_out_v[:, k, :]).then_inc(wo_in[2 * k // KT], 16)
            for n in range(2):
                sp.wait_ge(v_ready[n], (HH + 2 - n) // 2)

            load_gate(0, 0)
            load_residual(0, 0)
            load_qk(1, 1)
            load_gate(1, 1)
            load_residual(1, 1)

            def during_tile(n, t):
                load_qk(n + 1, t)
                load_gate(n + 1, t)
                store_h(n - 1, t)
                load_residual(n + 1, t)

            with sp.Fori(0, NT // 2 - 1) as i:
                for t in range(2):
                    during_tile(2 * i + 1 + t, t)

            sp.wait_ge(q_level, 8 * (NT - 1) + 1)
            sp.wait_ge(k_level, 8 * (NT - 1) + 1)
            sp.wait_ge(level_product, 8 * (NT - 1) + 1)
            sp.wait_ge(factors, 15 * (NT - 1) + 2)
            sp.dma_start(gain_ffn[:, :], g_ffn[0:1, :].to_broadcast([P, D])).then_inc(gain_in[1], 16)

            def load_h(n):
                sp.wait_ge(h_out, 16 * (n + 1))
                if 3 <= n < 5:
                    sp.wait_ge(turned, NT + n - 2)
                if n == 5:
                    sp.wait_ge(y_low, 2 * NT)
                sp.dma_start(h_row(n), h_dram[n]).then_inc(x_in[n], 16)

            def load_up(i):
                for half in range(2):
                    sp.wait_ge(w_lo, UP0 - 1 + 4 * i + half)
                    sp.dma_start(raw2[:, half, :, :], w_up_v[:, :, ds(F * half + SW * i, SW)]).then_inc(raw_in[half], 16)

            for n in range(3):
                load_h(n)
            load_up(0)
            store_h(NT - 2, 0)
            for n in range(3, NT - 2):
                load_h(n)
            store_h(NT - 1, 1)

            with sp.Fori(1, FT // 2) as i:
                load_up(i)

            def load_down(k, t, hf):
                sp.dma_start(d_raw[t][:, :],
                             w_down_v[:, ds(k, 1), 512 * hf:512 * hf + 512].rearrange("p a n -> p (a n)")).then_inc(d_in[t], 16)

            def down_loads(hf, start, stop):
                with sp.Fori(start, stop) as i:
                    for t in range(2):
                        sp.wait_ge(d_lo, FT * hf + 2 * i + t - 1)
                        load_down(2 * i + t, t, hf)

            for hf in range(2):
                for t in range(2):
                    if hf:
                        sp.wait_ge(d_lo, FT + t - 1)
                    elif t:
                        sp.wait_ge(silued, FT)
                    load_down(t, t, hf)
                if hf == 0:
                    down_loads(0, 1, 3)
                    sp.wait_ge(product, UP_END)
                    sp.wait_ge(h_out, 16 * NT)
                    for part in range(4):
                        n = NT // 4 * part
                        sp.dma_start(h[:, n:n + NT // 4, :],
                                     h_dram[n:n + NT // 4].rearrange("n p d -> p n d")).then_inc(h_in, 16)
                        down_loads(0, 3 + 2 * part, 5 + 2 * part)
                else:
                    down_loads(1, 1, 5)
                    for part in range(6):
                        if part < KT // 2:
                            sp.wait_ge(g_lo, FT + 2 * part + 2)
                            for k in (2 * part, 2 * part + 1):
                                sp.dma_start(gate_raw[:, k, :], w_gate_v[:, k, :]).then_inc(gate_w_in[part], 16)
                        elif part == KT // 2:
                            sp.wait_ge(g_lo, FT + 12)
                            sp.dma_start(pup_raw[:, :, :], w_pup_v).then_inc(pup_in, 16)
                        else:
                            sp.wait_ge(g_lo, FT + 14)
                            sp.dma_start(p_tok[:, :, :], p_t).then_inc(p_in, 16)
                        for t in range(2):
                            k = 10 + 2 * part + t
                            sp.wait_ge(d_lo, FT + k - 1)
                            load_down(k, t, 1)

            sp.wait_ge(d_lo, 2 * FT)
            sp.dma_start(gain_ple[:, :], g_ple[0:1, :].to_broadcast([P, D])).then_inc(gain_in[2], 16)
            sp.wait_ge(down_half, 2 * NT)
            sp.dma_start(gain_fin[:, :], g_final.rearrange("(a d) -> a d", a=1).to_broadcast([P, D])).then_inc(gain_in[3], 16)
            for n in range(NT):
                sp.wait_ge(fin_ready, n + 1)
                sp.dma_start(out_t[n], h[:, n, :]).then_inc(stored, 16)
            sp.wait_ge(stored, 16 * NT)

        def chunk(n):
            return ds(P * n, P)

        def f_off(l):
            return sum(HW >> m for m in range(l))

        def factor(t, l):
            return t[:, f_off(l):f_off(l) + (HW >> l)].rearrange("p (b two) -> p b two", two=2)

        @block.gpsimd
        def _(pool):
            nc.gpsimd.memset(ident[:, :], 0.0).then_inc(consts, 1)
            nc.gpsimd.memset(neg_half[:, :], -0.5).then_inc(consts, 1)
            pool.wait_ge(consts, 2)
            nc.gpsimd.affine_select(out=ident[:, :], in_=ident[:, :], compare_op=ALU.not_equal, fill=1.0, base=0,
                                    pattern=[[-1, P]], channel_multiplier=1).then_inc(consts, 1)

            def norm_rows(first, tiles=range(NT)):
                for n in tiles:
                    pool.wait_ge(squared, first + n + 1)
                    nc.gpsimd.tensor_scalar(msq[:, n:n + 1], ssq[:, n:n + 1], 1.0 / D, EPS,
                                            ALU.mult, ALU.add).then_inc(mean_ready, 1)
                    pool.wait_ge(mean_ready, first + n + 1)
                    nc.gpsimd.tensor_tensor(rstd[:, n:n + 1], msq[:, n:n + 1], neg_half[:, 0:1],
                                            ALU.pow).then_inc(rstd_ready, 1)

            pool.wait_ge(consts, 3)
            nc.gpsimd.tensor_copy(ident_b[:, :], ident[:, :]).then_inc(mask_step, 1)
            nc.gpsimd.memset(level_mask[:, :], 1.0).then_inc(mask_step, 1)
            nc.gpsimd.memset(band[:, 0:3, :], 0.0).then_inc(mask_step, 1)
            nc.gpsimd.memset(band[:, 3, :], MASK_VALUE)
            norm_rows(0)
            steps = 3
            pool.wait_ge(mask_step, steps)
            for block_of_band, (op, sign) in enumerate(((ALU.is_gt, 1), (ALU.is_ge, -1), (ALU.is_gt, 1))):
                nc.gpsimd.affine_select(out=band[:, block_of_band, :], in_=band[:, block_of_band, :], compare_op=op,
                                        fill=MASK_VALUE, base=0, pattern=[[sign, P]],
                                        channel_multiplier=-sign).then_inc(mask_step, 1)
                steps += 1
            for l in range(LEVELS):
                b = 1 << l
                m = level_mask[:, 256 * l:256 * l + 256].rearrange("p (a c r) -> p a c r", a=HH, r=b)
                nc.gpsimd.affine_select(out=m, in_=m, compare_op=ALU.is_ge, fill=0.0, base=0,
                                        pattern=[[0, HH], [-2 * b, 64 // b], [0, b]],
                                        channel_multiplier=1).then_inc(mask_step, 1)
                steps += 1
                pool.wait_ge(mask_step, steps)
                nc.gpsimd.affine_select(out=m, in_=m, compare_op=ALU.is_ge, fill=0.0, base=b - 1,
                                        pattern=[[0, HH], [2 * b, 64 // b], [0, b]],
                                        channel_multiplier=-1).then_inc(mask_step, 1)
                steps += 1
            assert steps == MASK_STEPS

            pool.wait_ge(product, N_IN)
            nc.gpsimd.memset(kst[:, 1, :], 0.0).then_inc(start_ready, 1)
            nc.gpsimd.memset(FQ[:, :], 1.0).then_inc(start_ready, 1)
            nc.gpsimd.memset(FK[:, :], 1.0).then_inc(start_ready, 1)
            nc.gpsimd.memset(attT[:, :], 0.0).then_inc(start_ready, 1)
            nc.gpsimd.memset(state[:, :], 0.0).then_inc(start_ready, 1)
            nc.gpsimd.memset(av_tok[:, 0, :], 0.0).then_inc(start_ready, 1)

            def k_step(n, l):
                if l == 1:
                    wait(pool, k_turned, n)
                else:
                    pool.wait_ge(level_product, 8 * n + l)
                pool.wait_ge(k_level, 8 * n + l)
                pool.wait_ge(factors, 15 * n + 2 * l)
                b = 1 << (l - 1)
                nc.gpsimd.tensor_tensor(Kl[:, l % 2, :].rearrange("p (c r) -> p c r", r=b),
                                        Kl[:, (l - 1) % 2, :].rearrange("p (c r) -> p c r", r=b),
                                        FK[:, f_off(l - 1):f_off(l)].unsqueeze(2).to_broadcast([P, HW // b, b]),
                                        ALU.mult).then_inc(k_level, 1)

            def o_norm(n):
                pool.wait_ge(o_sum, n + 1)
                pool.sem_inc(turn_of_mean, 1)
                nc.gpsimd.tensor_scalar(msq[:, NT:NT + HH], ssq[:, NT:NT + HH], 1.0 / P, EPS,
                                        ALU.mult, ALU.add).then_inc(o_mean, 1)
                pool.wait_ge(o_mean, n + 1)
                nc.gpsimd.tensor_tensor(rstd[:, NT:NT + HH], msq[:, NT:NT + HH], neg_half[:, :],
                                        ALU.pow).then_inc(o_rstd, 1)

            def pool_tile(n, first=False):
                k_step(n, 1)
                if not first:
                    o_norm(n - 1)
                for l in range(2, LEVELS + 1):
                    k_step(n, l)

            pool_tile(0, True)
            pool_tile(1)
            with pool.Fori(1, NT // 2) as i:
                for t in range(2):
                    pool_tile(2 * i + t)
            norm_rows(NT, range(2))
            o_norm(NT - 1)
            norm_rows(NT, range(2, NT))
            norm_rows(2 * NT, range(2))
            for n in range(NT):
                norm_rows(2 * NT, range(n + 2, min(n + 3, NT)))
                pool.wait_ge(fin_squared, n + 1)
                nc.gpsimd.tensor_scalar(msq[:, n:n + 1], ssq[:, n:n + 1], 1.0 / D, EPS,
                                        ALU.mult, ALU.add).then_inc(fin_mean, 1)
                pool.wait_ge(fin_mean, n + 1)
                nc.gpsimd.tensor_tensor(rstd[:, n:n + 1], msq[:, n:n + 1], neg_half[:, 0:1],
                                        ALU.pow).then_inc(fin_rstd, 1)

        N0 = 7
        N1 = 6

        def split_count(m):
            s = m // 2
            return sum(16 * len(in_strip(j)) for j in range(s % 2, s + 1, 2))

        def in_split(t, m):
            s = m // 2
            if t is raw1:
                if 8 <= s < 10:
                    return raw1[:, s % 2, :, :].rearrange("p k (a c) -> p k a c", a=2)[:, :, :, DH * (m % 2):DH * (m % 2) + DH]
                return raw1[:, s % 2, :, P * (m % 2):P * (m % 2) + P]
            v = t[:, m % 2, :, :]
            return v.rearrange("p k (a c) -> p k a c", a=2) if 8 <= s < 10 else v

        @block.scalar
        def _(act):
            def square(first, n, src, junk):
                wait(act, squared, first + n)
                nc.scalar.activation(junk[:, :], src, ACT.Square, accum_out=ssq[:, n:n + 1]).then_inc(squared, 1)

            def high_half(first, n, uh):
                act.wait_ge(turned, first + n + 1)
                nc.scalar.activation(uh[:, :, P * n:P * n + P], norm_psum(first, n)[:, :].rearrange("p (k c) -> p k c", c=P),
                                     ACT.Copy).then_inc(u_hi, 1)

            def split_in(m):
                act.wait_ge(raw_in[(m // 2) % 2], split_count(m))
                if m >= 2:
                    act.wait_ge(product, m - 1)
                nc.scalar.activation(in_split(wh1, m), in_split(raw1, m), ACT.Copy).then_inc(w_hi, 1)

            def square_x(n):
                act.wait_ge(x_in[n], 16)
                square(0, n, xt_mix[:, n, :], junk_mix)

            for n in range(3):
                square_x(n)
            for n in range(NT):
                high_half(0, n, uh1)
                if n + 3 < NT:
                    square_x(n + 3)
                if n in (2, 3):
                    split_in(n - 2)

            act.wait_ge(lb_step, 2)
            nc.scalar.activation(lbv[:, 2, :], lbv[:, 1, :], ACT.Exp).then_inc(lb_step, 1)

            for m in range(N_IN):
                if 1 <= m < N_IN - 1:
                    split_in(m + 1)
                act.wait_ge(product, m + 1)
                src = Q[m % 2][:, :]
                if m < 4:
                    nc.scalar.activation(qT[:, m, :], src, ACT.Sigmoid).then_inc(proj_act, 1)
                elif m < 8:
                    nc.scalar.activation(fT[:, m - 4, :], src, ACT.Sigmoid)
                    nc.scalar.activation(kT[:, m - 4, :], src, ACT.Sigmoid, scale=-1.0).then_inc(freed[m % 2], 1)
                elif m < 12:
                    nc.scalar.activation(vT[:, m - 8, :], src, ACT.Copy).then_inc(freed[m % 2], 1)
                elif m < 16:
                    nc.scalar.activation(sgT[:, m - 12, :], src, ACT.Sigmoid).then_inc(freed[m % 2], 1)
                elif m < 20:
                    nc.scalar.activation(aqT[:, m - 16, :], src, ACT.Copy).then_inc(freed[m % 2], 1)
                else:
                    nc.scalar.activation(akT[:, :] if m == 20 else vT[:, HH, :], src,
                                         ACT.Copy).then_inc(freed[m % 2], 1)

            act.wait_ge(product, N_IN)
            for c in range(1, HH + 1, 2):
                act.wait_ge(v_turned, c + 1)
                nc.scalar.activation(v_tok[:, :, P * c:P * c + P], v_psum[c][:, :].rearrange("p (n c) -> p n c", c=P),
                                     ACT.Copy).then_inc(v_ready[1], 1)

            def first_keys(n):
                wait(act, k_level, 8 * n)
                wait(act, level_product, 8 * n)
                nc.scalar.activation(Kl[:, 0, :].rearrange("p (a t) -> p a t", t=P), kT[:, :, chunk(n)],
                                     ACT.Copy).then_inc(k_level, 1)

            def exps(n, g):
                act.wait_ge(max_ready, 2 * n + g + 1)
                wait(act, probs_turned, 2 * n + g)
                for j in range(GR):
                    nc.scalar.activation(probs[:, j, :, :].rearrange("p a c -> p (a c)"),
                                         Q[0][:, 2 * P * j:2 * P * j + 2 * P], ACT.Exp,
                                         bias=smax[:, 2, GR * g + j:GR * g + j + 1], scale=DH ** -0.5,
                                         accum_out=sden[:, 0, GR * g + j:GR * g + j + 1]).then_inc(exped, 1)
                act.wait_ge(sink_arg, 2 * n + g + 1)
                nc.scalar.activation(sden[:, 2, GR * g:GR * g + GR], sden[:, 1, GR * g:GR * g + GR],
                                     ACT.Exp).then_inc(sink_exped, 1)

            def probs_out(n, g):
                act.wait_ge(probs_turned, 2 * n + g + 1)
                wait(act, attended, 2 * n + g)
                nc.scalar.activation(probsT[:, :, :, :].rearrange("p a b c -> p (a b c)"), Q[1][:, :],
                                     ACT.Copy).then_inc(probsT_ready, 1)

            def chunk_end(n):
                act.wait_ge(k_turned, n + 1)
                wait(act, delta_ready, n)
                nc.scalar.activation(k_tok[:, :], Q[3][:, 512:1024], ACT.Copy).then_inc(k_tok_ready, 1)
                act.wait_ge(o_ready, n + 1)
                wait(act, o_sum, n)
                nc.scalar.activation(osq[:, :], Q[3][:, 0:512], ACT.Square).then_inc(o_squared, 1)

            def split_y(n):
                act.wait_ge(y_turned, n + 1)
                nc.scalar.activation(yT_hi[:, HH:KT, :].rearrange("p k c -> p (k c)"), Q[1][:, 512:1024],
                                     ACT.Copy).then_inc(y_high, 1)
                act.wait_ge(y_gated, n + 1)
                nc.scalar.activation(yT_hi[:, 0:HH, :].rearrange("p k c -> p (k c)"), y_tok[:, 0:HW],
                                     ACT.Copy).then_inc(y_high, 1)

            def high_wo(half):
                act.wait_ge(wo_in[half], 16 * KT // 2)
                for k in range(KT // 2 * half, KT // 2 * half + KT // 2):
                    nc.scalar.activation(wo_hi[:, k, :], wo_raw[:, k, :], ACT.Copy).then_inc(wo_high, 1)

            def act_tile(n, t, first=False):
                first_keys(n)
                if not first:
                    chunk_end(n - 1)
                exps(n, 0)
                if not first:
                    split_y(n - 1)
                else:
                    high_wo(0)
                probs_out(n, 0)
                exps(n, 1)
                if first:
                    high_wo(1)
                probs_out(n, 1)

            act_tile(0, 0, True)
            act_tile(1, 1)
            with act.Fori(1, NT // 2) as i:
                for t in range(2):
                    act_tile(2 * i + t, t)
            def square_h(n):
                if n < NT - 2:
                    act.wait_ge(x_in[n], 32)
                else:
                    act.wait_ge(h_half, 2 * n + 2)
                square(NT, n, h_row(n) if n < NT - 1 else x2[:, 1, :], junk_ffn)

            def split_up(i, q):
                act.wait_ge(raw_in[q % 2], 16 * (N0 if q % 2 == 0 else N1) + 16 * i + 16)
                act.wait_ge(product, UP0 - 1 + 4 * i + q)
                nc.scalar.activation(wh2[:, q % 2, :, :], raw2[:, q % 2, :, P * (q // 2):P * (q // 2) + P],
                                     ACT.Copy).then_inc(w_hi, 1)

            for n in range(2):
                square_h(n)
            chunk_end(NT - 1)
            square_h(2)
            split_y(NT - 1)
            for n in range(NT):
                high_half(NT, n, uh2)
                if n + 3 < NT:
                    square_h(n + 3)
                if n in (2, 3):
                    act.wait_ge(turned, NT + n)
                    split_up(0, n - 2)

            def up_turn(i, first=False, last=False):
                for q in range(4):
                    if q < 3:
                        if q or not first:
                            split_up(i, q + 1)
                    elif not last:
                        split_up(i + 1, 0)
                    f = 2 * i + q // 2
                    if q % 2 == 0:
                        act.wait_ge(product, UP0 + 4 * i + q + 1)
                        act.wait_ge(freed[1], N_IN // 2 - 1 + f)
                        nc.scalar.activation(conv[:, q // 2, :], Q[q][:, :], ACT.Identity,
                                             bias=cols[:, ds(CONV_B0 + f, 1)],
                                             scale=cols[:, ds(CONV_W0 + 2 * FT + f, 1)]).then_inc(conv_a, 1)
                    else:
                        act.wait_ge(freed[0], N_IN // 2 + f + 1)
                        nc.scalar.activation(sgm[:, :], conv[:, q // 2, :], ACT.Sigmoid).then_inc(conv_sig, 1)

            up_turn(0, first=True)
            with act.Fori(1, FT // 2 - 1) as i:
                up_turn(i)
            up_turn(FT // 2 - 1, last=True)

            act.wait_ge(product, UP_END - 1)
            act.wait_ge(w_lo, UP_END)
            def split_down(k, t, s, turn=0):
                if s is not None:
                    act.wait_ge(d_in[t], 16 * (FT // 2) * (s // FT) + 16 * turn + 16)
                nc.scalar.activation(gh[:, t, :], G[:, ds(k, 1), :].rearrange("p a s -> p (a s)"),
                                     ACT.Copy).then_inc(g_hi, 1)
                nc.scalar.activation(dh[:, t, :], d_raw[t][:, :],
                                     ACT.Copy).then_inc(d_hi, 1)

            def high_weights(part):
                act.wait_ge(gate_w_in[part], 32)
                for k in (2 * part, 2 * part + 1):
                    nc.scalar.activation(gate_hi[:, k, :], gate_raw[:, k, :], ACT.Copy).then_inc(gate_w_hi, 1)

            def split_steps(hf, start, stop):
                with act.Fori(start, stop) as i:
                    for t in range(2):
                        act.wait_ge(down_step, (FT - 1) * hf + 2 * i + t - 1)
                        act.wait_ge(d_in[t], 16 * (FT // 2) * hf + 16 * i + 16)
                        split_down(2 * i + t, t, None)

            for t in range(2):
                split_down(t, t, t)
            act.wait_ge(freed[1], (N_IN + N_UP) // 2)
            split_steps(0, 1, FT // 2)
            act.wait_ge(down_step, FT - 1)
            split_down(0, 0, FT)
            act.wait_ge(down_half, NT)
            split_down(1, 1, FT + 1)
            split_steps(1, 1, FT // 2 - KT // 2)
            for part in range(KT // 2):
                i = FT // 2 - KT // 2 + part
                for t in range(2):
                    act.wait_ge(down_step, FT - 1 + 2 * i + t - 1)
                    split_down(2 * i + t, t, FT + 2 * i + t, i)
                high_weights(part)

            def square_sum(n):
                act.wait_ge(h_added, NT + n + 1)
                square(2 * NT, n, h[:, n, :], junk_ple)

            def high_sum(n):
                act.wait_ge(turned, 2 * NT + n + 1)
                nc.scalar.activation(uh3[:, n % 2, :, :], Q[0][:, :].rearrange("p (k c) -> p k c", c=P),
                                     ACT.Copy).then_inc(u_hi, 1)

            square_sum(0)
            square_sum(1)
            high_sum(0)
            act.wait_ge(pup_in, 16)
            for k in range(PK):
                nc.scalar.activation(pup_hi[:, k, :], pup_raw[:, k, :], ACT.Copy).then_inc(pw_hi, 1)
            for k in range(PK):
                act.wait_ge(p_turned, k + 1)
                nc.scalar.activation(pTh[:, k, :], Q[(1, 3)[k]][:, :], ACT.Copy).then_inc(p_hi, 1)
            for n in range(NT):
                if n + 1 < NT:
                    high_sum(n + 1)
                for half in range(2):
                    act.wait_ge(gate_half, 2 * n + half + 1)
                    if n >= 2:
                        act.wait_ge(ple_added, 2 * (n - 1))
                    nc.scalar.activation(gated[:, n % 2, halves(half)], Q[2 + n % 2][:, halves(half)],
                                         ACT.Sigmoid).then_inc(ple_gate, 1)
                if n + 2 < NT:
                    square_sum(n + 2)
                act.wait_ge(ple_added, 2 * n + 2)
                if n:
                    act.wait_ge(fin_squared, n)
                nc.scalar.activation(junk_fin[:, :], h[:, n, :], ACT.Square,
                                     accum_out=ssq[:, n:n + 1]).then_inc(fin_squared, 1)

        def parts(wh, wl, uh, ul):
            return ((wh, uh), (wh, ul), (wl, uh))

        @block.tensor
        def _(pe):
            def turn_rows(first, n, src):
                pe.wait_ge(normed, first + n + 1)
                if n >= 2:
                    pe.wait_ge(u_lo, first + n - 1)
                for k in range(KT):
                    tr = nc.tensor.transpose(norm_psum(first, n)[:, P * k:P * k + P], src[:, P * k:P * k + P],
                                             ident[:, :])
                tr.then_inc(turned, 1)

            def project(wh, wl, uh, ul, slot, dst, rows):
                last = wh.shape[2] - 1
                for k in rows:
                    for a, b in parts(wh, wl, uh, ul):
                        for half in range(2):
                            mm = nc.tensor.matmul(dst[:, 512 * half:512 * half + 512], a[:, slot, k, :],
                                                  b[:, k, 512 * half:512 * half + 512],
                                                  start=(k == 0 and a is wh and b is uh),
                                                  stop=(k == last and a is wl))
                return mm

            def project_half(wh, wl, uh, ul, slot, half, rows):
                for k in rows:
                    for a, b in parts(wh, wl, uh, ul):
                        mm = nc.tensor.matmul(Q[slot][:, halves(half)], a[:, slot, k, :], b[:, k, halves(half)],
                                              start=(k == 0 and a is wh and b is uh), stop=(k == KT - 1 and a is wl))
                return mm

            def first_products(first, wh, wl, uh, ul, src, done):
                pe.wait_ge(u_lo, first + NT // 2)
                pe.wait_ge(w_lo, done + 1)
                for quarter in range(4):
                    if quarter == 2:
                        pe.wait_ge(w_lo, done + 2)
                    project_half(wh, wl, uh, ul, quarter // 2, 0,
                                 range(KT // 2 * (quarter % 2), KT // 2 * (quarter % 2 + 1)))
                    if quarter < 3:
                        turn_rows(first, NT - 3 + quarter, src(NT - 3 + quarter))
                pe.wait_ge(u_lo, first + NT)
                for m in range(2):
                    project_half(wh, wl, uh, ul, m, 1, range(KT)).then_inc(product, 1)

            pe.wait_ge(consts, 3)
            for n in range(NT // 2 + 1):
                turn_rows(0, n, xt_mix[:, n, :])
                if n == 2:
                    pe.wait_ge(rows_in, 64)
                    nc.tensor.transpose(Q[1][:, 0:96], rows[0:96, :], ident[0:96, 0:96]).then_inc(colsT, 1)
            pe.wait_ge(cols_ready, 1)
            first_products(0, wh1, wl1, uh1, ul1, lambda n: xt_mix[:, n, :], 0)

            def in_turn(i):
                for t in range(2):
                    pe.wait_ge(w_lo, 2 * i + t + 1)
                    pe.wait_ge(freed[t], i)
                    project(wh1, wl1, uh1, ul1, t, Q[t], range(KT)).then_inc(product, 1)

            def turn_v(c):
                for n in range(NT):
                    tr = nc.tensor.transpose(v_psum[c][:, P * n:P * n + P], vT[:, c, P * n:P * n + P], ident[:, :])
                tr.then_inc(v_turned, 1)

            with pe.Fori(1, N_IN // 4 + 1) as i:
                in_turn(i)
            pe.wait_ge(u_lo, NT)
            for c in range(2):
                pe.wait_ge(freed[c], 5)
                turn_v(c)
            with pe.Fori(N_IN // 4 + 1, N_IN // 2) as i:
                in_turn(i)

            pe.wait_ge(freed[0], N_IN // 2)
            turn_v(2)
            pe.wait_ge(freed[1], N_IN // 2)
            turn_v(3)
            pe.wait_ge(v_ready[0], 1)
            turn_v(4)

            def score(n, t, g, first):
                if g == 0:
                    pe.wait_ge(qk_in, 32 * n + 32)
                    wait(pe, exped, 8 * n)
                else:
                    pe.wait_ge(exped, 8 * n + 4)
                mask = band[:, 0:2, :] if t else band[:, 1:4:2, :] if first else band[:, 1:3, :]
                for j in range(GR):
                    dst = Q[0][:, 2 * P * j:2 * P * j + 2 * P]
                    nc.tensor.matmul(dst, qst[DH * g:DH * g + DH, j, :],
                                     kst[DH * g:DH * g + DH, :, :].rearrange("p a c -> p (a c)"), start=True, stop=False)
                    mm = nc.tensor.matmul(dst.rearrange("p (a c) -> p a c", a=2), ident_b[:, :], mask,
                                          start=False, stop=True)
                mm.then_inc(scores, 1)

            def turn_probs(n, g):
                pe.wait_ge(exped, 8 * n + 4 * g + 4)
                if g == 0:
                    wait(pe, y_gated, n)
                    wait(pe, y_low, 2 * n - 1)
                else:
                    pe.wait_ge(probsT_ready, 2 * n + 1)
                for j in range(GR):
                    for s in range(2):
                        c = P * (2 * j + s)
                        tr = nc.tensor.transpose(Q[1][:, c:c + P], probs[:, j, s, :], ident[:, :])
                tr.then_inc(probs_turned, 1)

            def attend(n, t, g):
                pe.wait_ge(probsT_ready, 2 * n + g + 1)
                if g == 0:
                    wait(pe, y_hg, n)
                for j in range(GR):
                    for s in range(2):
                        blk = n + 1 if s == t else n
                        c = DH * (GR * g + j)
                        mm = nc.tensor.matmul(Q[3][:, c:c + DH], probsT[:, j, s, :],
                                              av_tok[:, ds(blk, 1), DH * g:DH * g + DH].rearrange("p a c -> p (a c)"),
                                              start=(s == 0), stop=(s == 1))
                mm.then_inc(attended, 1)

            def level(n, g):
                if g >= 2:
                    pe.wait_ge(picked, 8 * n + g - 1)
                else:
                    wait(pe, picked, 8 * n + g - 1)
                l = max(g - 1, 0)
                pe.wait_ge(k_level, 8 * n + l + 1)
                if g:
                    pe.wait_ge(q_level, 8 * n + l + 1)
                b = 1 << l
                base = 512 * (g % 2)
                for a in range(HH):
                    keys = Kl[:, l % 2, P * a:P * a + P]
                    if g == 0:
                        mm = nc.tensor.matmul(Q[2][:, base + P * a:base + P * a + P], keys, qT[:, a, chunk(n)],
                                              start=True, stop=True)
                    else:
                        right = Ql[:, l % 2, P * a:P * a + P].rearrange("p (c two r) -> p c two r", two=2, r=b)[:, :, 1, :]
                        mm = nc.tensor.matmul(Q[2][:, base + 64 * a:base + 64 * a + 64].rearrange("p (c r) -> p c r", r=b),
                                              keys, right, start=True, stop=True)
                mm.then_inc(level_product, 1)

            def hgrn_out(n):
                pe.wait_ge(q_level, 8 * n + 8)
                pe.wait_ge(k_level, 8 * n + 8)
                wait(pe, state_ready, 4 * n)
                wait(pe, h_half, 2 * n)
                for a in range(HH):
                    tr = nc.tensor.transpose(Q[3][:, 512 + P * a:512 + P * a + P], Kl[:, 1, P * a:P * a + P], ident[:, :])
                tr.then_inc(k_turned, 1)
                pe.wait_ge(picked, 8 * n + 8)
                pe.wait_ge(y_att, n + 1)
                for a in range(HH):
                    c = slice(P * a, P * a + P)
                    nc.tensor.matmul(Q[3][:, c], Ql[:, 1, c], state[:, c], start=True, stop=False)
                    mm = nc.tensor.matmul(Q[3][:, c], attT[:, c],
                                          v_tok[:, ds(n, 1), c].rearrange("p a c -> p (a c)"), start=False, stop=True)
                mm.then_inc(o_ready, 1)
                pe.wait_ge(k_tok_ready, n + 1)
                for a in range(HH):
                    c = slice(P * a, P * a + P)
                    mm = nc.tensor.matmul(Q[3][:, 512 + P * a:512 + P * a + P], k_tok[:, c],
                                          v_tok[:, ds(n, 1), c].rearrange("p a c -> p (a c)"), start=True, stop=True)
                mm.then_inc(delta_ready, 1)

            def turn_y(n):
                pe.wait_ge(y_hg, n + 1)
                pe.wait_ge(probsT_ready, 2 * n + 2)
                for k in range(KT):
                    tr = nc.tensor.transpose(Q[1][:, P * k:P * k + P], y_tok[:, P * k:P * k + P], ident[:, :])
                tr.then_inc(y_turned, 1)

            def mix_out(n, half, part, dst=None, wo_slabs=False):
                if part == 0 and half == 0:
                    pe.wait_ge(y_low, 2 * n + 2)
                elif part == 0 and dst is None:
                    pe.wait_ge(h_half, 2 * n + 1)
                if part == 0 and half == 0:
                    if dst is None:
                        pe.wait_ge(state_ready, 4 * n + 4)
                dst = Q[3][:, 512:1024] if dst is None else dst[:, halves(half)]
                if wo_slabs:
                    pe.wait_ge(wo_low, KT // 2 * (part + 1))
                for k in range(KT // 2 * part, KT // 2 * part + KT // 2):
                    for j, (a, b) in enumerate(parts(yT_hi, yT_lo, wo_hi, wo_lo)):
                        mm = nc.tensor.matmul(dst, a[:, k, :], b[:, k, halves(half)], start=(k == 0 and j == 0),
                                              stop=(k == KT - 1 and j == 2))
                if part:
                    mm.then_inc(mixed, 1)

            def pe_tile(n, t, first=False, second=False):
                score(n, t, 0, first)
                if first:
                    pe.wait_ge(v_ready[0], 3)
                level(n, 0)
                level(n, 1)
                if not first:
                    turn_y(n - 1)
                level(n, 2)
                score(n, t, 1, first)
                if first:
                    for parity in range(2):
                        pe.wait_ge(v_ready[parity], (HH + 2 - parity) // 2)
                turn_probs(n, 0)
                if not first:
                    mix_out(n - 1, 0, 0, wo_slabs=second)
                level(n, 3)
                attend(n, t, 0)
                turn_probs(n, 1)
                level(n, 4)
                if not first:
                    mix_out(n - 1, 0, 1, wo_slabs=second)
                level(n, 5)
                attend(n, t, 1)
                if not first:
                    mix_out(n - 1, 1, 0)
                level(n, 6)
                if not first:
                    mix_out(n - 1, 1, 1)
                level(n, 7)
                hgrn_out(n)

            pe.wait_ge(mask_step, MASK_STEPS)
            pe.wait_ge(start_ready, START_STEPS)
            pe.wait_ge(v_ready[0], 2)
            pe.wait_ge(scaled, 12)
            pe_tile(0, 0, True)
            pe_tile(1, 1, second=True)
            with pe.Fori(1, NT // 2) as i:
                for t in range(2):
                    pe_tile(2 * i + t, t)
            def turn_h(n):
                turn_rows(NT, n, h_row(n))

            turn_h(0)
            turn_y(NT - 1)
            turn_h(1)
            for quarter in range(4):
                mix_out(NT - 1, quarter // 2, quarter % 2, Q[0])
                if quarter < 3:
                    turn_h(quarter + 2)

            pe.wait_ge(h_half, 2 * NT)
            first_products(NT, wh2, wl2, uh2, ul2, h_row, UP0)

            def up_product(i, q):
                pe.wait_ge(w_lo, UP0 + 4 * i + q + 1)
                pe.wait_ge(freed[q % 2], N_IN // 2 - 1 + 2 * i + q // 2)
                project(wh2, wl2, uh2, ul2, q % 2, Q[q], range(KT)).then_inc(product, 1)

            for q in range(2, 4):
                up_product(0, q)
            with pe.Fori(1, FT // 2) as i:
                for q in range(4):
                    up_product(i, q)

            def down(k, t, hf, first, last):
                s = hf * FT + k
                pe.wait_ge(d_lo, s + 1)
                pe.wait_ge(g_lo, s + 1)
                for n in range(NT):
                    if first and not hf and n == NT - 2:
                        pe.wait_ge(freed[1], (N_IN + N_UP) // 2)
                    if first and hf:
                        pe.wait_ge(h_added, n + 1)
                    for j, (a, b) in enumerate(parts(gh, gl, dh, dl)):
                        mm = nc.tensor.matmul(acc[n], a[:, t, P * n:P * n + P], b[:, t, :],
                                              start=(first and j == 0), stop=(last and j == 2))
                    if last:
                        mm.then_inc(down_half, 1)
                return mm

            pe.wait_ge(freed[0], (N_IN + N_UP) // 2)
            pe.wait_ge(freed[1], (N_IN + N_UP) // 2 - 1)
            for hf in range(2):
                down(0, 0, hf, True, False).then_inc(down_step, 1)
                down(1, 1, hf, False, False).then_inc(down_step, 1)
                with pe.Fori(1, FT // 2 - 1) as i:
                    for t in range(2):
                        down(2 * i + t, t, hf, False, False).then_inc(down_step, 1)
                down(FT - 2, 0, hf, False, False).then_inc(down_step, 1)
                down(FT - 1, 1, hf, False, True)

            def turn_sum(n):
                pe.wait_ge(normed, 2 * NT + n + 1)
                if n:
                    pe.wait_ge(u_lo, 2 * NT + n)
                for k in range(KT):
                    tr = nc.tensor.transpose(Q[0][:, P * k:P * k + P], un_ple[:, n % 2, P * k:P * k + P], ident[:, :])
                tr.then_inc(turned, 1)

            def gate(n, half):
                for k in range(KT):
                    for j, (a, b) in enumerate(parts(uh3, ul3, gate_hi, gate_lo)):
                        mm = nc.tensor.matmul(Q[2 + n % 2][:, halves(half)], a[:, n % 2, k, :], b[:, k, halves(half)],
                                              start=(k == 0 and j == 0), stop=(k == KT - 1 and j == 2))
                mm.then_inc(gate_half, 1)

            def embed(n):
                wait(pe, ple_ready, 2 * n)
                for half in range(2):
                    for k in range(PK):
                        for j, (a, b) in enumerate(parts(pTh, pTl, pup_hi, pup_lo)):
                            mm = nc.tensor.matmul(Q[1][:, halves(half)], a[:, k, P * n:P * n + P],
                                                  b[:, k, halves(half)], start=(k == 0 and j == 0),
                                                  stop=(k == PK - 1 and j == 2))
                mm.then_inc(embedded, 1)

            pe.wait_ge(h_added, NT + 2)
            turn_sum(0)
            pe.wait_ge(gate_w_lo, KT)
            pe.wait_ge(h_added, NT + 6)
            for n in range(NT):
                pe.wait_ge(u_lo, 2 * NT + n + 1)
                if n >= 2:
                    pe.wait_ge(ple_gate, 2 * (n - 1))
                gate(n, 0)
                if n == 0:
                    pe.wait_ge(h_added, 2 * NT)
                    pe.wait_ge(p_in, 16)
                    for k in range(PK):
                        for m in range(NT):
                            tr = nc.tensor.transpose(Q[(1, 3)[k]][:, P * m:P * m + P],
                                                     p_tok[:, m, P * k:P * k + P], ident[:, :])
                        tr.then_inc(p_turned, 1)
                if n + 1 < NT:
                    turn_sum(n + 1)
                if n == 0:
                    gate(n, 1)
                    pe.wait_ge(p_lo, PK)
                    pe.wait_ge(pw_lo, PK)
                    embed(n)
                else:
                    embed(n)
                    gate(n, 1)

        @block.vector
        def _(dve):
            def normalise(first, n, src, dst, gain):
                dve.wait_ge(rstd_ready, first + n + 1)
                nc.vector.scalar_tensor_tensor(out=dst, in0=src, scalar=rstd[:, n:n + 1], in1=gain[:, :],
                                               op0=ALU.mult, op1=ALU.mult).then_inc(normed, 1)

            def low_half(first, n, ul, uh):
                dve.wait_ge(u_hi, first + n + 1)
                at = slice(P * n, P * n + P)
                nc.vector.tensor_tensor(ul[:, :, at], norm_psum(first, n)[:, :].rearrange("p (k c) -> p k c", c=P),
                                        uh[:, :, at].bitcast(F32), ALU.subtract).then_inc(u_lo, 1)

            dve.wait_ge(gain_in[0], 16)
            def split_in(m):
                dve.wait_ge(w_hi, m + 1)
                nc.vector.tensor_tensor(in_split(wl1, m), in_split(raw1, m), in_split(wh1, m).bitcast(F32),
                                        ALU.subtract).then_inc(w_lo, 1)

            for n in range(2):
                normalise(0, n, xt_mix[:, n, :], xt_mix[:, n, :], gain_mix)
            for n in range(NT):
                low_half(0, n, ul1, uh1)
                if n + 2 < NT:
                    normalise(0, n + 2, xt_mix[:, n + 2, :], xt_mix[:, n + 2, :], gain_mix)
                if n in (2, 3):
                    split_in(n - 2)
                if n == 2:
                    dve.wait_ge(colsT, 1)
                    nc.vector.tensor_copy(cols[:, 0:96], Q[1][:, 0:96]).then_inc(cols_ready, 1)

            dve.wait_ge(cols_ready, 1)
            nc.vector.tensor_copy(lbv[:, 0, :], cols[:, LB0:LB0 + HH]).then_inc(lb_step, 1)
            dve.wait_ge(lb_step, 1)
            nc.vector.tensor_tensor(lbv[:, 1, :], cols[:, LB0:LB0 + HH], lbv[:, 0, :], ALU.subtract).then_inc(lb_step, 1)
            dve.wait_ge(lb_step, 3)
            nc.vector.reciprocal(lbv[:, 3, :], lbv[:, 2, :]).then_inc(lb_step, 1)
            dve.wait_ge(lb_step, 4)
            nc.vector.tensor_tensor(lbv[:, 4, :], lbv[:, 2, :], lbv[:, 3, :], ALU.mult).then_inc(lb_step, 1)
            dve.wait_ge(lb_step, 5)
            nc.vector.tensor_tensor(lbv[:, 5, :], lbv[:, 4, :], lbv[:, 4, :], ALU.subtract).then_inc(lb_step, 1)
            dve.wait_ge(lb_step, 6)
            nc.vector.tensor_scalar(lbv[:, 6, :], lbv[:, 5, :], LB_FLOOR, None, ALU.max).then_inc(lb_step, 1)
            nc.vector.tensor_scalar(lbv[:, 7, :], lbv[:, 5, :], -1.0, 1.0, ALU.mult, ALU.add).then_inc(lb_step, 1)

            dve.wait_ge(lb_step, 8)
            for m in range(N_IN):
                if 1 <= m < N_IN - 1:
                    split_in(m + 1)
                if m < 4:
                    dve.wait_ge(proj_act, m + 1)
                    nc.vector.tensor_tensor(qT[:, m, :], Q[m % 2][:, :], qT[:, m, :], ALU.mult).then_inc(freed[m % 2], 1)
                elif m < 8:
                    a = m - 4
                    dve.wait_ge(freed[m % 2], m // 2 + 1)
                    nc.vector.tensor_scalar(fT[:, a, :], fT[:, a, :], lbv[:, 7, a:a + 1], lbv[:, 6, a:a + 1],
                                            ALU.mult, ALU.add).then_inc(scaled, 1)
                    nc.vector.tensor_scalar(kT[:, a, :], kT[:, a, :], lbv[:, 7, a:a + 1], None,
                                            ALU.mult).then_inc(scaled, 1)
                elif 12 <= m < 16:
                    a = m - 12
                    dve.wait_ge(freed[m % 2], m // 2 + 1)
                    nc.vector.tensor_scalar(sgT[:, a, :], sgT[:, a, :], cols[:, HGG0 + a:HGG0 + a + 1], None,
                                            ALU.mult).then_inc(scaled, 1)

            def values_out(c):
                dve.wait_ge(v_turned, c + 1)
                dst = v_tok[:, :, P * c:P * c + P] if c < HH else av_tok[:, 1:NT + 1, :]
                nc.vector.tensor_copy(dst, v_psum[c][:, :].rearrange("p (n c) -> p n c", c=P)).then_inc(v_ready[0], 1)

            dve.wait_ge(product, N_IN)
            values_out(0)
            values_out(2)

            def row_max(n, g):
                dve.wait_ge(scores, 2 * n + g + 1)
                c = slice(GR * g, GR * g + GR)
                z = 4 * n + 2 * g
                nc.vector.tensor_reduce(smax[:, 0, c], Q[0][:, :].rearrange("p (j k) -> p j k", j=GR), AX.X,
                                        ALU.max).then_inc(max_step, 1)
                dve.wait_ge(max_step, z + 1)
                nc.vector.scalar_tensor_tensor(out=smax[:, 1, c], in0=smax[:, 0, c], scalar=DH ** -0.5, in1=sink[:, c],
                                               op0=ALU.mult, op1=ALU.max).then_inc(max_step, 1)
                dve.wait_ge(max_step, z + 2)
                nc.vector.tensor_scalar(smax[:, 2, c], smax[:, 1, c], -1.0, None, ALU.mult).then_inc(max_ready, 1)
                nc.vector.tensor_tensor(sden[:, 1, c], sink[:, c], smax[:, 1, c], ALU.subtract).then_inc(sink_arg, 1)

            def denominators(n):
                dve.wait_ge(exped, 8 * n + 8)
                dve.wait_ge(sink_exped, 2 * n + 2)
                nc.vector.tensor_tensor(sden[:, 3, :], sden[:, 0, :], sden[:, 2, :], ALU.add).then_inc(den_step, 1)
                dve.wait_ge(den_step, n + 1)
                nc.vector.reciprocal(sden[:, 4, :], sden[:, 3, :]).then_inc(den_ready, 1)

            def att_rows(n):
                dve.wait_ge(attended, 2 * n + 2)
                dve.wait_ge(den_ready, n + 1)
                wait(dve, y_turned, n)
                nc.vector.tensor_tensor(y_tok[:, HW:D].rearrange("p (h d) -> p h d", d=DH),
                                        Q[3][:, 0:512].rearrange("p (h d) -> p h d", d=DH),
                                        sden[:, 4, :].unsqueeze(2).to_broadcast([P, QH, DH]), ALU.mult).then_inc(y_att, 1)

            def factor_step(n, l):
                if l == 0:
                    wait(dve, k_level, 8 * n)
                    wait(dve, q_level, 8 * n)
                    f = fT[:, :, chunk(n)].rearrange("p a (c two) -> p a c two", two=2)
                    nc.vector.tensor_copy(factor(FQ, 0)[:, :, 1].rearrange("p (a c) -> p a c", a=HH),
                                          f[:, :, :, 0]).then_inc(factors, 1)
                    nc.vector.tensor_copy(factor(FK, 0)[:, :, 0].rearrange("p (a c) -> p a c", a=HH),
                                          f[:, :, :, 1]).then_inc(factors, 1)
                    return
                dve.wait_ge(factors, 15 * n + 2 * l)
                left, right = factor(FQ, l - 1)[:, :, 1], factor(FK, l - 1)[:, :, 0]
                if l == LEVELS:
                    nc.vector.tensor_tensor(total[:, :], left, right, ALU.mult).then_inc(factors, 1)
                    return
                left = left.rearrange("p (c two) -> p c two", two=2)
                right = right.rearrange("p (c two) -> p c two", two=2)
                nc.vector.tensor_tensor(factor(FQ, l)[:, :, 1], left[:, :, 0], right[:, :, 0],
                                        ALU.mult).then_inc(factors, 1)
                nc.vector.tensor_tensor(factor(FK, l)[:, :, 0], left[:, :, 1], right[:, :, 1],
                                        ALU.mult).then_inc(factors, 1)

            def q_step(n, l):
                if l == 0:
                    wait(dve, level_product, 8 * n)
                    nc.vector.tensor_tensor(Ql[:, 0, :].rearrange("p (a t) -> p a t", t=P), qT[:, :, chunk(n)],
                                            fT[:, :, chunk(n)], ALU.mult).then_inc(q_level, 1)
                    return
                if l == 1:
                    wait(dve, o_ready, n)
                else:
                    dve.wait_ge(level_product, 8 * n + l)
                dve.wait_ge(q_level, 8 * n + l)
                dve.wait_ge(factors, 15 * n + 2 * l)
                b = 1 << (l - 1)
                nc.vector.tensor_tensor(Ql[:, l % 2, :].rearrange("p (c r) -> p c r", r=b),
                                        Ql[:, (l - 1) % 2, :].rearrange("p (c r) -> p c r", r=b),
                                        FQ[:, f_off(l - 1):f_off(l)].unsqueeze(2).to_broadcast([P, HW // b, b]),
                                        ALU.mult).then_inc(q_level, 1)

            def pick(n, g):
                dve.wait_ge(level_product, 8 * n + g + 1)
                base = 512 * (g % 2)
                if g == 0:
                    wait(dve, o_ready, n)
                else:
                    dve.wait_ge(picked, 8 * n + g)
                dve.sem_inc(turn_of_pick, 1)
                if g == 0:
                    nc.vector.copy_predicated(attT[:, :].rearrange("p (a t) -> p a t", t=P),
                                              ident_b[:, :].bitcast(U16).unsqueeze(1).to_broadcast([P, HH, P]),
                                              Q[2][:, base:base + HW].rearrange("p (a t) -> p a t", t=P)).then_inc(picked, 1)
                    return
                b = 1 << (g - 1)
                m = level_mask[:, 256 * (g - 1):256 * g].bitcast(U16)
                nc.vector.copy_predicated(attT[:, :].rearrange("p (c two r) -> p c two r", two=2, r=b)[:, :, 1, :],
                                          m.rearrange("p (c r) -> p c r", r=b),
                                          Q[2][:, base:base + 256].rearrange("p (c r) -> p c r", r=b)).then_inc(picked, 1)

            def output_half(n, t, pair, half, src=Q[3][:, 512:1024]):
                dve.wait_ge(mixed, 2 * n + half + 1)
                dve.wait_ge(x2_in[t], 16 * pair + 16)
                nc.vector.tensor_tensor(x2[:, t, halves(half)], src, x2[:, t, halves(half)],
                                        ALU.add).then_inc(h_half, 1)

            def o_sums(n):
                dve.wait_ge(o_squared, n + 1)
                nc.vector.tensor_reduce(ssq[:, NT:NT + HH], osq[:, :].rearrange("p (a c) -> p a c", a=HH), AX.X,
                                        ALU.add).then_inc(o_sum, 1)

            def next_state(n):
                dve.wait_ge(delta_ready, n + 1)
                dve.wait_ge(factors, 15 * n + 15)
                for a in range(HH):
                    c = slice(P * a, P * a + P)
                    nc.vector.scalar_tensor_tensor(out=state[:, c], in0=state[:, c], scalar=total[:, a:a + 1],
                                                   in1=Q[3][:, 512 + P * a:512 + P * a + P], op0=ALU.mult,
                                                   op1=ALU.add).then_inc(state_ready, 1)

            def hg_rows(n):
                dve.wait_ge(o_rstd, n + 1)
                nc.vector.tensor_tensor(y_tok[:, 0:HW].rearrange("p (a c) -> p a c", a=HH),
                                        Q[3][:, 0:512].rearrange("p (a c) -> p a c", a=HH),
                                        rstd[:, NT:NT + HH].unsqueeze(2).to_broadcast([P, HH, P]),
                                        ALU.mult).then_inc(y_hg, 1)

            def gated_rows(n, t):
                dve.wait_ge(y_turned, n + 1)
                dve.wait_ge(gate_in[t], 8 * (n - t) + 16)
                nc.vector.tensor_tensor(y_tok[:, 0:HW].rearrange("p (a c) -> p a c", a=HH),
                                        Q[1][:, 0:512].rearrange("p (a c) -> p a c", a=HH),
                                        gate_rows[:, t, :, :], ALU.mult).then_inc(y_gated, 1)

            def low_att(n):
                dve.wait_ge(y_high, 2 * n + 1)
                nc.vector.tensor_tensor(yT_lo[:, HH:KT, :].rearrange("p k c -> p (k c)"), Q[1][:, 512:1024],
                                        yT_hi[:, HH:KT, :].rearrange("p k c -> p (k c)").bitcast(F32),
                                        ALU.subtract).then_inc(y_low, 1)

            def low_gated(n):
                dve.wait_ge(y_high, 2 * n + 2)
                nc.vector.tensor_tensor(yT_lo[:, 0:HH, :].rearrange("p k c -> p (k c)"), y_tok[:, 0:HW],
                                        yT_hi[:, 0:HH, :].rearrange("p k c -> p (k c)").bitcast(F32),
                                        ALU.subtract).then_inc(y_low, 1)

            def low_wo(slabs):
                for k in slabs:
                    dve.wait_ge(wo_high, k + 1)
                    nc.vector.tensor_tensor(wo_lo[:, k, :], wo_raw[:, k, :], wo_hi[:, k, :].bitcast(F32),
                                            ALU.subtract).then_inc(wo_low, 1)

            def dve_tile(n, t, pair, first=False, second=False):
                last_pair = pair - 1 + t
                factor_step(n, 0)
                q_step(n, 0)
                factor_step(n, 1)
                if not first:
                    o_sums(n - 1)
                q_step(n, 1)
                if not first:
                    hg_rows(n - 1)
                else:
                    values_out(4)
                row_max(n, 0)
                pick(n, 0)
                factor_step(n, 2)
                q_step(n, 2)
                pick(n, 1)
                if not first:
                    gated_rows(n - 1, 1 - t)
                    low_att(n - 1)
                    next_state(n - 1)
                    low_gated(n - 1)
                if second:
                    low_wo(range(KT - 2, KT))
                pick(n, 2)
                factor_step(n, 3)
                q_step(n, 3)
                row_max(n, 1)
                pick(n, 3)
                if first:
                    low_wo([0])
                factor_step(n, 4)
                q_step(n, 4)
                pick(n, 4)
                if first:
                    low_wo([1])
                factor_step(n, 5)
                q_step(n, 5)
                denominators(n)
                if not first:
                    output_half(n - 1, 1 - t, last_pair, 0)
                pick(n, 5)
                if first:
                    low_wo([2])
                factor_step(n, 6)
                q_step(n, 6)
                att_rows(n)
                pick(n, 6)
                if first:
                    low_wo([3])
                factor_step(n, 7)
                q_step(n, 7)
                if not first:
                    output_half(n - 1, 1 - t, last_pair, 1)
                pick(n, 7)

            dve.wait_ge(sink_in, 16)
            dve.wait_ge(mask_step, MASK_STEPS)
            dve.wait_ge(start_ready, START_STEPS)
            dve.wait_ge(scaled, 12)
            dve_tile(0, 0, 0, True)
            low_wo(range(KT // 2, KT - 2))
            dve_tile(1, 1, 0, second=True)
            with dve.Fori(1, NT // 2) as i:
                for t in range(2):
                    dve_tile(2 * i + t, t, i)

            def normalise_h(n):
                if n == NT - 2:
                    dve.wait_ge(h_out, 16 * (NT - 1))
                if n == NT - 1:
                    dve.wait_ge(turned, NT + 4)
                normalise(NT, n, h_row(n) if n < NT - 1 else x2[:, 1, :], h_row(n), gain_ffn)

            def split_up(i, q):
                dve.wait_ge(w_hi, UP0 + 4 * i + q + 1)
                nc.vector.tensor_tensor(wl2[:, q % 2, :, :], raw2[:, q % 2, :, P * (q // 2):P * (q // 2) + P],
                                        wh2[:, q % 2, :, :].bitcast(F32), ALU.subtract).then_inc(w_lo, 1)

            dve.wait_ge(gain_in[1], 16)
            normalise_h(0)
            normalise_h(1)
            o_sums(NT - 1)
            hg_rows(NT - 1)
            gated_rows(NT - 1, 1)
            low_att(NT - 1)
            low_gated(NT - 1)
            for n in range(NT):
                if n in (3, 4):
                    output_half(NT - 1, 1, NT // 2 - 1, n - 3, Q[0][:, halves(n - 3)])
                low_half(NT, n, ul2, uh2)
                if n + 2 < NT:
                    normalise_h(n + 2)
                if n in (2, 3):
                    split_up(0, n - 2)

            def split_down(k, t, s):
                dve.wait_ge(g_hi, s + 1)
                nc.vector.tensor_tensor(gl[:, t, :], G[:, ds(k, 1), :].rearrange("p a s -> p (a s)"),
                                        gh[:, t, :].bitcast(F32), ALU.subtract).then_inc(g_lo, 1)
                dve.wait_ge(d_hi, s + 1)
                nc.vector.tensor_tensor(dl[:, t, :], d_raw[t][:, :],
                                        dh[:, t, :].bitcast(F32), ALU.subtract).then_inc(d_lo, 1)

            def up_turn(i, first=False, last=False):
                for q in range(4):
                    if q < 3:
                        if q or not first:
                            split_up(i, q + 1)
                    elif not last:
                        split_up(i + 1, 0)
                    f = 2 * i + q // 2
                    cv = conv[:, q // 2, :]
                    if q % 2 == 0:
                        dve.wait_ge(conv_a, f + 1)
                        nc.vector.scalar_tensor_tensor(out=cv[:, 1:S], in0=Q[q][:, 0:S - 1],
                                                       scalar=cols[:, ds(CONV_W0 + FT + f, 1)], in1=cv[:, 1:S],
                                                       op0=ALU.mult, op1=ALU.add).then_inc(conv_b1, 1)
                        dve.wait_ge(conv_b1, f + 1)
                        nc.vector.scalar_tensor_tensor(out=cv[:, 2:S], in0=Q[q][:, 0:S - 2],
                                                       scalar=cols[:, ds(CONV_W0 + f, 1)], in1=cv[:, 2:S],
                                                       op0=ALU.mult, op1=ALU.add).then_inc(freed[0], 1)
                    else:
                        dve.wait_ge(conv_sig, f + 1)
                        nc.vector.tensor_tensor(cv, cv, sgm[:, :], ALU.mult).then_inc(silued, 1)
                        if last and q == 3:
                            split_down(0, 0, 0)
                        dve.wait_ge(silued, f + 1)
                        dve.wait_ge(product, UP0 + 4 * i + q + 1)
                        nc.vector.tensor_tensor(G[:, ds(f, 1), :].rearrange("p a s -> p (a s)"), Q[q][:, :], cv,
                                                ALU.mult).then_inc(freed[1], 1)
            up_turn(0, first=True)
            with dve.Fori(1, FT // 2 - 1) as i:
                up_turn(i)
            up_turn(FT // 2 - 1, last=True)

            def add_down(hf, n):
                dve.wait_ge(down_half, NT * hf + n + 1)
                c = halves(hf)
                nc.vector.tensor_tensor(h[:, n, c], acc[n], h[:, n, c], ALU.add).then_inc(h_added, 1)

            def low_weights(part):
                for k in (2 * part, 2 * part + 1):
                    dve.wait_ge(gate_w_hi, k + 1)
                    nc.vector.tensor_tensor(gate_lo[:, k, :], gate_raw[:, k, :], gate_hi[:, k, :].bitcast(F32),
                                            ALU.subtract).then_inc(gate_w_lo, 1)

            split_down(1, 1, 1)
            with dve.Fori(1, FT // 2) as i:
                for t in range(2):
                    split_down(2 * i + t, t, 2 * i + t)
            split_down(0, 0, FT)
            dve.wait_ge(h_in, 16 * 4)
            for n in range(NT):
                add_down(0, n)
            split_down(1, 1, FT + 1)
            with dve.Fori(1, FT // 2 - KT // 2) as i:
                for t in range(2):
                    split_down(2 * i + t, t, FT + 2 * i + t)
            for part in range(KT // 2):
                for t in range(2):
                    k = FT - KT + 2 * part + t
                    split_down(k, t, FT + k)
                low_weights(part)

            def normalise_sum(n):
                wait(dve, turned, 2 * NT + n - 1 if n >= 2 else 0)
                normalise(2 * NT, n, h[:, n, :], un_ple[:, n % 2, :], gain_ple)

            def low_sum(n):
                dve.wait_ge(u_hi, 2 * NT + n + 1)
                nc.vector.tensor_tensor(ul3[:, n % 2, :, :], Q[0][:, :].rearrange("p (k c) -> p k c", c=P),
                                        uh3[:, n % 2, :, :].bitcast(F32), ALU.subtract).then_inc(u_lo, 1)

            for n in range(3):
                add_down(1, n)
            dve.wait_ge(gain_in[2], 16)
            normalise_sum(0)
            for n in range(3, 5):
                add_down(1, n)
            low_sum(0)
            add_down(1, 5)
            normalise_sum(1)
            for n in range(6, NT):
                add_down(1, n)
            for k in range(PK):
                dve.wait_ge(pw_hi, k + 1)
                nc.vector.tensor_tensor(pup_lo[:, k, :], pup_raw[:, k, :], pup_hi[:, k, :].bitcast(F32),
                                        ALU.subtract).then_inc(pw_lo, 1)
            for k in range(PK):
                dve.wait_ge(p_hi, k + 1)
                nc.vector.tensor_tensor(pTl[:, k, :], Q[(1, 3)[k]][:, :], pTh[:, k, :].bitcast(F32),
                                        ALU.subtract).then_inc(p_lo, 1)
            dve.wait_ge(gain_in[3], 16)
            for n in range(NT):
                if n + 1 < NT:
                    low_sum(n + 1)
                for half in range(2):
                    z = 2 * n + half + 1
                    dve.wait_ge(ple_gate, z)
                    dve.wait_ge(embedded, n + 1)
                    rows_of_gate = gated[:, n % 2, halves(half)]
                    nc.vector.tensor_tensor(rows_of_gate, Q[1][:, halves(half)], rows_of_gate,
                                            ALU.mult).then_inc(ple_ready, 1)
                    dve.wait_ge(ple_ready, z)
                    nc.vector.tensor_tensor(h[:, n, halves(half)], rows_of_gate, h[:, n, halves(half)],
                                            ALU.add).then_inc(ple_added, 1)
                if n + 2 < NT:
                    normalise_sum(n + 2)
                dve.wait_ge(fin_rstd, n + 1)
                nc.vector.scalar_tensor_tensor(out=h[:, n, :], in0=h[:, n, :], scalar=rstd[:, n:n + 1],
                                               in1=gain_fin[:, :], op0=ALU.mult, op1=ALU.mult).then_inc(fin_ready, 1)


_INS = ["x", "p", "g_mix", "w_in", "lb_logits", "hg_norm_g", "attn_sinks", "w_out", "g_ffn", "w_up", "conv_w",
        "conv_b", "w_down", "g_ple", "w_ple_gate", "w_ple_up", "g_final"]
_OUTS = [((1, 1024, 1024), "float32")]


def kernel(**inputs):
    import numpy as _np
    import concourse.bacc as _bacc
    from concourse import mybir as _mybir
    from concourse.bass_utils import run_bass_kernel_spmd as _run

    nc = _bacc.Bacc("TRN2", target_bir_lowering=False, num_devices=1)
    arrays, args = {}, []
    for name in _INS:
        a = _np.ascontiguousarray(inputs[name])
        arrays[f"in_{name}_dram"] = a
        args.append(nc.dram_tensor(f"in_{name}_dram", a.shape, _mybir.dt.from_np(a.dtype), kind="ExternalInput").ap())
    for i, (shape, dtype) in enumerate(_OUTS):
        dt = _mybir.dt.from_np(_np.dtype(dtype))
        args.append(nc.dram_tensor(f"out_{i}_dram", shape, dt, kind="ExternalOutput").ap())
    trunk_kernel(nc, *args)
    r = _run(nc, [arrays], core_ids=[0])
    got = tuple(r.results[0][f"out_{i}_dram"] for i in range(len(_OUTS)))
    return got[0]
```
